# Optimizing a Trainium2 kernel written in Bass

```python
import math
import jax, jax.numpy as jnp
from jax import lax
import numpy as np

D_MODEL = 2048
BATCH = 1
SEQ = 1024
DEPTH = 1

GRID_W = 64
CTX_LEN = 256
D_MIX = D_MODEL
DIFF_HEADS = 8
DIFF_HEAD_DIM = 64
DIFF_V_DIM = 2 * DIFF_HEAD_DIM
ATT_W = DIFF_HEADS * DIFF_V_DIM
CONV_W = D_MIX - ATT_W
CONV_K = 31
Q_BLOCK = 128
ROPE_BASE = 10000.0
EPS = 1e-6

Q0 = 0
K0 = Q0 + DIFF_HEADS * 2 * DIFF_HEAD_DIM
V0 = K0 + DIFF_HEADS * 2 * DIFF_HEAD_DIM
GA0 = V0 + ATT_W
U0 = GA0 + ATT_W
GC0 = U0 + 2 * CONV_W
IN_W = GC0 + CONV_W

kernel_name = "hybrid_diffattn_conformer_dit_layer"

def rms(x, g):
    xf = x.astype(jnp.float32)
    y = xf * lax.rsqrt(jnp.mean(xf * xf, axis=-1, keepdims=True) + EPS)
    return (y * g).astype(x.dtype)

def layernorm(x, g, b):
    xf = x.astype(jnp.float32)
    mu = jnp.mean(xf, axis=-1, keepdims=True)
    var = jnp.mean(jnp.square(xf - mu), axis=-1, keepdims=True)
    return ((xf - mu) * lax.rsqrt(var + EPS) * g + b).astype(x.dtype)

def adaln(cvec, w, b):
    m = jax.nn.silu(cvec) @ w + b
    return jnp.split(m, 3, axis=-1)

def modulate(x, g, shift, scale):
    return rms(x, g) * (1.0 + scale[:, None]) + shift[:, None]

def rope_tables(n_tokens):
    rows = n_tokens // GRID_W
    row = jnp.repeat(jnp.arange(rows), GRID_W).astype(jnp.float32)
    col = jnp.tile(jnp.arange(GRID_W), rows).astype(jnp.float32)
    nf = DIFF_HEAD_DIM // 4
    inv = ROPE_BASE ** (-jnp.arange(nf, dtype=jnp.float32) / nf)
    ang_r = row[:, None] * inv
    ang_c = col[:, None] * inv
    ang = jnp.concatenate([ang_r, ang_r, ang_c, ang_c], axis=-1)
    return jnp.cos(ang), jnp.sin(ang)

def rotate_half_2d(t):
    nf = DIFF_HEAD_DIM // 4
    xs = t.reshape(t.shape[:-1] + (2, 2, nf))
    x1 = xs[..., 0, :]
    x2 = xs[..., 1, :]
    return jnp.stack([-x2, x1], axis=-2).reshape(t.shape)

def apply_rope(t, cos, sin):
    c = cos[None, :, None, None, :]
    s = sin[None, :, None, None, :]
    return (t * c + rotate_half_2d(t) * s).astype(t.dtype)

def diff_attend(q, k_all, v_all, lam):
    B, N, H, _, d = q.shape
    nblk = N // Q_BLOCK
    qb = jnp.moveaxis(q.reshape(B, nblk, Q_BLOCK, H, 2, d), 1, 0)
    scale = 1.0 / math.sqrt(d)

    def one_block(qi):
        s = jnp.einsum('bqhmd,bkhmd->bhmqk', qi, k_all).astype(jnp.float32) * scale
        p = jax.nn.softmax(s, axis=-1)
        a = p[:, :, 0] - lam * p[:, :, 1]
        return jnp.einsum('bhqk,bkhe->bqhe', a.astype(v_all.dtype), v_all)

    o = lax.map(one_block, qb)
    return jnp.moveaxis(o, 0, 1).reshape(B, N, H, DIFF_V_DIM)

def diff_attn_branch(q, k_all, v_all, lam, lam_init, sub_g):
    B, N = q.shape[0], q.shape[1]
    o = diff_attend(q, k_all, v_all, lam)
    o = rms(o, sub_g) * (1.0 - lam_init)
    return o.reshape(B, N, ATT_W)

def depthwise_conv(y, w, b):
    out = lax.conv_general_dilated(
        y, w[:, None, :].astype(y.dtype), window_strides=(1,),
        padding=[(CONV_K // 2, CONV_K // 2)],
        dimension_numbers=('NWC', 'WIO', 'NWC'),
        feature_group_count=y.shape[-1])
    return out + b

def conformer_conv_branch(u, w, b, ln_g, ln_b):
    a, g = jnp.split(u, 2, axis=-1)
    y = a * jax.nn.sigmoid(g)
    y = depthwise_conv(y, w, b)
    y = layernorm(y, ln_g, ln_b)
    return jax.nn.silu(y)

def setup_inputs(seed: int = 0) -> dict:
    key = jax.random.key(seed)
    ks = jax.random.split(key, 24)
    f32 = jnp.float32
    nrm = lambda k, s, sc: (jax.random.normal(k, s, f32) * sc)
    d = DIFF_HEAD_DIM
    return {
        "x": nrm(ks[0], (BATCH, SEQ, D_MODEL), 1.0),
        "c": nrm(ks[1], (BATCH, D_MODEL), 1.0),
        "ctx": nrm(ks[2], (BATCH, CTX_LEN, D_MODEL), 1.0),
        "c_ctx": nrm(ks[3], (D_MODEL,), 1.0),
        "w_ada": nrm(ks[4], (DEPTH, D_MODEL, 3 * D_MODEL), 0.5 * D_MODEL ** -0.5),
        "b_ada": nrm(ks[5], (DEPTH, 3 * D_MODEL), 0.02),
        "norm_g": 1.0 + nrm(ks[6], (DEPTH, D_MODEL), 0.02),
        "w_in": nrm(ks[7], (DEPTH, D_MODEL, IN_W), D_MODEL ** -0.5),
        "q_norm_g": 1.0 + nrm(ks[8], (DEPTH, d), 0.02),
        "k_norm_g": 1.0 + nrm(ks[9], (DEPTH, d), 0.02),
        "lam_q1": nrm(ks[10], (DEPTH, d), 0.1),
        "lam_k1": nrm(ks[11], (DEPTH, d), 0.1),
        "lam_q2": nrm(ks[12], (DEPTH, d), 0.1),
        "lam_k2": nrm(ks[13], (DEPTH, d), 0.1),
        "sub_norm_g": 1.0 + nrm(ks[14], (DEPTH, DIFF_V_DIM), 0.02),
        "conv_w": nrm(ks[15], (DEPTH, CONV_K, CONV_W), CONV_K ** -0.5),
        "conv_b": nrm(ks[16], (DEPTH, CONV_W), 0.02),
        "conv_ln_g": 1.0 + nrm(ks[17], (DEPTH, CONV_W), 0.02),
        "conv_ln_b": nrm(ks[18], (DEPTH, CONV_W), 0.02),
        "w_out": nrm(ks[19], (DEPTH, D_MIX, D_MODEL), D_MIX ** -0.5),
    }

def reference(x, c, ctx, c_ctx, w_ada, b_ada, norm_g, w_in, q_norm_g, k_norm_g,
              lam_q1, lam_k1, lam_q2, lam_k2, sub_norm_g, conv_w, conv_b,
              conv_ln_g, conv_ln_b, w_out):
    B, N, _ = x.shape
    L_ctx = ctx.shape[1]
    H, d = DIFF_HEADS, DIFF_HEAD_DIM
    cos, sin = rope_tables(N)
    for i in range(DEPTH):
        last = i == DEPTH - 1
        lam_init = 0.8 - 0.6 * math.exp(-0.3 * i)
        lam = (jnp.exp(jnp.sum(lam_q1[i] * lam_k1[i]).astype(jnp.float32))
               - jnp.exp(jnp.sum(lam_q2[i] * lam_k2[i]).astype(jnp.float32)) + lam_init)

        shift_x, scale_x, gate_x = adaln(c, w_ada[i], b_ada[i])
        shift_c, scale_c, gate_c = adaln(c_ctx[None], w_ada[i], b_ada[i])
        h_x = modulate(x, norm_g[i], shift_x, scale_x)
        h_c = modulate(ctx, norm_g[i], shift_c, scale_c)

        p_x = h_x @ w_in[i]
        if last:
            p_c_kv = h_c @ w_in[i][:, K0:GA0]
        else:
            p_c = h_c @ w_in[i]
            p_c_kv = p_c[..., K0:GA0]

        k_c = rms(p_c_kv[..., :V0 - K0].reshape(B, L_ctx, H, 2, d), k_norm_g[i])
        v_c = p_c_kv[..., V0 - K0:].reshape(B, L_ctx, H, DIFF_V_DIM)

        q_x = apply_rope(rms(p_x[..., Q0:K0].reshape(B, N, H, 2, d), q_norm_g[i]), cos, sin)
        k_x = apply_rope(rms(p_x[..., K0:V0].reshape(B, N, H, 2, d), k_norm_g[i]), cos, sin)
        v_x = p_x[..., V0:GA0].reshape(B, N, H, DIFF_V_DIM)
        k_all = jnp.concatenate([k_c, k_x], axis=1)
        v_all = jnp.concatenate([v_c, v_x], axis=1)

        att_x = diff_attn_branch(q_x, k_all, v_all, lam, lam_init, sub_norm_g[i])
        conv_x = conformer_conv_branch(p_x[..., U0:GC0], conv_w[i], conv_b[i],
                                       conv_ln_g[i], conv_ln_b[i])
        mixed_x = jnp.concatenate([att_x * jax.nn.silu(p_x[..., GA0:U0]),
                                   conv_x * jax.nn.silu(p_x[..., GC0:IN_W])], axis=-1)
        y_x = mixed_x @ w_out[i]

        if not last:
            q_c = rms(p_c[..., Q0:K0].reshape(B, L_ctx, H, 2, d), q_norm_g[i])
            att_c = diff_attn_branch(q_c, k_c, v_c, lam, lam_init, sub_norm_g[i])
            conv_c = conformer_conv_branch(p_c[..., U0:GC0], conv_w[i], conv_b[i],
                                           conv_ln_g[i], conv_ln_b[i])
            mixed_c = jnp.concatenate([att_c * jax.nn.silu(p_c[..., GA0:U0]),
                                       conv_c * jax.nn.silu(p_c[..., GC0:IN_W])], axis=-1)
            ctx = ctx + gate_c[:, None] * (mixed_c @ w_out[i])

        x = x + gate_x[:, None] * y_x
    return x


_drawn_inputs = setup_inputs


def setup_inputs(seed=0):
    import zlib

    import numpy as np

    out = dict(_drawn_inputs(seed))
    spreads = {}
    factors = {'ctx': 3.704,
     'b_ada': 4.06,
     'norm_g': 8.0,
     'q_norm_g': 8.0,
     'k_norm_g': 8.0,
     'lam_q1': 64.0,
     'lam_k1': 5.545,
     'lam_q2': 64.0,
     'lam_k2': 49.32,
     'sub_norm_g': 30.56,
     'conv_b': 24.275,
     'conv_ln_g': 34.859,
     'conv_ln_b': 35.274}
    for name, (base, spread) in spreads.items():
        noise = np.random.default_rng([zlib.crc32(name.encode()), seed]).standard_normal(out[name].shape)
        drawn = base * np.exp(spread * noise) if base else spread * noise
        out[name] = __import__('jax').numpy.asarray(drawn.astype(out[name].dtype))
    for name, factor in factors.items():
        out[name] = (out[name] * factor).astype(out[name].dtype)
    return out
```

```python
from contextlib import ExitStack
import math

import numpy as np

import concourse.bass as bass
from concourse import mybir

F32 = mybir.dt.float32
F32R = mybir.dt.float32r
ALU = mybir.AluOpType
ACT = mybir.ActivationFunctionType
AXX = mybir.AxisListType.X

P = 128
D = 2048
JT = D // P
T = 1024
TC = 256
TT = T // P
HEADS = 8
DH = 64
ATT_W = 1024
CONV_W = 1024
CONV_K = 31
HALO = CONV_K // 2
GRID_W = 64
ROPE_BASE = 10000.0
EPS = 1e-6
Q0, K0, V0, GA0, U0 = 0, 1024, 2048, 3072, 4096
GC0 = U0 + 2 * CONV_W
CT = 8
CH = 4
JC = JT // CH
KEYS = TC + T
KT = KEYS // P
SCALE = 1.0 / math.sqrt(DH)
LAM_INIT = 0.8 - 0.6 * math.exp(-0.3 * 0)
BANK = 512
O_BOUND = 2.0 ** 65
O_DOWN = 2.0 ** -20
SQ_OVERFLOW = 2.0 ** 128 * O_DOWN ** 2

N_VC, N_KC, N_U, N_GA, N_GC, N_V, N_K, N_Q, N_END = 0, 8, 16, 32, 40, 48, 56, 64, 72


def rope_tables():
    tok = np.arange(T)
    nf = DH // 4
    inv = ROPE_BASE ** (-np.arange(nf, dtype=np.float32) / np.float32(nf))
    row = (tok // GRID_W).astype(np.float32)[:, None] * inv.astype(np.float32)
    col = (tok % GRID_W).astype(np.float32)[:, None] * inv.astype(np.float32)
    ang = np.concatenate([row, row, col, col], axis=-1).astype(np.float32)
    sign = np.concatenate([-np.ones(nf), np.ones(nf)] * 2).astype(np.float32)
    cos = np.cos(ang).T
    sin = (np.sin(ang) * sign).T
    return (np.ascontiguousarray(np.concatenate([cos, cos]).astype(np.float32)),
            np.ascontiguousarray(np.concatenate([sin, sin]).astype(np.float32)))


def split_matmuls(pe, out, w_hi, w_lo, x_hi, x_lo, start, stop):
    pe.matmul(out, w_hi, x_hi, start=start, stop=False)
    pe.matmul(out, w_hi, x_lo, start=False, stop=False)
    return pe.matmul(out, w_lo, x_hi, start=False, stop=stop)


def build(nc, t):
    with ExitStack() as ctx:
        sem_names = []

        def sem(name):
            sem_names.append(name)
            return ctx.enter_context(nc.semaphore(name))

        base = (nc.sbuf_base + 31) // 32 * 32
        limit = nc.sbuf_usable_end // 32 * 32

        class Region:
            def __init__(self, start):
                self.at = start

            def take(self, name, cols, dtype=F32):
                h = nc.alloc_sbuf_tensor_at(name, [P, cols], dtype, offset=self.at)
                self.at += (cols * 4 + 31) // 32 * 32
                assert self.at <= limit, (name, self.at, limit)
                return h

        o_all = Region(limit - HEADS * T * 4).take("o_all", HEADS * T)[:].rearrange("p (h t) -> p h t", h=HEADS)

        psum = ctx.enter_context(nc.psum_tensor("psum", [P, 8 * BANK], F32))

        def bank(b, n=1):
            return psum[:, b * BANK:(b + n) * BANK]

        ctx_kv_d = nc.dram_tensor("ctx_kv", [(N_U - N_VC) * P, TC], F32, kind="Internal").ap()
        proj_d = nc.dram_tensor("proj", [(N_END - N_GA) * P, T], F32, kind="Internal").ap()
        gate_d = nc.dram_tensor("gate_row", [1, D], F32, kind="Internal").ap()

        projections(nc, t, sem, Region, base, bank, ctx_kv_d, proj_d, gate_d)
        attention(nc, t, sem, Region, base, bank, ctx_kv_d, proj_d, o_all)
        output(nc, t, sem, Region, base, bank, proj_d, gate_d, o_all)


def projections(nc, t, sem, Region, base, bank, ctx_kv_d, proj_d, gate_d):
    r = Region(base)
    h_hi = r.take("h_hi", JT * T, F32R)[:].rearrange("p (j t) -> p j t", j=JT)
    lo_at = r.at
    h_lo = r.take("h_lo", JT * T, F32R)[:].rearrange("p (j t) -> p j t", j=JT)
    w_raw = r.take("w_raw", JT * P)[:].rearrange("p (c j n) -> p c j n", c=CH, n=P)
    w_hi = r.take("w_hi", JT * P, F32R)[:].rearrange("p (c j n) -> p c j n", c=CH, n=P)
    w_lo = r.take("w_lo", JT * P, F32R)[:].rearrange("p (c j n) -> p c j n", c=CH, n=P)
    shared_at = r.at
    hc = r.take("hc", JT * 2 * TC, F32R)[:].rearrange("p (j t) -> p j t", j=JT)
    late_at = r.at
    stage = r.take("stage", 2 * T)[:].rearrange("p (s t) -> p s t", s=2)
    evac = r.take("evac", 2 * T)[:].rearrange("p (s t) -> p s t", s=2)
    y_pad = r.take("y_pad", T + 2 * HALO + 2)
    n_par = CONV_K + 3
    chan_par = r.take("chan_par", CT * n_par)[:].rearrange("p (i k) -> p i k", i=CT)
    tap_w = r.take("tap_w", n_par)
    block_ones = r.take("block_ones", P)
    mean_ones = r.take("mean_ones", P)
    eps_col, q_gain, k_gain = (r.take(name, 1)[:] for name in ("eps_col", "q_gain", "k_gain"))
    mod = r.take("mod", 4 * JT)[:].rearrange("p (k j v) -> p k j v", k=2, v=2)

    xT = Region(lo_at).take("xT", JT * T)[:].rearrange("p (j t) -> p j t", j=JT)
    s = Region(base)
    ada_w = s.take("ada_w", CH * JC * BANK)[:].rearrange("p (c j n) -> p c j n", c=CH, n=BANK)
    x_tok = s.take("x_tok", 2 * D)[:].rearrange("p (s d) -> p s d", s=2)
    x_sq = s.take("x_sq", D)
    chan_rows = s.take("chan_rows", CONV_W)
    ident = s.take("ident", P)
    c_col = s.take("c_col", 2 * JT)[:].rearrange("p (v j) -> p v j", v=2)
    c_act = s.take("c_act", 2 * JT)[:].rearrange("p (j v) -> p j v", v=2)
    ln_x = s.take("ln_x", 3 * (TT + 2))[:].rearrange("p (k t) -> p k t", k=3)
    g_col = s.take("g_col", JT)
    b_col = s.take("b_col", 2 * JT)[:].rearrange("p (k j) -> p k j", k=2)
    assert s.at <= lo_at
    s = Region(shared_at)
    ada_rows = s.take("ada_rows", 3 * D)
    b_gate = s.take("b_gate", D)
    s = Region(late_at)
    xcT = s.take("xcT", JT * TC)[:].rearrange("p (j t) -> p j t", j=JT)
    conv = Region(shared_at).take("conv", CT * T)[:].rearrange("p (i t) -> p i t", i=CT)
    s = Region(shared_at)
    cos = s.take("cos", T)
    sin = s.take("sin", T)
    sq = s.take("sq", 2 * T)[:].rearrange("p (s t) -> p s t", s=2)
    roped = s.take("roped", 2 * T)[:].rearrange("p (s t) -> p s t", s=2)
    turned = s.take("turned", T)
    rstd = s.take("rstd", T)

    ada_v = t["w_ada"].rearrange("l (p j) n -> p (l j) n", p=P)
    w_v = t["w_in"].rearrange("l (p j) n -> p (l j) n", p=P)

    par_landed = sem("par_landed")
    ada_landed = [sem(f"ada_landed{c}") for c in range(CH)]
    ada_used = [sem(f"ada_used{c}") for c in range(CH)]
    ident_ready = sem("ident_ready")
    c_ready = sem("c_ready")
    rows_ready = sem("rows_ready")
    cols_done = sem("cols_done")
    mod_ready = sem("mod_ready")
    x_landed = [sem(f"x_landed{p}") for p in range(2)]
    x_squared = sem("x_squared")
    x_root = sem("x_root")
    x_recip = sem("x_recip")
    x_normed = sem("x_normed")
    x_turned = sem("x_turned")
    xT_by_act = sem("xT_by_act")
    xT_by_dve = sem("xT_by_dve")
    hc_mod = sem("hc_mod")
    hc_hi = sem("hc_hi")
    hc_ready = sem("hc_ready")
    h_mod = sem("h_mod")
    h_hi_done = sem("h_hi_done")
    h_ready = sem("h_ready")
    par_done = sem("par_done")
    mod_step = sem("mod_step")
    gate_stored = sem("gate_stored")
    w_landed = [sem(f"w_landed{c}") for c in range(CH)]
    w_hi_ready = [sem(f"w_hi_ready{c}") for c in range(CH)]
    w_lo_ready = [sem(f"w_lo_ready{c}") for c in range(CH)]
    w_used = [sem(f"w_used{c}") for c in range(CH)]
    tile_done = w_used[CH - 1]
    ctx_half = sem("ctx_half")
    ctx_freed = sem("ctx_freed")
    psum_freed = sem("psum_freed")
    ctx_squared = sem("ctx_squared")
    ctx_summed = sem("ctx_summed")
    ctx_root = sem("ctx_root")
    ctx_recip = sem("ctx_recip")
    ctx_normed = sem("ctx_normed")
    stored = [sem(f"stored{p}") for p in range(2)]
    glu_in = sem("glu_in")
    glu_used = sem("glu_used")
    conv_done = sem("conv_done")
    mean_done = sem("mean_done")
    centred = sem("centred")
    ln_squared = sem("ln_squared")
    ln_sq_used = sem("ln_sq_used")
    ln_root = sem("ln_root")
    ln_ready = sem("ln_ready")
    ln_recip = sem("ln_recip")
    taps_ready = sem("taps_ready")
    tap_done = sem("tap_done")
    gate_used = sem("gate_used")
    eps_ready = sem("eps_ready")
    rope_landed = sem("rope_landed")
    conv_used = sem("conv_used")
    qk_scaled = sem("qk_scaled")
    qk_cos = sem("qk_cos")
    qk_turned = sem("qk_turned")
    qk_roped = sem("qk_roped")
    qk_recip = sem("qk_recip")
    qk_summed = sem("qk_summed")
    qk_root = sem("qk_root")
    qk_done = sem("qk_done")

    N_PAR = 14
    X_TILES = TT + 2

    with nc.Block(name="projections") as block:

        @block.sync
        def _(sp):
            sp.dma_start(c_col[:, 0, :], t["c"].rearrange("l (p j) -> (l p) j", p=P)).then_inc(par_landed, 16)
            sp.dma_start(c_col[:, 1, :], t["c_ctx"].rearrange("(p j) -> p j", p=P)).then_inc(par_landed, 16)
            sp.dma_start(g_col[:], t["norm_g"].rearrange("l (p j) -> (l p) j", p=P)).then_inc(par_landed, 16)
            for k in range(2):
                sp.dma_start(b_col[:, k, :], t["b_ada"][:, k * D:(k + 1) * D].rearrange("l (p j) -> (l p) j", p=P)
                             ).then_inc(par_landed, 16)
            sp.dma_start(b_gate[0:1, :], t["b_ada"][:, 2 * D:]).then_inc(par_landed, 16)
            sp.dma_start(chan_rows[0:CONV_K, :], t["conv_w"].rearrange("l k n -> (l k) n")).then_inc(par_landed, 16)
            for k, name in enumerate(("conv_b", "conv_ln_g", "conv_ln_b")):
                sp.dma_start(chan_rows[CONV_K + k:CONV_K + k + 1, :], t[name]).then_inc(par_landed, 16)
            for m in range(2):
                sp.dma_start(q_gain[m * DH:(m + 1) * DH, :], t["q_norm_g"].rearrange("l d -> d l")).then_inc(par_landed, 16)
                sp.dma_start(k_gain[m * DH:(m + 1) * DH, :], t["k_norm_g"].rearrange("l d -> d l")).then_inc(par_landed, 16)

            def load_ada(nb, first=False):
                for c in range(CH):
                    if not first:
                        sp.wait_ge(ada_used[c], nb)
                    sp.dma_start(ada_w[:, c], ada_v[:, c * JC:(c + 1) * JC, bass.ds(nb * BANK, BANK)]
                                 ).then_inc(ada_landed[c], 16)

            load_ada(0, first=True)
            with sp.Fori(1, 12) as nb:
                load_ada(nb)

            def load_w(n, col, first=False):
                for c in range(CH):
                    if not first:
                        sp.wait_ge(w_lo_ready[c], n)
                    sp.dma_start(w_raw[:, c], w_v[:, c * JC:(c + 1) * JC, bass.ds(col, P)]
                                 ).then_inc(w_landed[c], 16)

            def store_ctx(n, par, ready, count):
                sp.wait_ge(ready, count)
                sp.dma_start(ctx_kv_d[bass.ds(n * P, P), :], stage[:, par, 0:TC]).then_inc(stored[par], 16)

            def store(n, par):
                sp.dma_start(proj_d[bass.ds((n - N_GA) * P, P), :], stage[:, par, :]).then_inc(stored[par], 16)

            def store_after_act(n, par):
                sp.wait_ge(psum_freed, n - N_U + 1)
                store(n, par)

            def store_gc(n, par):
                sp.wait_ge(gate_used, n - N_GC + 2)
                store(n, par)

            def store_qk(n, par):
                sp.wait_ge(qk_done, n - N_K + 1)
                store(n, par)

            sp.wait_ge(mod_step, 1)
            sp.dma_start(gate_d, ada_rows[0:1, 2 * D:3 * D]).then_inc(gate_stored, 16)

            load_w(0, V0, first=True)
            load_w(1, V0 + P)
            with sp.Fori(1, 4) as i:
                for s_ in range(2):
                    load_w(2 * i + s_, V0 + (2 * i + s_) * P)
                    store_ctx(2 * i + s_ - 2, s_, ctx_freed, 2 * i + s_ - 1)
            for s_ in range(2):
                load_w(N_KC + s_, K0 + s_ * P)
                store_ctx(N_KC + s_ - 2, s_, ctx_freed, N_KC + s_ - 1)
            with sp.Fori(1, 4) as i:
                for s_ in range(2):
                    load_w(N_KC + 2 * i + s_, K0 + (2 * i + s_) * P)
                    store_ctx(N_KC + 2 * i + s_ - 2, s_, ctx_normed, 2 * i + s_ - 1)
            for s_ in range(2):
                load_w(N_U + s_, U0 + s_ * CONV_W)
                store_ctx(N_U + s_ - 2, s_, ctx_normed, CT + s_ - 1)
            with sp.Fori(1, CT) as i:
                for s_ in range(2):
                    load_w(N_U + 2 * i + s_, U0 + i * P + s_ * CONV_W)
            for n0, col0, last_store, own_store in ((N_GA, GA0, None, store_after_act),
                                                    (N_GC, GC0, store_after_act, store_gc),
                                                    (N_V, V0, store_gc, store_after_act),
                                                    (N_K, K0, store_after_act, store_qk),
                                                    (N_Q, Q0, store_qk, store_qk)):
                for s_ in range(2):
                    load_w(n0 + s_, col0 + s_ * P)
                    if last_store:
                        last_store(n0 + s_ - 2, s_)
                if n0 == N_V:
                    sp.wait_ge(conv_used, CT)
                    sp.dma_start(cos[:], t["rope_cos"]).then_inc(rope_landed, 16)
                    sp.dma_start(sin[:], t["rope_sin"]).then_inc(rope_landed, 16)
                with sp.Fori(1, CT // 2) as i:
                    for s_ in range(2):
                        load_w(n0 + 2 * i + s_, col0 + (2 * i + s_) * P)
                        own_store(n0 + 2 * i + s_ - 2, s_)
            for s_ in range(2):
                store_qk(N_END - 2 + s_, s_)
            for par in range(2):
                sp.wait_ge(stored[par], 16 * ((N_U - N_VC) + (N_END - N_GA)) // 2)

        @block.gpsimd
        def _(pool):
            pool.memset(ident[:], 0.0).then_inc(ident_ready, 1)
            pool.wait_ge(ident_ready, 1)
            pool.affine_select(out=ident[:], in_=ident[:], compare_op=ALU.not_equal, fill=1.0, base=0,
                               pattern=[[-1, P]], channel_multiplier=1).then_inc(ident_ready, 1)

            xl = t["x"].rearrange("b t d -> (b t) d")
            xc = t["ctx"].rearrange("b t d -> (b t) d")
            for k in range(2):
                pool.dma_start(x_tok[:, k], xl[k * P:(k + 1) * P, :]).then_inc(x_landed[k], 16)
            with pool.Fori(1, TT // 2) as i:
                for k in range(2):
                    pool.wait_ge(x_turned, 8 * i + 4 * k - 4)
                    pool.dma_start(x_tok[:, k], xl[bass.ds((2 * i + k) * P, P), :]).then_inc(x_landed[k], 16)
            for k in range(2):
                pool.wait_ge(x_turned, 4 * (TT + k - 1))
                pool.dma_start(x_tok[:, k], xc[k * P:(k + 1) * P, :]).then_inc(x_landed[k], 16)

            with pool.Fori(0, N_END) as n:
                for c in range(CH):
                    pool.wait_ge(w_hi_ready[c], n + 1)
                    pool.tensor_tensor(w_lo[:, c], w_raw[:, c], w_hi[:, c].bitcast(F32), ALU.subtract
                                       ).then_inc(w_lo_ready[c], 1)

        @block.tensor
        def _(pe):
            pe.wait_ge(ident_ready, 2)
            pe.wait_ge(par_landed, 16 * N_PAR)
            for i in range(CT):
                mm = pe.matmul(bank(6)[:, i * n_par:(i + 1) * n_par], chan_rows[0:n_par, i * P:(i + 1) * P],
                               ident[0:n_par, 0:n_par], start=True, stop=True)
            mm.then_inc(cols_done, 1)

            def ada_block(nb, s_, first=False):
                for c in range(CH):
                    pe.wait_ge(ada_landed[c], 16 * (nb + 1))
                    if c == 0 and not first:
                        pe.wait_ge(rows_ready, nb - 1)
                    for j in range(JC):
                        mm = pe.matmul(bank(s_)[0:2, :], c_act[:, c * JC + j, :], ada_w[:, c, j, :],
                                       start=(c == 0 and j == 0), stop=(c == CH - 1 and j == JC - 1))
                    mm.then_inc(ada_used[c], 1)

            def turn_x(i, k, first=False):
                pe.wait_ge(x_normed, i + 1)
                if not first:
                    pe.wait_ge(xT_by_act, 2 * i)
                    pe.wait_ge(xT_by_dve, 2 * i)
                xv = x_tok[:, k, :].rearrange("p (c j) -> p j c", j=JT)
                for b in range(4):
                    for j in range(4):
                        mm = pe.transpose(bank(2 + b)[:, j * P:(j + 1) * P], xv[:, 4 * b + j, :], ident[:])
                    mm.then_inc(x_turned, 1)

            pe.wait_ge(c_ready, 1)
            ada_block(0, 0, first=True)
            turn_x(0, 0, first=True)
            ada_block(1, 1, first=True)
            turn_x(1, 1)
            with pe.Fori(1, 5) as i:
                for s_ in range(2):
                    ada_block(2 * i + s_, s_)
                    turn_x(2 * i + s_, s_)
            for nb in (10, 11):
                ada_block(nb, nb % 2)
            pe.wait_ge(rows_ready, 12)
            pe.wait_ge(par_done, 1)
            for k in range(2):
                for j in range(JT):
                    rows = ada_rows[0:2, k * D:(k + 1) * D].rearrange("v (c j) -> v j c", j=JT)[:, j, :]
                    mm = pe.matmul(bank(6)[:, 2 * (k * JT + j):2 * (k * JT + j) + 2], rows, ident[0:2, 0:2],
                                   start=True, stop=True)
            mm.then_inc(cols_done, 1)

            def ctx_tile(n, s_, head=False, second=False):
                if not (head or second):
                    pe.wait_ge(ctx_freed, n - 1)
                for c in range(CH):
                    pe.wait_ge(w_hi_ready[c], n + 1)
                    pe.wait_ge(w_lo_ready[c], n + 1)
                    for j in range(JC):
                        jj = c * JC + j
                        if head:
                            pe.wait_ge(hc_ready, jj + 1)
                        pe.matmul(bank(s_), w_hi[:, c, j, :], hc[:, jj, :], start=(jj == 0), stop=False,
                                  skip_group_check=True)
                        mm = pe.matmul(bank(s_)[:, 0:TC], w_lo[:, c, j, :], hc[:, jj, 0:TC], start=False,
                                       stop=(jj == JT - 1), skip_group_check=True)
                    mm.then_inc(w_used[c], 1)

            def ctx_sums(k, par):
                pe.wait_ge(ctx_squared, k + 1)
                pe.matmul(bank(4 + par)[:, 0:TC], block_ones[:], evac[:, par, 512:512 + TC], start=True, stop=True
                          ).then_inc(ctx_summed, 1)

            ctx_tile(0, 0, head=True)
            ctx_tile(1, 1, second=True)
            with pe.Fori(1, 4) as i:
                for s_ in range(2):
                    ctx_tile(2 * i + s_, s_)
            ctx_tile(N_KC, 0)
            ctx_tile(N_KC + 1, 1)
            ctx_sums(0, 0)
            with pe.Fori(1, 4) as i:
                for s_ in range(2):
                    ctx_tile(N_KC + 2 * i + s_, s_)
                    ctx_sums(2 * i + s_ - 1, (s_ + 1) % 2)

            def tile(n, s_):
                for c in range(CH):
                    pe.wait_ge(w_hi_ready[c], n + 1)
                    pe.wait_ge(w_lo_ready[c], n + 1)
                    for j in range(JC):
                        jj = c * JC + j
                        for w, x, last in ((w_hi, h_hi, False), (w_hi, h_lo, False), (w_lo, h_hi, jj == JT - 1)):
                            for hf in range(2):
                                mm = pe.matmul(bank(2 * s_ + hf), w[:, c, j, :], x[:, jj, hf * BANK:(hf + 1) * BANK],
                                               start=(jj == 0 and w is w_hi and x is h_hi), stop=last)
                    mm.then_inc(w_used[c], 1)

            pe.wait_ge(h_ready, JT)
            pe.wait_ge(ctx_freed, N_U)
            tile(N_U, 0)
            ctx_sums(CT - 1, 1)
            tile(N_U + 1, 1)

            def pair(n):
                for s_ in range(2):
                    pe.wait_ge(psum_freed, n + s_ - N_U - 1)
                    tile(n + s_, s_)

            with pe.Fori(1, CT) as i:
                pair(N_U + 2 * i)
            pair(N_GA)
            pe.wait_ge(ctx_root, CT)
            for i in range(CT):
                pe.wait_ge(conv_done, i + 1)
                for hf in range(2):
                    mm = pe.matmul(bank(4 + hf), mean_ones[:], conv[:, i, hf * BANK:(hf + 1) * BANK],
                                   start=(i == 0), stop=(i == CT - 1))
            mm.then_inc(mean_done, 1)
            pair(N_GA + 2)
            for i in range(CT):
                pe.wait_ge(ln_squared, i + 1)
                for hf in range(2):
                    mm = pe.matmul(bank(6 + hf), mean_ones[:], evac[:, i % 2, hf * BANK:(hf + 1) * BANK],
                                   start=(i == 0), stop=(i == CT - 1))
                mm.then_inc(ln_sq_used, 1)
            with pe.Fori(2, 4) as i:
                pair(N_GA + 2 * i)
            for n0 in (N_GC, N_V):
                with pe.Fori(0, 4) as i:
                    pair(n0 + 2 * i)

            def qk_sums(k, par):
                pe.wait_ge(psum_freed, N_K - N_U + k + 1)
                for hf in range(2):
                    mm = pe.matmul(bank(4 + hf), block_ones[:], sq[:, par, hf * BANK:(hf + 1) * BANK],
                                   start=True, stop=True)
                mm.then_inc(qk_summed, 1)

            pair(N_K)
            qk_sums(0, 0)
            with pe.Fori(1, CT) as i:
                for s_ in range(2):
                    n = N_K + 2 * i + s_
                    pe.wait_ge(psum_freed, n - N_U - 1)
                    tile(n, s_)
                    pe.wait_ge(qk_root, 2 * i + s_ - 1)
                    qk_sums(2 * i + s_ - 1, (s_ + 1) % 2)
            pe.wait_ge(qk_root, 2 * CT - 1)
            qk_sums(2 * CT - 1, 1)

        @block.scalar
        def _(act):
            act.wait_ge(par_landed, 16 * N_PAR)
            nc.scalar.activation(c_act[:].rearrange("p j v -> p v j"), c_col[:], ACT.Silu).then_inc(c_ready, 1)
            act.preload_act_table(ACT.Sqrt)
            act.wait_ge(eps_ready, 1)

            def norm_tile(i, k, half):
                act.wait_ge(x_landed[k], 16 * (half + 1))
                nc.scalar.activation(x_sq[:], x_tok[:, k, :], ACT.Square, accum_out=ln_x[:, 0, bass.ds(i, 1)]
                                     ).then_inc(x_squared, 1)
                act.wait_ge(x_squared, i + 1)
                nc.scalar.activation(ln_x[:, 1, bass.ds(i, 1)], ln_x[:, 0, bass.ds(i, 1)], ACT.Sqrt, scale=1.0 / D,
                                     bias=eps_col).then_inc(x_root, 1)

            def copy_xT(i, dst, col):
                for b in range(2):
                    act.wait_ge(x_turned, 4 * i + b + 1)
                    nc.scalar.activation(dst[:, 4 * b:4 * b + 4, bass.ds(col, P)],
                                         bank(2 + b).rearrange("p (j c) -> p j c", j=4), ACT.Copy).then_inc(xT_by_act, 1)

            def copy_rows(nb, s_):
                act.wait_ge(ada_used[CH - 1], nb + 1)
                nc.scalar.activation(ada_rows[0:2, bass.ds(nb * BANK, BANK)], bank(s_)[0:2, :], ACT.Copy
                                     ).then_inc(rows_ready, 1)

            with act.Fori(0, TT // 2) as i:
                for k in range(2):
                    norm_tile(2 * i + k, k, i)
                    copy_rows(2 * i + k, k)
                    copy_xT(2 * i + k, xT, (2 * i + k) * P)
            for k in range(2):
                norm_tile(TT + k, k, TT // 2)
                copy_rows(TT + k, k)
                copy_xT(TT + k, xcT, k * P)
            for nb in (10, 11):
                copy_rows(nb, nb % 2)

            def split_w(n, first=False):
                for c in range(CH):
                    act.wait_ge(w_landed[c], 16 * (n + 1))
                    if not first:
                        act.wait_ge(w_used[c], n)
                    nc.scalar.activation(w_hi[:, c], w_raw[:, c], ACT.Copy).then_inc(w_hi_ready[c], 1)

            split_w(0, first=True)
            act.wait_ge(gate_stored, 16)
            for j in range(JT):
                act.wait_ge(hc_mod, j + 1)
                nc.scalar.activation(hc[:, j, 0:TC], xcT[:, j, :], ACT.Copy).then_inc(hc_hi, 1)
            for j in range(JT):
                act.wait_ge(h_mod, j + 1)
                nc.scalar.activation(h_hi[:, j, :], xT[:, j, :], ACT.Copy).then_inc(h_hi_done, 1)

            def ctx_evac(n, s_, freed=True):
                act.wait_ge(tile_done, n + 1)
                if freed:
                    act.wait_ge(ctx_freed, n - 1)
                nc.scalar.activation(evac[:, s_, TC:2 * TC], bank(s_)[:, TC:2 * TC], ACT.Copy).then_inc(ctx_half, 1)

            for n in range(2):
                split_w(n + 1)
                ctx_evac(n, n, freed=False)
            with act.Fori(1, 4) as i:
                for s_ in range(2):
                    split_w(2 * i + s_ + 1)
                    ctx_evac(2 * i + s_, s_)

            def ctx_square(k, par):
                act.wait_ge(ctx_freed, N_KC + k + 1)
                nc.scalar.activation(evac[:, par, 2 * TC:3 * TC], evac[:, par, 0:TC], ACT.Square).then_inc(ctx_squared, 1)

            def ctx_sqrt(k, par):
                act.wait_ge(ctx_summed, k + 1)
                nc.scalar.activation(evac[:, par, 3 * TC:4 * TC], bank(4 + par)[:, 0:TC], ACT.Sqrt,
                                     scale=1.0 / DH, bias=eps_col).then_inc(ctx_root, 1)

            for k in range(2):
                split_w(N_KC + k + 1)
                ctx_evac(N_KC + k, k)
                ctx_square(k, k)
            ctx_sqrt(0, 0)
            with act.Fori(1, 4) as i:
                for s_ in range(2):
                    k = 2 * i + s_
                    split_w(N_KC + k + 1)
                    act.wait_ge(ctx_normed, k - 1)
                    ctx_evac(N_KC + k, s_)
                    ctx_square(k, s_)
                    ctx_sqrt(k - 1, (s_ + 1) % 2)

            def glu_value(n, i, first=False):
                split_w(n + 1)
                act.wait_ge(tile_done, n + 1)
                if not first:
                    act.wait_ge(glu_used, i)
                nc.scalar.activation(evac[:, 0, :], bank(0, 2), ACT.Copy).then_inc(psum_freed, 1)

            def glu_gate(n):
                split_w(n + 1)
                act.wait_ge(tile_done, n + 1)
                nc.scalar.activation(evac[:, 1, :], bank(2, 2), ACT.Sigmoid).then_inc(psum_freed, 1)

            split_w(N_U + 1)
            ctx_sqrt(CT - 1, 1)
            act.wait_ge(ctx_normed, CT)
            act.preload_act_table(ACT.Sigmoid)
            act.wait_ge(tile_done, N_U + 1)
            nc.scalar.activation(evac[:, 0, :], bank(0, 2), ACT.Copy).then_inc(psum_freed, 1)
            glu_gate(N_U + 1)
            with act.Fori(1, CT) as i:
                glu_value(N_U + 2 * i, i)
                glu_gate(N_U + 2 * i + 1)

            def to_stage(n, s_, count, func):
                split_w(n + 1)
                act.wait_ge(tile_done, n + 1)
                act.wait_ge(stored[s_], count)
                nc.scalar.activation(stage[:, s_, :], bank(2 * s_, 2), func).then_inc(psum_freed, 1)

            act.preload_act_table(ACT.Silu)
            for k in range(4):
                to_stage(N_GA + k, k % 2, 16 * (CT + k // 2), ACT.Silu)
            for i in range(CT):
                act.wait_ge(centred, i + 1)
                if i >= 2:
                    act.wait_ge(ln_sq_used, i - 1)
                nc.scalar.activation(evac[:, i % 2, :], conv[:, i, :], ACT.Square).then_inc(ln_squared, 1)
            act.wait_ge(ln_sq_used, CT)
            nc.scalar.activation(evac[:, 0, :], bank(6, 2), ACT.Sqrt, bias=eps_col).then_inc(ln_root, 1)
            act.preload_act_table(ACT.Silu)
            with act.Fori(2, 4) as i:
                for s_ in range(2):
                    to_stage(N_GA + 2 * i + s_, s_, 16 * (CT + i), ACT.Silu)

            act.wait_ge(ln_ready, CT)

            def conv_gate(k, s_):
                split_w(N_GC + k + 1)
                act.wait_ge(gate_used, k + 1)
                par = chan_par[:, bass.ds(k, 1), :].rearrange("p i k -> p (i k)")
                nc.scalar.activation(evac[:, 1, :], conv[:, bass.ds(k, 1), :].rearrange("p i t -> p (i t)"), ACT.Silu,
                                     scale=par[:, CONV_K + 1:CONV_K + 2], bias=par[:, CONV_K + 2:CONV_K + 3]
                                     ).then_inc(conv_used, 1)
                act.wait_ge(tile_done, N_GC + k + 1)
                nc.scalar.activation(evac[:, 0, :], bank(2 * s_, 2), ACT.Silu).then_inc(psum_freed, 1)

            with act.Fori(0, 4) as i:
                for s_ in range(2):
                    conv_gate(2 * i + s_, s_)
            with act.Fori(0, 4) as i:
                for s_ in range(2):
                    to_stage(N_V + 2 * i + s_, s_, 16 * (CT + 8 + i), ACT.Copy)
            act.preload_act_table(ACT.Sqrt)

            def qk_evac(n, k, s_, gain, last=False):
                if not last:
                    split_w(n + 1)
                act.wait_ge(tile_done, n + 1)
                nc.scalar.activation(evac[:, s_, :], bank(2 * s_, 2), ACT.Copy, scale=gain).then_inc(qk_scaled, 1)
                nc.scalar.activation(sq[:, s_, :], bank(2 * s_, 2), ACT.Square).then_inc(psum_freed, 1)

            def qk_sqrt(k):
                act.wait_ge(qk_summed, k + 1)
                nc.scalar.activation(rstd[:], bank(4, 2), ACT.Sqrt, scale=1.0 / DH, bias=eps_col).then_inc(qk_root, 1)

            act.wait_ge(gate_used, CT + 1)
            qk_evac(N_K, 0, 0, k_gain)
            qk_evac(N_K + 1, 1, 1, k_gain)
            qk_sqrt(0)

            def qk_pair(n, k, gain, last=False):
                for s_ in range(2):
                    act.wait_ge(qk_roped, k + s_ - 1)
                    act.wait_ge(qk_summed, k + s_ - 1)
                    qk_evac(n + s_, k + s_, s_, gain, last and s_ == 1)
                    act.wait_ge(qk_done, k + s_ - 1)
                    qk_sqrt(k + s_ - 1)

            with act.Fori(1, 4) as i:
                qk_pair(N_K + 2 * i, 2 * i, k_gain)
            with act.Fori(4, 7) as i:
                qk_pair(N_K + 2 * i, 2 * i, q_gain)
            qk_pair(N_END - 2, 2 * CT - 2, q_gain, last=True)
            act.wait_ge(qk_done, 2 * CT - 1)
            qk_sqrt(2 * CT - 1)

        @block.vector
        def _(dve):
            nc.vector.memset(eps_col, EPS).then_inc(eps_ready, 1)
            nc.vector.memset(mean_ones[:], 1.0 / CONV_W)
            nc.vector.memset(block_ones[0:DH, 0:DH], 1.0)
            nc.vector.memset(block_ones[0:DH, DH:P], 0.0)
            nc.vector.memset(block_ones[DH:P, 0:DH], 0.0)
            nc.vector.memset(block_ones[DH:P, DH:P], 1.0)
            nc.vector.memset(y_pad[:, 0:HALO], 0.0)
            nc.vector.memset(y_pad[:, HALO + T:], 0.0)
            dve.wait_ge(cols_done, 1)
            nc.vector.tensor_copy(chan_par[:].rearrange("p i k -> p (i k)"), bank(6)[:, 0:CT * n_par]).then_inc(par_done, 1)

            def norm_tile(i, k):
                dve.wait_ge(x_root, i + 1)
                nc.vector.reciprocal(ln_x[:, 2, bass.ds(i, 1)], ln_x[:, 1, bass.ds(i, 1)]).then_inc(x_recip, 1)
                dve.wait_ge(x_recip, i + 1)
                nc.vector.tensor_scalar(x_tok[:, k, :], x_tok[:, k, :], ln_x[:, 2, bass.ds(i, 1)], None, ALU.mult
                                        ).then_inc(x_normed, 1)

            def copy_xT(i, dst, col):
                for b in range(2, 4):
                    dve.wait_ge(x_turned, 4 * i + b + 1)
                    nc.vector.tensor_copy(dst[:, 4 * b:4 * b + 4, bass.ds(col, P)],
                                          bank(2 + b).rearrange("p (j c) -> p j c", j=4)).then_inc(xT_by_dve, 1)

            with dve.Fori(0, TT // 2) as i:
                for k in range(2):
                    norm_tile(2 * i + k, k)
                    copy_xT(2 * i + k, xT, (2 * i + k) * P)
            for k in range(2):
                norm_tile(TT + k, k)
                copy_xT(TT + k, xcT, k * P)

            dve.wait_ge(rows_ready, 12)
            nc.vector.tensor_tensor(ada_rows[0:1, 2 * D:], ada_rows[0:1, 2 * D:], b_gate[0:1, :], ALU.add
                                    ).then_inc(mod_step, 1)
            dve.wait_ge(cols_done, 2)
            cols = bank(6)[:, 0:4 * JT].rearrange("p (k j v) -> p k j v", k=2, v=2)
            for v in range(2):
                nc.vector.tensor_tensor(mod[:, 1, :, v], cols[:, 0, :, v], b_col[:, 0, :], ALU.add)
                nc.vector.tensor_tensor(mod[:, 0, :, v], cols[:, 1, :, v], b_col[:, 1, :], ALU.add).then_inc(mod_step, 1)
            dve.wait_ge(mod_step, 3)
            for v in range(2):
                nc.vector.scalar_tensor_tensor(out=mod[:, 0, :, v], in0=mod[:, 0, :, v], scalar=1.0, in1=g_col[:],
                                               op0=ALU.add, op1=ALU.mult).then_inc(mod_ready, 1)
            dve.wait_ge(mod_ready, 2)
            dve.wait_ge(xT_by_act, 2 * X_TILES)
            for j in range(JT):
                nc.vector.tensor_scalar(xcT[:, j, :], xcT[:, j, :], mod[:, 0, j, 1:2], mod[:, 1, j, 1:2], ALU.mult, ALU.add
                                        ).then_inc(hc_mod, 1)
            for j in range(JT):
                dve.wait_ge(hc_hi, j + 1)
                nc.vector.tensor_tensor(hc[:, j, TC:2 * TC], xcT[:, j, :], hc[:, j, 0:TC].bitcast(F32), ALU.subtract
                                        ).then_inc(hc_ready, 1)
            for j in range(JT):
                nc.vector.tensor_scalar(xT[:, j, :], xT[:, j, :], mod[:, 0, j, 0:1], mod[:, 1, j, 0:1], ALU.mult, ALU.add
                                        ).then_inc(h_mod, 1)
                if j >= 1:
                    dve.wait_ge(h_hi_done, j)
                    nc.vector.tensor_tensor(h_lo[:, j - 1, :], xT[:, j - 1, :], h_hi[:, j - 1, :].bitcast(F32), ALU.subtract
                                            ).then_inc(h_ready, 1)
            dve.wait_ge(h_hi_done, JT)
            nc.vector.tensor_tensor(h_lo[:, JT - 1, :], xT[:, JT - 1, :], h_hi[:, JT - 1, :].bitcast(F32), ALU.subtract
                                    ).then_inc(h_ready, 1)

            def ctx_v(n, s_, stores):
                dve.wait_ge(ctx_half, n + 1)
                if stores is not None:
                    dve.wait_ge(stored[s_], stores)
                nc.vector.tensor_tensor(stage[:, s_, 0:TC], bank(s_)[:, 0:TC], evac[:, s_, TC:2 * TC], ALU.add
                                        ).then_inc(ctx_freed, 1)

            for n in range(2):
                ctx_v(n, n, None)
            with dve.Fori(1, 4) as i:
                for s_ in range(2):
                    ctx_v(2 * i + s_, s_, 16 * i)

            def ctx_k_sum(k, s_):
                dve.wait_ge(ctx_half, N_KC + k + 1)
                nc.vector.tensor_tensor(evac[:, s_, 0:TC], bank(s_)[:, 0:TC], evac[:, s_, TC:2 * TC], ALU.add
                                        ).then_inc(ctx_freed, 1)

            def ctx_k_norm(k, s_, stores):
                dve.wait_ge(ctx_root, k + 1)
                nc.vector.reciprocal(evac[:, s_, 3 * TC:4 * TC], evac[:, s_, 3 * TC:4 * TC]).then_inc(ctx_recip, 1)
                dve.wait_ge(ctx_recip, k + 1)
                dve.wait_ge(stored[s_], stores)
                nc.vector.scalar_tensor_tensor(out=stage[:, s_, 0:TC], in0=evac[:, s_, 0:TC], scalar=k_gain,
                                               in1=evac[:, s_, 3 * TC:4 * TC], op0=ALU.mult, op1=ALU.mult
                                               ).then_inc(ctx_normed, 1)

            ctx_k_sum(0, 0)
            ctx_k_sum(1, 1)
            ctx_k_norm(0, 0, 16 * 4)
            with dve.Fori(1, 4) as i:
                ctx_k_sum(2 * i, 0)
                ctx_k_norm(2 * i - 1, 1, 16 * (3 + i))
                ctx_k_sum(2 * i + 1, 1)
                ctx_k_norm(2 * i, 0, 16 * (4 + i))
            ctx_k_norm(CT - 1, 1, 16 * 7)

            y = y_pad[:, HALO:HALO + T]
            acc = conv[:, CT - 1, :]

            def conv_tile(i):
                dve.wait_ge(psum_freed, 2 * i + 2)
                nc.vector.tensor_tensor(y, evac[:, 0, :], evac[:, 1, :], ALU.mult).then_inc(glu_used, 1)
                nc.vector.tensor_copy(tap_w[:], chan_par[:, bass.ds(i, 1), :].rearrange("p i k -> p (i k)")
                                      ).then_inc(taps_ready, 1)
                dve.wait_ge(taps_ready, i + 1)
                dve.wait_ge(glu_used, i + 1)
                nc.vector.tensor_scalar(acc, y_pad[:, 0:T], tap_w[:, 0:1], tap_w[:, CONV_K:CONV_K + 1], ALU.mult, ALU.add
                                        ).then_inc(tap_done, 1)
                for k in range(1, CONV_K):
                    dve.wait_ge(tap_done, i * (CONV_K - 1) + k)
                    last = k == CONV_K - 1
                    out = conv[:, bass.ds(i, 1), :].rearrange("p i t -> p (i t)") if last else acc
                    nc.vector.scalar_tensor_tensor(out=out, in0=y_pad[:, k:k + T], scalar=tap_w[:, k:k + 1], in1=acc,
                                                   op0=ALU.mult, op1=ALU.add).then_inc(conv_done if last else tap_done, 1)
                dve.wait_ge(conv_done, i + 1)

            with dve.Fori(0, CT) as i:
                conv_tile(i)

            dve.wait_ge(mean_done, 1)
            for i in range(CT):
                nc.vector.tensor_tensor(conv[:, i, :], conv[:, i, :], bank(4, 2), ALU.subtract).then_inc(centred, 1)
            dve.wait_ge(ln_root, 1)
            nc.vector.reciprocal(evac[:, 0, :], evac[:, 0, :]).then_inc(ln_recip, 1)
            dve.wait_ge(ln_recip, 1)
            for i in range(CT):
                nc.vector.tensor_tensor(conv[:, i, :], conv[:, i, :], evac[:, 0, :], ALU.mult).then_inc(ln_ready, 1)
            dve.wait_ge(ln_ready, CT)
            dve.sem_inc(gate_used, 1)

            with dve.Fori(0, 4) as i:
                for s_ in range(2):
                    dve.wait_ge(conv_used, 2 * i + s_ + 1)
                    dve.wait_ge(psum_freed, N_GC - N_U + 2 * i + s_ + 1)
                    dve.wait_ge(stored[s_], 16 * (CT + 4 + i))
                    nc.vector.tensor_tensor(stage[:, s_, :], evac[:, 0, :], evac[:, 1, :], ALU.mult
                                            ).then_inc(gate_used, 1)

            swap = [(q + 16) % 32 for q in range(32)]

            def rope(k, s_, first=False):
                dve.wait_ge(qk_scaled, k + 1)
                if not first:
                    dve.wait_ge(qk_roped, k)
                nc.vector.tensor_tensor(roped[:, s_, :], evac[:, s_, :], cos[:], ALU.mult).then_inc(qk_cos, 1)
                nc.vector.stream_shuffle(turned[:], evac[:, s_, :], swap).then_inc(qk_turned, 1)
                dve.wait_ge(qk_turned, 2 * k + 1)
                nc.vector.tensor_tensor(turned[:], turned[:], sin[:], ALU.mult).then_inc(qk_turned, 1)
                dve.wait_ge(qk_turned, 2 * k + 2)
                dve.wait_ge(qk_cos, k + 1)
                nc.vector.tensor_tensor(roped[:, s_, :], roped[:, s_, :], turned[:], ALU.add).then_inc(qk_roped, 1)

            def qk_norm(k, s_, stores):
                dve.wait_ge(qk_root, k + 1)
                nc.vector.reciprocal(rstd[:], rstd[:]).then_inc(qk_recip, 1)
                dve.wait_ge(qk_recip, k + 1)
                dve.wait_ge(stored[s_], stores)
                nc.vector.tensor_tensor(stage[:, s_, :], roped[:, s_, :], rstd[:], ALU.mult).then_inc(qk_done, 1)

            dve.wait_ge(rope_landed, 32)
            rope(0, 0, first=True)
            rope(1, 1)
            qk_norm(0, 0, 16 * (CT + 12))
            with dve.Fori(1, CT) as i:
                dve.wait_ge(qk_done, 2 * i - 1)
                rope(2 * i, 0)
                qk_norm(2 * i - 1, 1, 16 * (CT + 11 + i))
                dve.wait_ge(qk_done, 2 * i)
                rope(2 * i + 1, 1)
                qk_norm(2 * i, 0, 16 * (CT + 12 + i))
            qk_norm(2 * CT - 1, 1, 16 * (CT + 12 + 7))


def attention(nc, t, sem, Region, base, bank, ctx_kv_d, proj_d, o_all):
    r = Region(base)
    q_st = r.take("q_st", 2 * 2 * T, F32R)[:].rearrange("p (b m t) -> p b m t", b=2, m=2)
    k_hi = r.take("k_hi", 2 * 2 * KEYS, F32R)[:].rearrange("p (b m t) -> p b m t", b=2, m=2)
    k_lo = r.take("k_lo", 2 * 2 * KEYS, F32R)[:].rearrange("p (b m t) -> p b m t", b=2, m=2)
    v_hi = r.take("v_hi", 2 * KEYS, F32R)[:].rearrange("p (b t) -> p b t", b=2)
    v_lo = r.take("v_lo", 2 * KEYS, F32R)[:].rearrange("p (b t) -> p b t", b=2)
    q_raw = r.take("q_raw", 2 * T)[:].rearrange("p (m t) -> p m t", m=2)
    k_raw = r.take("k_raw", 2 * KEYS)[:].rearrange("p (m t) -> p m t", m=2)
    v_raw = r.take("v_raw", KEYS)
    prob = r.take("prob", 2 * 2 * KEYS)[:].rearrange("p (b m t) -> p b m t", b=2, m=2)
    diff = r.take("diff", 2 * KEYS)[:].rearrange("p (b t) -> p b t", b=2)
    QG = 2 * P
    dT_hi = r.take("dT_hi", 2 * KT * QG, F32R)[:].rearrange("p (b k q) -> p b k q", b=2, k=KT)
    dT_lo = r.take("dT_lo", 2 * KT * QG, F32R)[:].rearrange("p (b k q) -> p b k q", b=2, k=KT)
    ident = r.take("ident_b", P)
    top = r.take("top", 4)[:].rearrange("p (b m) -> p b m", b=2)
    neg_top = r.take("neg_top", 4)[:].rearrange("p (b m) -> p b m", b=2)
    total = r.take("total", 4)[:].rearrange("p (b m) -> p b m", b=2)
    inv = r.take("inv", 4)[:].rearrange("p (b m) -> p b m", b=2)
    inv_lam = r.take("inv_lam", 2)
    lam_rows = r.take("lam_rows", 4 * DH)[:].rearrange("p (k d) -> p k d", k=4)
    lam_dots = r.take("lam_dots", 2)
    lam_exp = r.take("lam_exp", 2)
    lam = r.take("lam", 1)
    ones_row = r.take("ones_row", P)
    lam_tmp = r.take("lam_tmp", 2 * DH)[:].rearrange("p (k d) -> p k d", k=2)
    assert r.at <= o_all_start(nc), r.at

    ROUNDS = ((0, 4), (4, 8), (8, 10))
    FRONT = 2
    V_STEP = 4
    PER_HEAD = 2 * TT + len(ROUNDS)

    def v_before(h, st):
        return 0 if isinstance(h, int) and h == HEADS - 1 else min(max(st - V_STEP, 0), len(ROUNDS))

    def use6(h, st, second):
        return len(ROUNDS) + PER_HEAD * h + 2 * st + v_before(h, st) + second

    def use6_v(h, rd):
        return len(ROUNDS) + PER_HEAD * h + 2 * (V_STEP + rd) + 2 + rd

    def ahead(h, st, by):
        return (h, st + by) if st + by < TT else (h + 1, st + by - TT)

    q_landed, k_landed, v_landed, lam_landed = (sem(n) for n in ("q_landed", "k_landed", "v_landed", "lam_landed"))
    id_ready = sem("id_ready")
    ones_ready = sem("ones_ready")
    lam_step = sem("lam_step")
    lam_spread = sem("lam_spread")
    lam_ready = sem("lam_ready")
    k_rounded = sem("k_rounded")
    q_rounded = sem("q_rounded")
    k_split = sem("k_split")
    q_split = sem("q_split")
    v_turned = sem("v_turned")
    scores_done = [sem(f"scores_done{m}") for m in range(2)]
    top_found = [sem(f"top_found{m}") for m in range(2)]
    top_ready = [sem(f"top_ready{m}") for m in range(2)]
    exp_done = [sem(f"exp_done{m}") for m in range(2)]
    inv_ready = sem("inv_ready")
    scale_ready = sem("scale_ready")
    map1_scaled = sem("map1_scaled")
    diff_ready = sem("diff_ready")
    turned6, hi6, free6 = sem("turned6"), sem("hi6"), sem("free6")
    turned7, hi7, free7 = sem("turned7"), sem("hi7"), sem("free7")
    pv_done = sem("pv_done")
    o_copied = sem("o_copied")
    v_read = sem("v_read")

    with nc.Block(name="attention") as block:

        @block.sync
        def _(sp):
            for k, name in enumerate(("lam_q1", "lam_k1", "lam_q2", "lam_k2")):
                sp.dma_start(lam_rows[0:1, k, :], t[name]).then_inc(lam_landed, 16)

            def load_head(h, first=False):
                row_k = (N_K - N_GA) * P + h * P
                if not first:
                    sp.wait_ge(k_split, 2 * h)
                for half in range(2):
                    dst = k_raw[half * DH:(half + 1) * DH]
                    sp.dma_start(dst[:, :, 0:TC], ctx_kv_d[bass.ds(N_KC * P + h * P, P), :]
                                 .rearrange("(m p) t -> p m t", m=2)).then_inc(k_landed, 16)
                    sp.dma_start(dst[:, :, TC:], proj_d[bass.ds(row_k, P), :]
                                 .rearrange("(m p) t -> p m t", m=2)).then_inc(k_landed, 16)
                if not first:
                    sp.wait_ge(q_split, 2 * h)
                for half in range(2):
                    sp.dma_start(q_raw[half * DH:(half + 1) * DH], proj_d[bass.ds((N_Q - N_GA) * P + h * P, P), :]
                                 .rearrange("(m p) t -> p m t", m=2)).then_inc(q_landed, 16)
                if not first:
                    sp.wait_ge(v_read, h)
                sp.dma_start(v_raw[:, 0:TC], ctx_kv_d[bass.ds(h * P, P), :]).then_inc(v_landed, 16)
                sp.dma_start(v_raw[:, TC:], proj_d[bass.ds((N_V - N_GA) * P + h * P, P), :]).then_inc(v_landed, 16)

            load_head(0, first=True)
            with sp.Fori(1, HEADS) as h:
                load_head(h)

        @block.tensor
        def _(pe):
            pe.wait_ge(lam_step, 2)
            pe.wait_ge(ones_ready, 1)
            pe.matmul(bank(7)[:, 0:2], ones_row[0:1, :], lam_dots[0:1, :], start=True, stop=True).then_inc(lam_spread, 1)

            def turn_v(h, rd, use, first=False):
                if rd == 0:
                    pe.wait_ge(v_landed, 32 * (h + 1))
                if not first:
                    pe.wait_ge(free6, use)
                k0, k1 = ROUNDS[rd]
                for k in range(k0, k1):
                    mm = pe.transpose(bank(6)[:, (k - k0) * P:(k - k0 + 1) * P], v_raw[:, k * P:(k + 1) * P], ident[:])
                mm.then_inc(turned6, 1)

            def scores(h, st, b, m, s_, first=False):
                if st == 0:
                    pe.wait_ge(k_split, 2 * (h + 1))
                    pe.wait_ge(q_split, 2 * (h + 1))
                if not first:
                    pe.wait_ge(exp_done[m], s_)
                q = q_st[:, b, m, st * P:(st + 1) * P]
                for c0 in range(0, KEYS, BANK):
                    c1 = min(c0 + BANK, KEYS)
                    out = bank(3 * m, 3)[:, c0:c1]
                    pe.matmul(out, q, k_hi[:, b, m, c0:c1], start=True, stop=False)
                    mm = pe.matmul(out, q, k_lo[:, b, m, c0:c1], start=False, stop=True)
                mm.then_inc(scores_done[m], 1)

            def turn_diff(h, st, s_, rd):
                if rd == 0:
                    pe.wait_ge(diff_ready, s_ + 1)
                if rd == 1:
                    pe.wait_ge(free7, s_ + 1)
                    if st % 2 == 0:
                        pe.wait_ge(o_copied, 4 * h + st // 2 + 1)
                else:
                    pe.wait_ge(free6, use6(h, st, rd // 2))
                k0, k1 = ROUNDS[rd]
                for k in range(k0, k1):
                    mm = pe.transpose(bank(7 if rd == 1 else 6)[:, (k - k0) * P:(k - k0 + 1) * P],
                                      diff[:, st % 2, k * P:(k + 1) * P], ident[:])
                mm.then_inc(turned7 if rd == 1 else turned6, 1)

            def product_v(h, st, b, s_):
                pe.wait_ge(free7, s_ + 2)
                pe.wait_ge(free6, use6(h, st, 1) + 1)
                g = st // 2 % 2
                for k in range(KT):
                    vh, vl = v_hi[:, b, k * P:(k + 1) * P], v_lo[:, b, k * P:(k + 1) * P]
                    mm = split_matmuls(pe, bank(7)[:, 0:QG], vh, vl, dT_hi[:, g, k, :], dT_lo[:, g, k, :],
                                       k == 0, k == KT - 1)
                mm.then_inc(pv_done, 1)

            pe.wait_ge(id_ready, 2)
            for rd in range(3):
                turn_v(0, rd, rd, first=rd == 0)
            pe.sem_inc(pv_done, 2)
            scores(0, 0, 0, 0, 0, first=True)
            scores(0, 0, 0, 1, 0, first=True)
            scores(0, 1, 0, 0, 1)
            scores(0, 1, 0, 1, 1)

            def head(h, b, prep, last):
                for st in range(TT):
                    s_ = TT * h + st
                    h2, st2 = ahead(h, st, FRONT)
                    b2 = b if st + FRONT < TT else 1 - b
                    front = not last or st + FRONT < TT
                    if front:
                        scores(h2, st2, b2, 0, s_ + FRONT)
                    turn_diff(h, st, s_, 0)
                    turn_diff(h, st, s_, 1)
                    if front:
                        scores(h2, st2, b2, 1, s_ + FRONT)
                    turn_diff(h, st, s_, 2)
                    if st % 2:
                        product_v(h, st, b, s_)
                    if prep and V_STEP <= st < V_STEP + 3:
                        turn_v(h + 1, st - V_STEP, use6_v(h, st - V_STEP))

            with pe.Fori(0, HEADS // 2 - 1) as i:
                head(2 * i, 0, True, False)
                head(2 * i + 1, 1, True, False)
            head(HEADS - 2, 0, True, False)
            head(HEADS - 1, 1, False, True)

        @block.scalar
        def _(act):
            act.sem_inc(o_copied, 1)
            act.preload_act_table(ACT.Exp)
            act.wait_ge(lam_spread, 1)
            nc.scalar.activation(lam_exp[:], bank(7)[:, 0:2], ACT.Exp).then_inc(lam_step, 1)

            def round_k(h, b, m):
                if m == 0:
                    act.wait_ge(k_landed, 64 * (h + 1))
                nc.scalar.activation(k_hi[:, b, m, :], k_raw[:, m, :], ACT.Copy).then_inc(k_rounded, 1)

            def round_q(h, b):
                act.wait_ge(q_landed, 32 * (h + 1))
                nc.scalar.activation(q_st[:, b], q_raw[:], ACT.Copy).then_inc(q_rounded, 1)

            def v_high(rd, b, use):
                act.wait_ge(turned6, use + 1)
                k0, k1 = ROUNDS[rd]
                nc.scalar.activation(v_hi[:, b, k0 * P:k1 * P], bank(6)[:, 0:(k1 - k0) * P], ACT.Copy).then_inc(hi6, 1)

            def exp(st, m, s_, first=False):
                act.wait_ge(top_ready[m], s_ + 1)
                if not first:
                    act.wait_ge(diff_ready, s_ - 1)
                nc.scalar.activation(prob[:, st % 2, m, :], bank(3 * m, 3)[:, 0:KEYS], ACT.Exp, scale=SCALE,
                                     bias=neg_top[:, st % 2, m:m + 1], accum_out=total[:, st % 2, m:m + 1]
                                     ).then_inc(exp_done[m], 1)

            def diff_high(h, st, s_, rd):
                if rd == 1:
                    act.wait_ge(turned7, s_ + 1)
                else:
                    act.wait_ge(turned6, use6(h, st, rd // 2) + 1)
                if rd == 0 and st % 2 == 0:
                    act.wait_ge(pv_done, 4 * h + st // 2 + 1)
                k0, k1 = ROUNDS[rd]
                nc.scalar.activation(dT_hi[:, st // 2 % 2, k0:k1, (st % 2) * P:(st % 2 + 1) * P],
                                     bank(7 if rd == 1 else 6)[:, 0:(k1 - k0) * P].rearrange("p (k q) -> p k q", q=P),
                                     ACT.Copy).then_inc(hi7 if rd == 1 else hi6, 1)

            def copy_o(h, st):
                act.wait_ge(pv_done, 4 * h + st // 2 + 3)
                nc.scalar.activation(o_all[:, bass.ds(h, 1), (st - 1) * P:(st + 1) * P].rearrange("p h t -> p (h t)"),
                                     bank(7)[:, 0:QG], ACT.Copy).then_inc(o_copied, 1)

            round_k(0, 0, 0)
            round_k(0, 0, 1)
            round_q(0, 0)
            for rd in range(3):
                v_high(rd, 0, rd)
            exp(0, 0, 0, first=True)
            exp(0, 1, 0, first=True)
            exp(1, 0, 1, first=True)
            exp(1, 1, 1, first=True)

            def head(h, b, prep, last):
                for st in range(TT):
                    s_ = TT * h + st
                    front = not last or st + FRONT < TT
                    diff_high(h, st, s_, 0)
                    diff_high(h, st, s_, 1)
                    if front:
                        exp(st + FRONT, 0, s_ + FRONT)
                    diff_high(h, st, s_, 2)
                    if front:
                        exp(st + FRONT, 1, s_ + FRONT)
                    if st % 2:
                        copy_o(h, st)
                    if prep and st < 2:
                        round_k(h + 1, 1 - b, st)
                    if prep and st == 2:
                        round_q(h + 1, 1 - b)
                    if prep and V_STEP <= st < V_STEP + 3:
                        v_high(st - V_STEP, 1 - b, use6_v(h, st - V_STEP))

            with act.Fori(0, HEADS // 2 - 1) as i:
                head(2 * i, 0, True, False)
                head(2 * i + 1, 1, True, False)
            head(HEADS - 2, 0, True, False)
            head(HEADS - 1, 1, False, True)

        @block.gpsimd
        def _(pool):
            pool.memset(ident[:], 0.0).then_inc(id_ready, 1)
            pool.wait_ge(id_ready, 1)
            pool.affine_select(out=ident[:], in_=ident[:], compare_op=ALU.not_equal, fill=1.0, base=0,
                               pattern=[[-1, P]], channel_multiplier=1).then_inc(id_ready, 1)

            def low_k(h, b, m):
                pool.wait_ge(k_rounded, 2 * h + m + 1)
                pool.tensor_tensor(k_lo[:, b, m, :], k_raw[:, m, :], k_hi[:, b, m, :].bitcast(F32), ALU.subtract
                                   ).then_inc(k_split, 1)

            def low_q(h, b, m):
                pool.wait_ge(q_rounded, h + 1)
                pool.tensor_tensor(q_st[DH:P, b, m, :], q_raw[DH:P, m, :], q_st[DH:P, b, m, :].bitcast(F32), ALU.subtract
                                   ).then_inc(q_split, 1)

            def scale_map1(st, s_):
                pool.wait_ge(scale_ready, s_ + 1)
                pr = prob[:, st % 2, 1, :]
                pool.tensor_tensor(pr, pr, inv_lam[:, st % 2:st % 2 + 1].to_broadcast([P, KEYS]), ALU.mult
                                   ).then_inc(map1_scaled, 1)

            for m in range(2):
                low_k(0, 0, m)
            pool.wait_ge(k_split, 2)
            for m in range(2):
                low_q(0, 0, m)
            pool.wait_ge(q_split, 2)
            scale_map1(0, 0)

            def head(h, b, prep, last):
                for st in range(TT):
                    if prep and 4 <= st < 6:
                        pool.wait_ge(q_split, 2 * (h + 1) + st - 3)
                    if not last or st + 1 < TT:
                        scale_map1(st + 1, TT * h + st + 1)
                    if prep and 1 <= st < 3:
                        low_k(h + 1, 1 - b, st - 1)
                    if prep and 3 <= st < 5:
                        pool.wait_ge(map1_scaled, TT * h + st + 2)
                        low_q(h + 1, 1 - b, st - 3)

            with pool.Fori(0, HEADS // 2 - 1) as i:
                head(2 * i, 0, True, False)
                head(2 * i + 1, 1, True, False)
            head(HEADS - 2, 0, True, False)
            head(HEADS - 1, 1, False, True)

        @block.vector
        def _(dve):
            nc.vector.memset(ones_row[0:1, :], 1.0).then_inc(ones_ready, 1)
            dve.sem_inc(free7, 1)
            dve.wait_ge(lam_landed, 64)
            for k in range(2):
                nc.vector.tensor_tensor(lam_tmp[0:1, k, :], lam_rows[0:1, 2 * k, :], lam_rows[0:1, 2 * k + 1, :], ALU.mult
                                        ).then_inc(lam_ready, 1)
            dve.wait_ge(lam_ready, 2)
            for k in range(2):
                nc.vector.tensor_reduce(lam_dots[0:1, k:k + 1], lam_tmp[0:1, k, :], AXX, ALU.add).then_inc(lam_step, 1)
            dve.wait_ge(lam_step, 3)
            nc.vector.scalar_tensor_tensor(out=lam[:], in0=lam_exp[:, 0:1], scalar=LAM_INIT, in1=lam_exp[:, 1:2],
                                           op0=ALU.add, op1=ALU.subtract).then_inc(lam_ready, 1)
            dve.wait_ge(lam_ready, 3)

            def v_low(h, rd, b, use):
                dve.wait_ge(hi6, use + 1)
                k0, k1 = ROUNDS[rd]
                part = slice(k0 * P, k1 * P)
                nc.vector.tensor_tensor(v_lo[:, b, part], bank(6)[:, 0:(k1 - k0) * P], v_hi[:, b, part].bitcast(F32),
                                        ALU.subtract).then_inc(free6, 1)
                if rd == 2:
                    dve.wait_ge(free6, use + 1)
                    dve.sem_inc(v_read, 1)

            def find_top(st, m, s_):
                dve.wait_ge(scores_done[m], s_ + 1)
                nc.vector.tensor_reduce(top[:, st % 2, m:m + 1], bank(3 * m, 3)[:, 0:KEYS], AXX, ALU.max
                                        ).then_inc(top_found[m], 1)
                dve.wait_ge(top_found[m], s_ + 1)
                nc.vector.tensor_scalar(neg_top[:, st % 2, m:m + 1], top[:, st % 2, m:m + 1], -SCALE, None, ALU.mult
                                        ).then_inc(top_ready[m], 1)

            def invert(st, s_):
                dve.wait_ge(exp_done[0], s_ + 1)
                dve.wait_ge(exp_done[1], s_ + 1)
                nc.vector.reciprocal(inv[:, st % 2, :], total[:, st % 2, :]).then_inc(inv_ready, 1)
                dve.wait_ge(inv_ready, s_ + 1)
                nc.vector.tensor_tensor(inv_lam[:, st % 2:st % 2 + 1], inv[:, st % 2, 1:2], lam[:], ALU.mult
                                        ).then_inc(scale_ready, 1)

            def difference(st, s_):
                dve.wait_ge(map1_scaled, s_ + 1)
                nc.vector.scalar_tensor_tensor(out=diff[:, st % 2, :], in0=prob[:, st % 2, 0, :],
                                               scalar=inv[:, st % 2, 0:1], in1=prob[:, st % 2, 1, :],
                                               op0=ALU.mult, op1=ALU.subtract).then_inc(diff_ready, 1)

            def diff_low(h, st, s_, rd):
                if rd == 1:
                    dve.wait_ge(hi7, s_ + 1)
                else:
                    dve.wait_ge(hi6, use6(h, st, rd // 2) + 1)
                k0, k1 = ROUNDS[rd]
                at = (slice(None), st // 2 % 2, slice(k0, k1), slice((st % 2) * P, (st % 2 + 1) * P))
                nc.vector.tensor_tensor(dT_lo[at], bank(7 if rd == 1 else 6)[:, 0:(k1 - k0) * P]
                                        .rearrange("p (k q) -> p k q", q=P), dT_hi[at].bitcast(F32), ALU.subtract
                                        ).then_inc(free7 if rd == 1 else free6, 1)

            for rd in range(3):
                v_low(0, rd, 0, rd)
            find_top(0, 0, 0)
            find_top(0, 1, 0)
            invert(0, 0)
            find_top(1, 0, 1)
            find_top(1, 1, 1)
            difference(0, 0)

            def head(h, b, prep, last):
                for st in range(TT):
                    s_ = TT * h + st
                    front = not last or st + FRONT < TT
                    nxt = not last or st + 1 < TT
                    if nxt:
                        invert(st + 1, s_ + 1)
                    if front:
                        find_top(st + FRONT, 0, s_ + FRONT)
                    diff_low(h, st, s_, 0)
                    diff_low(h, st, s_, 1)
                    if front:
                        find_top(st + FRONT, 1, s_ + FRONT)
                    diff_low(h, st, s_, 2)
                    if nxt:
                        difference(st + 1, s_ + 1)
                    if prep and V_STEP <= st < V_STEP + 3:
                        v_low(h + 1, st - V_STEP, 1 - b, use6_v(h, st - V_STEP))

            with dve.Fori(0, HEADS // 2 - 1) as i:
                head(2 * i, 0, True, False)
                head(2 * i + 1, 1, True, False)
            head(HEADS - 2, 0, True, False)
            head(HEADS - 1, 1, False, True)


def o_all_start(nc):
    return nc.sbuf_usable_end // 32 * 32 - HEADS * T * 4


def output(nc, t, sem, Region, base, bank, proj_d, gate_d, o_all):
    GROUPS = 8
    GT = 4
    RING = 4
    CONV_T = CONV_W // P
    r = Region(base)
    m_hi = r.take("m_hi", JT * T, F32R)[:].rearrange("p (k t) -> p k t", k=JT)
    lo_at = r.at
    m_lo = r.take("m_lo", JT * T, F32R)[:].rearrange("p (k t) -> p k t", k=JT)
    mixed = Region(lo_at).take("mixed", JT * T)[:].rearrange("p (k t) -> p k t", k=JT)
    o_sq = Region(base + CONV_T * T * 4).take("o_sq", HEADS * T)[:].rearrange("p (h t) -> p h t", h=HEADS)
    wo_raw = r.take("wo_raw", RING * BANK)[:].rearrange("p (s n) -> p s n", s=RING)
    wo_hi = r.take("wo_hi", RING * BANK, F32R)[:].rearrange("p (s n) -> p s n", s=RING)
    wo_lo = r.take("wo_lo", RING * BANK, F32R)[:].rearrange("p (s n) -> p s n", s=RING)
    gate = r.take("gate", D)
    xy = r.take("xy", GT * BANK)[:].rearrange("p (s n) -> p s n", s=GT)
    tmp_at = r.at
    tmp = r.take("tmp", 2 * BANK)[:].rearrange("p (s n) -> p s n", s=2)
    diag = Region(tmp_at).take("diag", TT * P)[:].rearrange("p (t q) -> p t q", t=TT)
    ident = r.take("ident_c", P)
    ones = r.take("ones_c", P)
    root = r.take("root", HEADS * TT)
    no_overflow = r.take("no_overflow", HEADS * TT)
    head_gain = r.take("head_gain", 1)
    root_eps = r.take("root_eps", 1)
    assert r.at <= o_all_start(nc), r.at

    gain_landed = sem("gain_landed")
    gate_landed = sem("gate_landed")
    mix_landed = [sem(f"mix_landed{k}") for k in range(JT // 4)]
    wo_landed = [sem(f"wo_landed{k}") for k in range(RING)]
    wo_hi_ready = [sem(f"wo_hi_ready{k}") for k in range(RING)]
    wo_lo_ready = [sem(f"wo_lo_ready{k}") for k in range(RING)]
    wo_used = [sem(f"wo_used{k}") for k in range(RING)]
    id2_ready = sem("id2_ready")
    const_ready = sem("const_ready")
    o_squared = sem("o_squared")
    o_bounded = sem("o_bounded")
    o_summed = sem("o_summed")
    o_root = sem("o_root")
    o_recip = sem("o_recip")
    diag_ready = sem("diag_ready")
    spread = sem("spread")
    o_normed = sem("o_normed")
    mix_gated = sem("mix_gated")
    mix_rounded = sem("mix_rounded")
    mix_ready = sem("mix_ready")
    sum_done = sem("sum_done")
    sum_freed = sem("sum_freed")
    y_done = sem("y_done")
    xo_landed = sem("xo_landed")
    out_stored = sem("out_stored")

    x_v = t["x"].rearrange("b (g s p) d -> p (b g) s d", p=P, s=GT)
    out_v = t["out"].rearrange("b (g s p) d -> p (b g) s d", p=P, s=GT)

    def w_row(k):
        return (ATT_W + k * P, (N_GC - N_GA + k) * P) if k < CONV_T else ((k - CONV_T) * P, (k - CONV_T) * P)

    with nc.Block(name="output") as block:

        @block.sync
        def _(sp):
            def columns(cb):
                return bass.ds((cb + 1) * BANK - BANK, BANK)

            def load_w(n4, k, cb, first=False):
                if not first:
                    sp.wait_ge(wo_lo_ready[k % RING], n4)
                row = w_row(k)[0]
                sp.dma_start(wo_raw[:, k % RING, :], t["w_out"][0, row:row + P, columns(cb)]
                             ).then_inc(wo_landed[k % RING], 16)

            def group(g, half, cb, first=False):
                uses = [4 * g + q for q in range(JT // RING)]
                if not isinstance(g, int):
                    uses = [sp.snap(u) for u in uses]
                for k in range(JT):
                    load_w(uses[k // RING], k, cb, first and k < RING)
                    if first and 0 <= k - RING + 1 < 4:
                        for kk in range(4 * (k - RING + 1), 4 * (k - RING + 2)):
                            row = w_row(kk)[1]
                            sp.dma_start(mixed[:, kk, :], proj_d[row:row + P, :]).then_inc(mix_landed[kk // 4], 16)
                    if k == 4 and not first:
                        sp.wait_ge(y_done, 4 * g)
                        last_cb = cb if half else cb - 1
                        sp.dma_start(out_v[:, 1 - half, :, columns(last_cb)], xy[:]).then_inc(out_stored, 16)
                    if k == 8:
                        if first:
                            sp.dma_start(gate[:], gate_d.to_broadcast([P, D])).then_inc(gate_landed, 16)
                        else:
                            sp.wait_ge(out_stored, 16 * g)
                        sp.dma_start(xy[:], x_v[:, half, :, columns(cb)]).then_inc(xo_landed, 16)

            sp.dma_start(head_gain[:], t["sub_norm_g"].rearrange("l d -> d l")).then_inc(gain_landed, 16)
            group(0, 0, 0, first=True)
            group(1, 1, 0)
            with sp.Fori(1, GROUPS // 2) as cb:
                for half in range(2):
                    group(2 * cb + half, half, cb)
            sp.wait_ge(y_done, GT * GROUPS)
            sp.dma_start(out_v[:, 1, :, D - BANK:D], xy[:]).then_inc(out_stored, 16)
            sp.wait_ge(out_stored, 16 * GROUPS)

        @block.gpsimd
        def _(pool):
            pool.memset(ident[:], 0.0).then_inc(id2_ready, 1)
            pool.wait_ge(id2_ready, 1)
            pool.affine_select(out=ident[:], in_=ident[:], compare_op=ALU.not_equal, fill=1.0, base=0,
                               pattern=[[-1, P]], channel_multiplier=1).then_inc(id2_ready, 1)
            with pool.Fori(0, GROUPS * JT // RING) as n:
                for s_ in range(RING):
                    pool.wait_ge(wo_hi_ready[s_], n + 1)
                    pool.tensor_tensor(wo_lo[:, s_, :], wo_raw[:, s_, :], wo_hi[:, s_, :].bitcast(F32), ALU.subtract
                                       ).then_inc(wo_lo_ready[s_], 1)

        @block.tensor
        def _(pe):
            pe.wait_ge(const_ready, 1)
            for h in range(HEADS):
                pe.wait_ge(o_squared, h + 1)
                for tt in range(TT):
                    mm = pe.matmul(bank(4)[:, h * TT + tt:h * TT + tt + 1], o_sq[:, h, tt * P:(tt + 1) * P], ones[:, 0:1],
                                   start=True, stop=True, skip_group_check=True)
            mm.then_inc(o_summed, 1)

            def spread_norm(h):
                pe.wait_ge(diag_ready, h + 1)
                if h >= 2:
                    pe.wait_ge(o_normed, h - 1)
                for tt in range(TT):
                    b = 4 + 2 * (h % 2) + tt // 4
                    mm = pe.matmul(bank(b)[:, (tt % 4) * P:(tt % 4 + 1) * P], ones[:], diag[:, tt, :],
                                   start=True, stop=True, skip_group_check=True)
                mm.then_inc(spread, 1)

            def group(g, half, first=False):
                for k in range(JT):
                    if first and k >= CONV_T:
                        if k == CONV_T:
                            spread_norm(0)
                        if k + 1 < JT:
                            spread_norm(k + 1 - CONV_T)
                    if first:
                        pe.wait_ge(mix_ready, k + 1)
                    n = 4 * g + k // RING + 1
                    s_ = k % RING
                    pe.wait_ge(wo_hi_ready[s_], n)
                    pe.wait_ge(wo_lo_ready[s_], n)
                    for q in range(GT):
                        if k == 0 and not first:
                            if isinstance(g, int):
                                pass
                            else:
                                pe.wait_ge(sum_freed, 4 * g - 8 + q + 1)
                        tok = slice((half * GT + q) * P, (half * GT + q + 1) * P)
                        mm = split_matmuls(pe, bank(half * GT + q), m_hi[:, k, tok], m_lo[:, k, tok],
                                           wo_hi[:, s_, :], wo_lo[:, s_, :], k == 0, k == JT - 1)
                        if k == JT - 1:
                            mm.then_inc(sum_done, 1)
                    if k < JT - 1:
                        mm.then_inc(wo_used[s_], 1)
                    else:
                        pe.wait_ge(sum_done, 4 * g + GT)
                        pe.sem_inc(wo_used[s_], 1)

            group(0, 0, first=True)
            pe.wait_ge(o_normed, HEADS)
            group(1, 1)
            with pe.Fori(1, GROUPS // 2) as cb:
                for half in range(2):
                    group(2 * cb + half, half)

        @block.scalar
        def _(act):
            for h in range(HEADS):
                act.wait_ge(o_bounded, h + 1)
                nc.scalar.activation(o_sq[:, h, :], o_sq[:, h, :], ACT.Square, scale=O_DOWN).then_inc(o_squared, 1)

            def round_w(g, k, first=False):
                s_ = k % RING
                n = 4 * g + k // RING
                act.wait_ge(wo_landed[s_], 16 * (n + 1))
                if not (first and k < RING):
                    act.wait_ge(wo_used[s_], n)
                nc.scalar.activation(wo_hi[:, s_, :], wo_raw[:, s_, :], ACT.Copy).then_inc(wo_hi_ready[s_], 1)

            def round_mix(k):
                nc.scalar.activation(m_hi[:, k, :], mixed[:, k, :], ACT.Copy).then_inc(mix_rounded, 1)

            for k in range(CONV_T):
                if k == RING:
                    act.wait_ge(o_summed, 1)
                    act.wait_ge(const_ready, 2)
                    nc.scalar.activation(root[:], bank(4)[:, 0:HEADS * TT], ACT.Sqrt, scale=1.0 / P, bias=root_eps[:]
                                         ).then_inc(o_root, 1)
                round_w(0, k, first=True)
                act.wait_ge(mix_landed[k // 4], 16 * 4)
                round_mix(k)
            for k in range(CONV_T, JT):
                round_w(0, k, first=True)
                act.wait_ge(mix_gated, k - CONV_T + 1)
                round_mix(k)
            for k in range(JT):
                round_w(1, k)
            with act.Fori(1, GROUPS // 2) as cb:
                for half in range(2):
                    for k in range(JT):
                        round_w(2 * cb + half, k)

        @block.vector
        def _(dve):
            nc.vector.memset(ones[:], 1.0).then_inc(const_ready, 1)
            nc.vector.memset(root_eps[:], EPS * O_DOWN ** 2).then_inc(const_ready, 1)
            for h in range(HEADS):
                nc.vector.tensor_scalar(o_sq[:, h, :], o_all[:, h, :], O_BOUND, -O_BOUND, ALU.min, ALU.max
                                        ).then_inc(o_bounded, 1)

            def low_mix(k):
                dve.wait_ge(mix_rounded, k + 1)
                nc.vector.tensor_tensor(m_lo[:, k, :], mixed[:, k, :], m_hi[:, k, :].bitcast(F32), ALU.subtract
                                        ).then_inc(mix_ready, 1)

            for k in range(RING):
                low_mix(k)
            dve.wait_ge(gain_landed, 16)
            nc.vector.tensor_scalar(head_gain[:], head_gain[:], (1.0 - LAM_INIT) * O_DOWN, None, ALU.mult
                                    ).then_inc(o_recip, 1)
            dve.wait_ge(o_root, 1)
            nc.vector.reciprocal(root[:], root[:]).then_inc(o_recip, 1)
            nc.vector.tensor_scalar(no_overflow[:], bank(4)[:, 0:HEADS * TT], SQ_OVERFLOW, None, ALU.is_lt).then_inc(o_recip, 1)
            dve.wait_ge(o_recip, 3)
            nc.vector.tensor_tensor(root[:], root[:], no_overflow[:], ALU.mult).then_inc(o_recip, 1)
            dve.wait_ge(o_recip, 4)
            dve.wait_ge(id2_ready, 2)

            def spread_diag(h):
                if h >= 1:
                    dve.wait_ge(spread, h)
                nc.vector.tensor_tensor(diag[:], ident[:].unsqueeze(1).to_broadcast([P, TT, P]),
                                        root[:, h * TT:(h + 1) * TT].unsqueeze(2).to_broadcast([P, TT, P]), ALU.mult
                                        ).then_inc(diag_ready, 1)

            spread_diag(0)
            for k in range(RING, CONV_T):
                low_mix(k)
            for h in range(HEADS):
                if h + 1 < HEADS:
                    spread_diag(h + 1)
                k = CONV_T + h
                dve.wait_ge(spread, h + 1)
                nc.vector.scalar_tensor_tensor(out=o_all[:, h, :], in0=o_all[:, h, :], scalar=head_gain[:],
                                               in1=bank(4 + 2 * (h % 2), 2), op0=ALU.mult, op1=ALU.mult
                                               ).then_inc(o_normed, 1)
                dve.wait_ge(o_normed, h + 1)
                dve.wait_ge(mix_landed[k // 4], 16 * 4)
                nc.vector.tensor_tensor(mixed[:, k, :], mixed[:, k, :], o_all[:, h, :], ALU.mult).then_inc(mix_gated, 1)
                low_mix(k)

            def result(g, half, cb):
                for q in range(GT):
                    dve.wait_ge(sum_done, 4 * g + q + 1)
                    if q == 0:
                        dve.wait_ge(xo_landed, 16 * (g + 1))
                    nc.vector.tensor_tensor(tmp[:, q % 2, :], bank(half * GT + q), gate[:, bass.ds(cb * BANK, BANK)], ALU.mult
                                            ).then_inc(sum_freed, 1)
                    dve.wait_ge(sum_freed, 4 * g + q + 1)
                    nc.vector.tensor_tensor(xy[:, q, :], xy[:, q, :], tmp[:, q % 2, :], ALU.add).then_inc(y_done, 1)

            dve.wait_ge(gate_landed, 16)
            with dve.Fori(0, GROUPS // 2) as cb:
                for half in range(2):
                    result(2 * cb + half, half, cb)


_INS = ["x", "c", "ctx", "c_ctx", "w_ada", "b_ada", "norm_g", "w_in", "q_norm_g", "k_norm_g", "lam_q1", "lam_k1",
        "lam_q2", "lam_k2", "sub_norm_g", "conv_w", "conv_b", "conv_ln_g", "conv_ln_b", "w_out"]


def kernel(**inputs):
    import concourse.bacc as _bacc
    from concourse.bass_utils import run_bass_kernel_spmd as _run

    nc = _bacc.Bacc("TRN2", target_bir_lowering=False, num_devices=1)
    cos, sin = rope_tables()
    arrays, tensors = {}, {}
    for name in _INS + ["rope_cos", "rope_sin"]:
        a = {"rope_cos": cos, "rope_sin": sin}.get(name)
        if a is None:
            a = np.ascontiguousarray(inputs[name])
        arrays[f"in_{name}_dram"] = a
        tensors[name] = nc.dram_tensor(f"in_{name}_dram", a.shape, mybir.dt.from_np(a.dtype), kind="ExternalInput").ap()
    tensors["out"] = nc.dram_tensor("out_0_dram", (1, T, D), F32, kind="ExternalOutput").ap()
    with nc.allow_non_contiguous_dma(reason="gains of 64 or 128 channels, one per partition"):
        build(nc, tensors)
    r = _run(nc, [arrays], core_ids=[0])
    return r.results[0]["out_0_dram"]
```

```python
from contextlib import ExitStack
import math

import numpy as np

import concourse.bass as bass
from concourse import mybir

F32 = mybir.dt.float32
F32R = mybir.dt.float32r
ALU = mybir.AluOpType
ACT = mybir.ActivationFunctionType
AXX = mybir.AxisListType.X

P = 128
D = 2048
JT = D // P
T = 1024
TC = 256
TT = T // P
HEADS = 8
DH = 64
ATT_W = 1024
CONV_W = 1024
CONV_K = 31
HALO = CONV_K // 2
GRID_W = 64
ROPE_BASE = 10000.0
EPS = 1e-6
Q0, K0, V0, GA0, U0 = 0, 1024, 2048, 3072, 4096
GC0 = U0 + 2 * CONV_W
CT = 8
CH = 4
JC = JT // CH
KEYS = TC + T
KT = KEYS // P
SCALE = 1.0 / math.sqrt(DH)
LAM_INIT = 0.8 - 0.6 * math.exp(-0.3 * 0)
BANK = 512
P0_DOWN = 11
O_BOUND = 2.0 ** 65
O_DOWN = 2.0 ** -20
SQ_OVERFLOW = 2.0 ** 128 * O_DOWN ** 2

N_VC, N_KC, N_U, N_GA, N_GC, N_V, N_K, N_Q, N_END = 0, 8, 16, 32, 40, 48, 56, 64, 72


def rope_tables():
    tok = np.arange(T)
    nf = DH // 4
    inv = ROPE_BASE ** (-np.arange(nf, dtype=np.float32) / np.float32(nf))
    row = (tok // GRID_W).astype(np.float32)[:, None] * inv.astype(np.float32)
    col = (tok % GRID_W).astype(np.float32)[:, None] * inv.astype(np.float32)
    ang = np.concatenate([row, row, col, col], axis=-1).astype(np.float32)
    sign = np.concatenate([-np.ones(nf), np.ones(nf)] * 2).astype(np.float32)
    cos = np.cos(ang).T
    sin = (np.sin(ang) * sign).T
    return (np.ascontiguousarray(np.concatenate([cos, cos]).astype(np.float32)),
            np.ascontiguousarray(np.concatenate([sin, sin]).astype(np.float32)))


def split_matmuls(pe, out, w_hi, w_lo, x_hi, x_lo, start, stop):
    pe.matmul(out, w_hi, x_hi, start=start, stop=False)
    pe.matmul(out, w_hi, x_lo, start=False, stop=False)
    return pe.matmul(out, w_lo, x_hi, start=False, stop=stop)


def build(nc, t):
    with ExitStack() as ctx:
        sem_names = []

        def sem(name):
            sem_names.append(name)
            return ctx.enter_context(nc.semaphore(name))

        base = (nc.sbuf_base + 31) // 32 * 32
        limit = nc.sbuf_usable_end // 32 * 32

        class Region:
            def __init__(self, start):
                self.at = start

            def take(self, name, cols, dtype=F32):
                h = nc.alloc_sbuf_tensor_at(name, [P, cols], dtype, offset=self.at)
                self.at += (cols * 4 + 31) // 32 * 32
                assert self.at <= limit, (name, self.at, limit)
                return h

        o_all = Region(limit - HEADS * T * 4).take("o_all", HEADS * T)[:].rearrange("p (h t) -> p h t", h=HEADS)

        p0_sum = Region(o_all_start(nc)).take("p0_sum", HEADS * TT)

        psum = ctx.enter_context(nc.psum_tensor("psum", [P, 8 * BANK], F32))

        def bank(b, n=1):
            return psum[:, b * BANK:(b + n) * BANK]

        ctx_kv_d = nc.dram_tensor("ctx_kv", [(N_U - N_VC) * P, TC], F32, kind="Internal").ap()
        proj_d = nc.dram_tensor("proj", [(N_END - N_GA) * P, T], F32, kind="Internal").ap()
        gate_d = nc.dram_tensor("gate_row", [1, D], F32, kind="Internal").ap()

        projections(nc, t, sem, Region, base, bank, ctx_kv_d, proj_d, gate_d)
        attention(nc, t, sem, Region, base, bank, ctx_kv_d, proj_d, o_all, p0_sum)
        output(nc, t, sem, Region, base, bank, proj_d, gate_d, o_all, p0_sum)


def projections(nc, t, sem, Region, base, bank, ctx_kv_d, proj_d, gate_d):
    r = Region(base)
    h_hi = r.take("h_hi", JT * T, F32R)[:].rearrange("p (j t) -> p j t", j=JT)
    lo_at = r.at
    h_lo = r.take("h_lo", JT * T, F32R)[:].rearrange("p (j t) -> p j t", j=JT)
    w_raw = r.take("w_raw", JT * P)[:].rearrange("p (c j n) -> p c j n", c=CH, n=P)
    w_hi = r.take("w_hi", JT * P, F32R)[:].rearrange("p (c j n) -> p c j n", c=CH, n=P)
    w_lo = r.take("w_lo", JT * P, F32R)[:].rearrange("p (c j n) -> p c j n", c=CH, n=P)
    shared_at = r.at
    hc = r.take("hc", JT * 2 * TC, F32R)[:].rearrange("p (j t) -> p j t", j=JT)
    late_at = r.at
    stage = r.take("stage", 2 * T)[:].rearrange("p (s t) -> p s t", s=2)
    evac = r.take("evac", 2 * T)[:].rearrange("p (s t) -> p s t", s=2)
    y_pad = r.take("y_pad", T + 2 * HALO + 2)
    n_par = CONV_K + 3
    chan_par = r.take("chan_par", CT * n_par)[:].rearrange("p (i k) -> p i k", i=CT)
    tap_w = r.take("tap_w", n_par)
    block_ones = r.take("block_ones", P)
    mean_ones = r.take("mean_ones", P)
    eps_col, q_gain, k_gain = (r.take(name, 1)[:] for name in ("eps_col", "q_gain", "k_gain"))
    mod = r.take("mod", 4 * JT)[:].rearrange("p (k j v) -> p k j v", k=2, v=2)

    xT = Region(lo_at).take("xT", JT * T)[:].rearrange("p (j t) -> p j t", j=JT)
    s = Region(base)
    ada_w = s.take("ada_w", CH * JC * BANK)[:].rearrange("p (c j n) -> p c j n", c=CH, n=BANK)
    x_tok = s.take("x_tok", 2 * D)[:].rearrange("p (s d) -> p s d", s=2)
    x_sq = s.take("x_sq", D)
    chan_rows = s.take("chan_rows", CONV_W)
    ident = s.take("ident", P)
    c_col = s.take("c_col", 2 * JT)[:].rearrange("p (v j) -> p v j", v=2)
    c_act = s.take("c_act", 2 * JT)[:].rearrange("p (j v) -> p j v", v=2)
    ln_x = s.take("ln_x", 3 * (TT + 2))[:].rearrange("p (k t) -> p k t", k=3)
    g_col = s.take("g_col", JT)
    b_col = s.take("b_col", 2 * JT)[:].rearrange("p (k j) -> p k j", k=2)
    assert s.at <= lo_at
    s = Region(shared_at)
    ada_rows = s.take("ada_rows", 3 * D)
    b_gate = s.take("b_gate", D)
    s = Region(late_at)
    xcT = s.take("xcT", JT * TC)[:].rearrange("p (j t) -> p j t", j=JT)
    conv = Region(shared_at).take("conv", CT * T)[:].rearrange("p (i t) -> p i t", i=CT)
    s = Region(shared_at)
    cos = s.take("cos", T)
    sin = s.take("sin", T)
    sq = s.take("sq", 2 * T)[:].rearrange("p (s t) -> p s t", s=2)
    roped = s.take("roped", 2 * T)[:].rearrange("p (s t) -> p s t", s=2)
    turned = s.take("turned", T)
    rstd = s.take("rstd", T)

    ada_v = t["w_ada"].rearrange("l (p j) n -> p (l j) n", p=P)
    w_v = t["w_in"].rearrange("l (p j) n -> p (l j) n", p=P)

    par_landed = sem("par_landed")
    ada_landed = [sem(f"ada_landed{c}") for c in range(CH)]
    ada_used = [sem(f"ada_used{c}") for c in range(CH)]
    ident_ready = sem("ident_ready")
    c_ready = sem("c_ready")
    rows_ready = sem("rows_ready")
    cols_done = sem("cols_done")
    mod_ready = sem("mod_ready")
    x_landed = [sem(f"x_landed{p}") for p in range(2)]
    x_squared = sem("x_squared")
    x_root = sem("x_root")
    x_recip = sem("x_recip")
    x_normed = sem("x_normed")
    x_turned = sem("x_turned")
    xT_by_act = sem("xT_by_act")
    xT_by_dve = sem("xT_by_dve")
    hc_mod = sem("hc_mod")
    hc_hi = sem("hc_hi")
    hc_ready = sem("hc_ready")
    h_mod = sem("h_mod")
    h_hi_done = sem("h_hi_done")
    h_ready = sem("h_ready")
    par_done = sem("par_done")
    mod_step = sem("mod_step")
    gate_stored = sem("gate_stored")
    w_landed = [sem(f"w_landed{c}") for c in range(CH)]
    w_hi_ready = [sem(f"w_hi_ready{c}") for c in range(CH)]
    w_lo_ready = [sem(f"w_lo_ready{c}") for c in range(CH)]
    w_used = [sem(f"w_used{c}") for c in range(CH)]
    tile_done = w_used[CH - 1]
    ctx_half = sem("ctx_half")
    ctx_freed = sem("ctx_freed")
    psum_freed = sem("psum_freed")
    ctx_squared = sem("ctx_squared")
    ctx_summed = sem("ctx_summed")
    ctx_root = sem("ctx_root")
    ctx_recip = sem("ctx_recip")
    ctx_normed = sem("ctx_normed")
    stored = [sem(f"stored{p}") for p in range(2)]
    glu_in = sem("glu_in")
    glu_used = sem("glu_used")
    conv_done = sem("conv_done")
    mean_done = sem("mean_done")
    centred = sem("centred")
    ln_squared = sem("ln_squared")
    ln_sq_used = sem("ln_sq_used")
    ln_root = sem("ln_root")
    ln_ready = sem("ln_ready")
    ln_recip = sem("ln_recip")
    taps_ready = sem("taps_ready")
    tap_done = sem("tap_done")
    gate_used = sem("gate_used")
    eps_ready = sem("eps_ready")
    rope_landed = sem("rope_landed")
    conv_used = sem("conv_used")
    qk_scaled = sem("qk_scaled")
    qk_cos = sem("qk_cos")
    qk_turned = sem("qk_turned")
    qk_roped = sem("qk_roped")
    qk_recip = sem("qk_recip")
    qk_summed = sem("qk_summed")
    qk_root = sem("qk_root")
    qk_done = sem("qk_done")

    N_PAR = 14
    X_TILES = TT + 2

    with nc.Block(name="projections") as block:

        @block.sync
        def _(sp):
            sp.dma_start(c_col[:, 0, :], t["c"].rearrange("l (p j) -> (l p) j", p=P)).then_inc(par_landed, 16)
            sp.dma_start(c_col[:, 1, :], t["c_ctx"].rearrange("(p j) -> p j", p=P)).then_inc(par_landed, 16)
            sp.dma_start(g_col[:], t["norm_g"].rearrange("l (p j) -> (l p) j", p=P)).then_inc(par_landed, 16)
            for k in range(2):
                sp.dma_start(b_col[:, k, :], t["b_ada"][:, k * D:(k + 1) * D].rearrange("l (p j) -> (l p) j", p=P)
                             ).then_inc(par_landed, 16)
            sp.dma_start(b_gate[0:1, :], t["b_ada"][:, 2 * D:]).then_inc(par_landed, 16)
            sp.dma_start(chan_rows[0:CONV_K, :], t["conv_w"].rearrange("l k n -> (l k) n")).then_inc(par_landed, 16)
            for k, name in enumerate(("conv_b", "conv_ln_g", "conv_ln_b")):
                sp.dma_start(chan_rows[CONV_K + k:CONV_K + k + 1, :], t[name]).then_inc(par_landed, 16)
            for m in range(2):
                sp.dma_start(q_gain[m * DH:(m + 1) * DH, :], t["q_norm_g"].rearrange("l d -> d l")).then_inc(par_landed, 16)
                sp.dma_start(k_gain[m * DH:(m + 1) * DH, :], t["k_norm_g"].rearrange("l d -> d l")).then_inc(par_landed, 16)

            def load_ada(nb, first=False):
                for c in range(CH):
                    if not first:
                        sp.wait_ge(ada_used[c], nb)
                    sp.dma_start(ada_w[:, c], ada_v[:, c * JC:(c + 1) * JC, bass.ds(nb * BANK, BANK)]
                                 ).then_inc(ada_landed[c], 16)

            load_ada(0, first=True)
            with sp.Fori(1, 12) as nb:
                load_ada(nb)

            def load_w(n, col, first=False):
                for c in range(CH):
                    if not first:
                        sp.wait_ge(w_lo_ready[c], n)
                    sp.dma_start(w_raw[:, c], w_v[:, c * JC:(c + 1) * JC, bass.ds(col, P)]
                                 ).then_inc(w_landed[c], 16)

            def store_ctx(n, par, ready, count):
                sp.wait_ge(ready, count)
                sp.dma_start(ctx_kv_d[bass.ds(n * P, P), :], stage[:, par, 0:TC]).then_inc(stored[par], 16)

            def store(n, par):
                sp.dma_start(proj_d[bass.ds((n - N_GA) * P, P), :], stage[:, par, :]).then_inc(stored[par], 16)

            def store_after_act(n, par):
                sp.wait_ge(psum_freed, n - N_U + 1)
                store(n, par)

            def store_gc(n, par):
                sp.wait_ge(gate_used, n - N_GC + 2)
                store(n, par)

            def store_qk(n, par):
                sp.wait_ge(qk_done, n - N_K + 1)
                store(n, par)

            sp.wait_ge(mod_step, 1)
            sp.dma_start(gate_d, ada_rows[0:1, 2 * D:3 * D]).then_inc(gate_stored, 16)

            load_w(0, V0, first=True)
            load_w(1, V0 + P)
            with sp.Fori(1, 4) as i:
                for s_ in range(2):
                    load_w(2 * i + s_, V0 + (2 * i + s_) * P)
                    store_ctx(2 * i + s_ - 2, s_, ctx_freed, 2 * i + s_ - 1)
            for s_ in range(2):
                load_w(N_KC + s_, K0 + s_ * P)
                store_ctx(N_KC + s_ - 2, s_, ctx_freed, N_KC + s_ - 1)
            with sp.Fori(1, 4) as i:
                for s_ in range(2):
                    load_w(N_KC + 2 * i + s_, K0 + (2 * i + s_) * P)
                    store_ctx(N_KC + 2 * i + s_ - 2, s_, ctx_normed, 2 * i + s_ - 1)
            for s_ in range(2):
                load_w(N_U + s_, U0 + s_ * CONV_W)
                store_ctx(N_U + s_ - 2, s_, ctx_normed, CT + s_ - 1)
            with sp.Fori(1, CT) as i:
                for s_ in range(2):
                    load_w(N_U + 2 * i + s_, U0 + i * P + s_ * CONV_W)
            for n0, col0, last_store, own_store in ((N_GA, GA0, None, store_after_act),
                                                    (N_GC, GC0, store_after_act, store_gc),
                                                    (N_V, V0, store_gc, store_after_act),
                                                    (N_K, K0, store_after_act, store_qk),
                                                    (N_Q, Q0, store_qk, store_qk)):
                for s_ in range(2):
                    load_w(n0 + s_, col0 + s_ * P)
                    if last_store:
                        last_store(n0 + s_ - 2, s_)
                if n0 == N_V:
                    sp.wait_ge(conv_used, CT)
                    sp.dma_start(cos[:], t["rope_cos"]).then_inc(rope_landed, 16)
                    sp.dma_start(sin[:], t["rope_sin"]).then_inc(rope_landed, 16)
                with sp.Fori(1, CT // 2) as i:
                    for s_ in range(2):
                        load_w(n0 + 2 * i + s_, col0 + (2 * i + s_) * P)
                        own_store(n0 + 2 * i + s_ - 2, s_)
            for s_ in range(2):
                store_qk(N_END - 2 + s_, s_)
            for par in range(2):
                sp.wait_ge(stored[par], 16 * ((N_U - N_VC) + (N_END - N_GA)) // 2)

        @block.gpsimd
        def _(pool):
            pool.memset(ident[:], 0.0).then_inc(ident_ready, 1)
            pool.wait_ge(ident_ready, 1)
            pool.affine_select(out=ident[:], in_=ident[:], compare_op=ALU.not_equal, fill=1.0, base=0,
                               pattern=[[-1, P]], channel_multiplier=1).then_inc(ident_ready, 1)

            xl = t["x"].rearrange("b t d -> (b t) d")
            xc = t["ctx"].rearrange("b t d -> (b t) d")
            for k in range(2):
                pool.dma_start(x_tok[:, k], xl[k * P:(k + 1) * P, :]).then_inc(x_landed[k], 16)
            with pool.Fori(1, TT // 2) as i:
                for k in range(2):
                    pool.wait_ge(x_turned, 8 * i + 4 * k - 4)
                    pool.dma_start(x_tok[:, k], xl[bass.ds((2 * i + k) * P, P), :]).then_inc(x_landed[k], 16)
            for k in range(2):
                pool.wait_ge(x_turned, 4 * (TT + k - 1))
                pool.dma_start(x_tok[:, k], xc[k * P:(k + 1) * P, :]).then_inc(x_landed[k], 16)

            with pool.Fori(0, N_END) as n:
                for c in range(CH):
                    pool.wait_ge(w_hi_ready[c], n + 1)
                    pool.tensor_tensor(w_lo[:, c], w_raw[:, c], w_hi[:, c].bitcast(F32), ALU.subtract
                                       ).then_inc(w_lo_ready[c], 1)

        @block.tensor
        def _(pe):
            pe.wait_ge(ident_ready, 2)
            pe.wait_ge(par_landed, 16 * N_PAR)
            for i in range(CT):
                mm = pe.matmul(bank(6)[:, i * n_par:(i + 1) * n_par], chan_rows[0:n_par, i * P:(i + 1) * P],
                               ident[0:n_par, 0:n_par], start=True, stop=True)
            mm.then_inc(cols_done, 1)

            def ada_block(nb, s_, first=False):
                for c in range(CH):
                    pe.wait_ge(ada_landed[c], 16 * (nb + 1))
                    if c == 0 and not first:
                        pe.wait_ge(rows_ready, nb - 1)
                    for j in range(JC):
                        mm = pe.matmul(bank(s_)[0:2, :], c_act[:, c * JC + j, :], ada_w[:, c, j, :],
                                       start=(c == 0 and j == 0), stop=(c == CH - 1 and j == JC - 1))
                    mm.then_inc(ada_used[c], 1)

            def turn_x(i, k, first=False):
                pe.wait_ge(x_normed, i + 1)
                if not first:
                    pe.wait_ge(xT_by_act, 2 * i)
                    pe.wait_ge(xT_by_dve, 2 * i)
                xv = x_tok[:, k, :].rearrange("p (c j) -> p j c", j=JT)
                for b in range(4):
                    for j in range(4):
                        mm = pe.transpose(bank(2 + b)[:, j * P:(j + 1) * P], xv[:, 4 * b + j, :], ident[:])
                    mm.then_inc(x_turned, 1)

            pe.wait_ge(c_ready, 1)
            ada_block(0, 0, first=True)
            turn_x(0, 0, first=True)
            ada_block(1, 1, first=True)
            turn_x(1, 1)
            with pe.Fori(1, 5) as i:
                for s_ in range(2):
                    ada_block(2 * i + s_, s_)
                    turn_x(2 * i + s_, s_)
            for nb in (10, 11):
                ada_block(nb, nb % 2)
            pe.wait_ge(rows_ready, 12)
            pe.wait_ge(par_done, 1)
            for k in range(2):
                for j in range(JT):
                    rows = ada_rows[0:2, k * D:(k + 1) * D].rearrange("v (c j) -> v j c", j=JT)[:, j, :]
                    mm = pe.matmul(bank(6)[:, 2 * (k * JT + j):2 * (k * JT + j) + 2], rows, ident[0:2, 0:2],
                                   start=True, stop=True)
            mm.then_inc(cols_done, 1)

            def ctx_tile(n, s_, head=False, second=False):
                if not (head or second):
                    pe.wait_ge(ctx_freed, n - 1)
                for c in range(CH):
                    pe.wait_ge(w_hi_ready[c], n + 1)
                    pe.wait_ge(w_lo_ready[c], n + 1)
                    for j in range(JC):
                        jj = c * JC + j
                        if head:
                            pe.wait_ge(hc_ready, jj + 1)
                        pe.matmul(bank(s_), w_hi[:, c, j, :], hc[:, jj, :], start=(jj == 0), stop=False,
                                  skip_group_check=True)
                        mm = pe.matmul(bank(s_)[:, 0:TC], w_lo[:, c, j, :], hc[:, jj, 0:TC], start=False,
                                       stop=(jj == JT - 1), skip_group_check=True)
                    mm.then_inc(w_used[c], 1)

            def ctx_sums(k, par):
                pe.wait_ge(ctx_squared, k + 1)
                pe.matmul(bank(4 + par)[:, 0:TC], block_ones[:], evac[:, par, 512:512 + TC], start=True, stop=True
                          ).then_inc(ctx_summed, 1)

            ctx_tile(0, 0, head=True)
            ctx_tile(1, 1, second=True)
            with pe.Fori(1, 4) as i:
                for s_ in range(2):
                    ctx_tile(2 * i + s_, s_)
            ctx_tile(N_KC, 0)
            ctx_tile(N_KC + 1, 1)
            ctx_sums(0, 0)
            with pe.Fori(1, 4) as i:
                for s_ in range(2):
                    ctx_tile(N_KC + 2 * i + s_, s_)
                    ctx_sums(2 * i + s_ - 1, (s_ + 1) % 2)

            def tile(n, s_):
                for c in range(CH):
                    pe.wait_ge(w_hi_ready[c], n + 1)
                    pe.wait_ge(w_lo_ready[c], n + 1)
                    for j in range(JC):
                        jj = c * JC + j
                        for w, x, last in ((w_hi, h_hi, False), (w_hi, h_lo, False), (w_lo, h_hi, jj == JT - 1)):
                            for hf in range(2):
                                mm = pe.matmul(bank(2 * s_ + hf), w[:, c, j, :], x[:, jj, hf * BANK:(hf + 1) * BANK],
                                               start=(jj == 0 and w is w_hi and x is h_hi), stop=last)
                    mm.then_inc(w_used[c], 1)

            pe.wait_ge(h_ready, JT)
            pe.wait_ge(ctx_freed, N_U)
            tile(N_U, 0)
            ctx_sums(CT - 1, 1)
            tile(N_U + 1, 1)

            def pair(n):
                for s_ in range(2):
                    pe.wait_ge(psum_freed, n + s_ - N_U - 1)
                    tile(n + s_, s_)

            with pe.Fori(1, CT) as i:
                pair(N_U + 2 * i)
            pair(N_GA)
            pe.wait_ge(ctx_root, CT)
            for i in range(CT):
                pe.wait_ge(conv_done, i + 1)
                for hf in range(2):
                    mm = pe.matmul(bank(4 + hf), mean_ones[:], conv[:, i, hf * BANK:(hf + 1) * BANK],
                                   start=(i == 0), stop=(i == CT - 1))
            mm.then_inc(mean_done, 1)
            pair(N_GA + 2)
            for i in range(CT):
                pe.wait_ge(ln_squared, i + 1)
                for hf in range(2):
                    mm = pe.matmul(bank(6 + hf), mean_ones[:], evac[:, i % 2, hf * BANK:(hf + 1) * BANK],
                                   start=(i == 0), stop=(i == CT - 1))
                mm.then_inc(ln_sq_used, 1)
            with pe.Fori(2, 4) as i:
                pair(N_GA + 2 * i)
            for n0 in (N_GC, N_V):
                with pe.Fori(0, 4) as i:
                    pair(n0 + 2 * i)

            def qk_sums(k, par):
                pe.wait_ge(psum_freed, N_K - N_U + k + 1)
                for hf in range(2):
                    mm = pe.matmul(bank(4 + hf), block_ones[:], sq[:, par, hf * BANK:(hf + 1) * BANK],
                                   start=True, stop=True)
                mm.then_inc(qk_summed, 1)

            pair(N_K)
            qk_sums(0, 0)
            with pe.Fori(1, CT) as i:
                for s_ in range(2):
                    n = N_K + 2 * i + s_
                    pe.wait_ge(psum_freed, n - N_U - 1)
                    tile(n, s_)
                    pe.wait_ge(qk_root, 2 * i + s_ - 1)
                    qk_sums(2 * i + s_ - 1, (s_ + 1) % 2)
            pe.wait_ge(qk_root, 2 * CT - 1)
            qk_sums(2 * CT - 1, 1)

        @block.scalar
        def _(act):
            act.wait_ge(par_landed, 16 * N_PAR)
            nc.scalar.activation(c_act[:].rearrange("p j v -> p v j"), c_col[:], ACT.Silu).then_inc(c_ready, 1)
            act.preload_act_table(ACT.Sqrt)
            act.wait_ge(eps_ready, 1)

            def norm_tile(i, k, half):
                act.wait_ge(x_landed[k], 16 * (half + 1))
                nc.scalar.activation(x_sq[:], x_tok[:, k, :], ACT.Square, accum_out=ln_x[:, 0, bass.ds(i, 1)]
                                     ).then_inc(x_squared, 1)
                act.wait_ge(x_squared, i + 1)
                nc.scalar.activation(ln_x[:, 1, bass.ds(i, 1)], ln_x[:, 0, bass.ds(i, 1)], ACT.Sqrt, scale=1.0 / D,
                                     bias=eps_col).then_inc(x_root, 1)

            def copy_xT(i, dst, col):
                for b in range(2):
                    act.wait_ge(x_turned, 4 * i + b + 1)
                    nc.scalar.activation(dst[:, 4 * b:4 * b + 4, bass.ds(col, P)],
                                         bank(2 + b).rearrange("p (j c) -> p j c", j=4), ACT.Copy).then_inc(xT_by_act, 1)

            def copy_rows(nb, s_):
                act.wait_ge(ada_used[CH - 1], nb + 1)
                nc.scalar.activation(ada_rows[0:2, bass.ds(nb * BANK, BANK)], bank(s_)[0:2, :], ACT.Copy
                                     ).then_inc(rows_ready, 1)

            with act.Fori(0, TT // 2) as i:
                for k in range(2):
                    norm_tile(2 * i + k, k, i)
                    copy_rows(2 * i + k, k)
                    copy_xT(2 * i + k, xT, (2 * i + k) * P)
            for k in range(2):
                norm_tile(TT + k, k, TT // 2)
                copy_rows(TT + k, k)
                copy_xT(TT + k, xcT, k * P)
            for nb in (10, 11):
                copy_rows(nb, nb % 2)

            def split_w(n, first=False):
                for c in range(CH):
                    act.wait_ge(w_landed[c], 16 * (n + 1))
                    if not first:
                        act.wait_ge(w_used[c], n)
                    nc.scalar.activation(w_hi[:, c], w_raw[:, c], ACT.Copy).then_inc(w_hi_ready[c], 1)

            split_w(0, first=True)
            act.wait_ge(gate_stored, 16)
            for j in range(JT):
                act.wait_ge(hc_mod, j + 1)
                nc.scalar.activation(hc[:, j, 0:TC], xcT[:, j, :], ACT.Copy).then_inc(hc_hi, 1)
            for j in range(JT):
                act.wait_ge(h_mod, j + 1)
                nc.scalar.activation(h_hi[:, j, :], xT[:, j, :], ACT.Copy).then_inc(h_hi_done, 1)

            def ctx_evac(n, s_, freed=True):
                act.wait_ge(tile_done, n + 1)
                if freed:
                    act.wait_ge(ctx_freed, n - 1)
                nc.scalar.activation(evac[:, s_, TC:2 * TC], bank(s_)[:, TC:2 * TC], ACT.Copy).then_inc(ctx_half, 1)

            for n in range(2):
                split_w(n + 1)
                ctx_evac(n, n, freed=False)
            with act.Fori(1, 4) as i:
                for s_ in range(2):
                    split_w(2 * i + s_ + 1)
                    ctx_evac(2 * i + s_, s_)

            def ctx_square(k, par):
                act.wait_ge(ctx_freed, N_KC + k + 1)
                nc.scalar.activation(evac[:, par, 2 * TC:3 * TC], evac[:, par, 0:TC], ACT.Square).then_inc(ctx_squared, 1)

            def ctx_sqrt(k, par):
                act.wait_ge(ctx_summed, k + 1)
                nc.scalar.activation(evac[:, par, 3 * TC:4 * TC], bank(4 + par)[:, 0:TC], ACT.Sqrt,
                                     scale=1.0 / DH, bias=eps_col).then_inc(ctx_root, 1)

            for k in range(2):
                split_w(N_KC + k + 1)
                ctx_evac(N_KC + k, k)
                ctx_square(k, k)
            ctx_sqrt(0, 0)
            with act.Fori(1, 4) as i:
                for s_ in range(2):
                    k = 2 * i + s_
                    split_w(N_KC + k + 1)
                    act.wait_ge(ctx_normed, k - 1)
                    ctx_evac(N_KC + k, s_)
                    ctx_square(k, s_)
                    ctx_sqrt(k - 1, (s_ + 1) % 2)

            def glu_value(n, i, first=False):
                split_w(n + 1)
                act.wait_ge(tile_done, n + 1)
                if not first:
                    act.wait_ge(glu_used, i)
                nc.scalar.activation(evac[:, 0, :], bank(0, 2), ACT.Copy).then_inc(psum_freed, 1)

            def glu_gate(n):
                split_w(n + 1)
                act.wait_ge(tile_done, n + 1)
                nc.scalar.activation(evac[:, 1, :], bank(2, 2), ACT.Sigmoid).then_inc(psum_freed, 1)

            split_w(N_U + 1)
            ctx_sqrt(CT - 1, 1)
            act.wait_ge(ctx_normed, CT)
            act.preload_act_table(ACT.Sigmoid)
            act.wait_ge(tile_done, N_U + 1)
            nc.scalar.activation(evac[:, 0, :], bank(0, 2), ACT.Copy).then_inc(psum_freed, 1)
            glu_gate(N_U + 1)
            with act.Fori(1, CT) as i:
                glu_value(N_U + 2 * i, i)
                glu_gate(N_U + 2 * i + 1)

            def to_stage(n, s_, count, func):
                split_w(n + 1)
                act.wait_ge(tile_done, n + 1)
                act.wait_ge(stored[s_], count)
                nc.scalar.activation(stage[:, s_, :], bank(2 * s_, 2), func).then_inc(psum_freed, 1)

            act.preload_act_table(ACT.Silu)
            for k in range(4):
                to_stage(N_GA + k, k % 2, 16 * (CT + k // 2), ACT.Silu)
            for i in range(CT):
                act.wait_ge(centred, i + 1)
                if i >= 2:
                    act.wait_ge(ln_sq_used, i - 1)
                nc.scalar.activation(evac[:, i % 2, :], conv[:, i, :], ACT.Square).then_inc(ln_squared, 1)
            act.wait_ge(ln_sq_used, CT)
            nc.scalar.activation(evac[:, 0, :], bank(6, 2), ACT.Sqrt, bias=eps_col).then_inc(ln_root, 1)
            act.preload_act_table(ACT.Silu)
            with act.Fori(2, 4) as i:
                for s_ in range(2):
                    to_stage(N_GA + 2 * i + s_, s_, 16 * (CT + i), ACT.Silu)

            act.wait_ge(ln_ready, CT)

            def conv_gate(k, s_):
                split_w(N_GC + k + 1)
                act.wait_ge(gate_used, k + 1)
                par = chan_par[:, bass.ds(k, 1), :].rearrange("p i k -> p (i k)")
                nc.scalar.activation(evac[:, 1, :], conv[:, bass.ds(k, 1), :].rearrange("p i t -> p (i t)"), ACT.Silu,
                                     scale=par[:, CONV_K + 1:CONV_K + 2], bias=par[:, CONV_K + 2:CONV_K + 3]
                                     ).then_inc(conv_used, 1)
                act.wait_ge(tile_done, N_GC + k + 1)
                nc.scalar.activation(evac[:, 0, :], bank(2 * s_, 2), ACT.Silu).then_inc(psum_freed, 1)

            with act.Fori(0, 4) as i:
                for s_ in range(2):
                    conv_gate(2 * i + s_, s_)
            with act.Fori(0, 4) as i:
                for s_ in range(2):
                    to_stage(N_V + 2 * i + s_, s_, 16 * (CT + 8 + i), ACT.Copy)
            act.preload_act_table(ACT.Sqrt)

            def qk_evac(n, k, s_, gain, last=False):
                if not last:
                    split_w(n + 1)
                act.wait_ge(tile_done, n + 1)
                nc.scalar.activation(evac[:, s_, :], bank(2 * s_, 2), ACT.Copy, scale=gain).then_inc(qk_scaled, 1)
                nc.scalar.activation(sq[:, s_, :], bank(2 * s_, 2), ACT.Square).then_inc(psum_freed, 1)

            def qk_sqrt(k):
                act.wait_ge(qk_summed, k + 1)
                nc.scalar.activation(rstd[:], bank(4, 2), ACT.Sqrt, scale=1.0 / DH, bias=eps_col).then_inc(qk_root, 1)

            act.wait_ge(gate_used, CT + 1)
            qk_evac(N_K, 0, 0, k_gain)
            qk_evac(N_K + 1, 1, 1, k_gain)
            qk_sqrt(0)

            def qk_pair(n, k, gain, last=False):
                for s_ in range(2):
                    act.wait_ge(qk_roped, k + s_ - 1)
                    act.wait_ge(qk_summed, k + s_ - 1)
                    qk_evac(n + s_, k + s_, s_, gain, last and s_ == 1)
                    act.wait_ge(qk_done, k + s_ - 1)
                    qk_sqrt(k + s_ - 1)

            with act.Fori(1, 4) as i:
                qk_pair(N_K + 2 * i, 2 * i, k_gain)
            with act.Fori(4, 7) as i:
                qk_pair(N_K + 2 * i, 2 * i, q_gain)
            qk_pair(N_END - 2, 2 * CT - 2, q_gain, last=True)
            act.wait_ge(qk_done, 2 * CT - 1)
            qk_sqrt(2 * CT - 1)

        @block.vector
        def _(dve):
            nc.vector.memset(eps_col, EPS).then_inc(eps_ready, 1)
            nc.vector.memset(mean_ones[:], 1.0 / CONV_W)
            nc.vector.memset(block_ones[0:DH, 0:DH], 1.0)
            nc.vector.memset(block_ones[0:DH, DH:P], 0.0)
            nc.vector.memset(block_ones[DH:P, 0:DH], 0.0)
            nc.vector.memset(block_ones[DH:P, DH:P], 1.0)
            nc.vector.memset(y_pad[:, 0:HALO], 0.0)
            nc.vector.memset(y_pad[:, HALO + T:], 0.0)
            dve.wait_ge(cols_done, 1)
            nc.vector.tensor_copy(chan_par[:].rearrange("p i k -> p (i k)"), bank(6)[:, 0:CT * n_par]).then_inc(par_done, 1)

            def norm_tile(i, k):
                dve.wait_ge(x_root, i + 1)
                nc.vector.reciprocal(ln_x[:, 2, bass.ds(i, 1)], ln_x[:, 1, bass.ds(i, 1)]).then_inc(x_recip, 1)
                dve.wait_ge(x_recip, i + 1)
                nc.vector.tensor_scalar(x_tok[:, k, :], x_tok[:, k, :], ln_x[:, 2, bass.ds(i, 1)], None, ALU.mult
                                        ).then_inc(x_normed, 1)

            def copy_xT(i, dst, col):
                for b in range(2, 4):
                    dve.wait_ge(x_turned, 4 * i + b + 1)
                    nc.vector.tensor_copy(dst[:, 4 * b:4 * b + 4, bass.ds(col, P)],
                                          bank(2 + b).rearrange("p (j c) -> p j c", j=4)).then_inc(xT_by_dve, 1)

            with dve.Fori(0, TT // 2) as i:
                for k in range(2):
                    norm_tile(2 * i + k, k)
                    copy_xT(2 * i + k, xT, (2 * i + k) * P)
            for k in range(2):
                norm_tile(TT + k, k)
                copy_xT(TT + k, xcT, k * P)

            dve.wait_ge(rows_ready, 12)
            nc.vector.tensor_tensor(ada_rows[0:1, 2 * D:], ada_rows[0:1, 2 * D:], b_gate[0:1, :], ALU.add
                                    ).then_inc(mod_step, 1)
            dve.wait_ge(cols_done, 2)
            cols = bank(6)[:, 0:4 * JT].rearrange("p (k j v) -> p k j v", k=2, v=2)
            for v in range(2):
                nc.vector.tensor_tensor(mod[:, 1, :, v], cols[:, 0, :, v], b_col[:, 0, :], ALU.add)
                nc.vector.tensor_tensor(mod[:, 0, :, v], cols[:, 1, :, v], b_col[:, 1, :], ALU.add).then_inc(mod_step, 1)
            dve.wait_ge(mod_step, 3)
            for v in range(2):
                nc.vector.scalar_tensor_tensor(out=mod[:, 0, :, v], in0=mod[:, 0, :, v], scalar=1.0, in1=g_col[:],
                                               op0=ALU.add, op1=ALU.mult).then_inc(mod_ready, 1)
            dve.wait_ge(mod_ready, 2)
            dve.wait_ge(xT_by_act, 2 * X_TILES)
            for j in range(JT):
                nc.vector.tensor_scalar(xcT[:, j, :], xcT[:, j, :], mod[:, 0, j, 1:2], mod[:, 1, j, 1:2], ALU.mult, ALU.add
                                        ).then_inc(hc_mod, 1)
            for j in range(JT):
                dve.wait_ge(hc_hi, j + 1)
                nc.vector.tensor_tensor(hc[:, j, TC:2 * TC], xcT[:, j, :], hc[:, j, 0:TC].bitcast(F32), ALU.subtract
                                        ).then_inc(hc_ready, 1)
            for j in range(JT):
                nc.vector.tensor_scalar(xT[:, j, :], xT[:, j, :], mod[:, 0, j, 0:1], mod[:, 1, j, 0:1], ALU.mult, ALU.add
                                        ).then_inc(h_mod, 1)
                if j >= 1:
                    dve.wait_ge(h_hi_done, j)
                    nc.vector.tensor_tensor(h_lo[:, j - 1, :], xT[:, j - 1, :], h_hi[:, j - 1, :].bitcast(F32), ALU.subtract
                                            ).then_inc(h_ready, 1)
            dve.wait_ge(h_hi_done, JT)
            nc.vector.tensor_tensor(h_lo[:, JT - 1, :], xT[:, JT - 1, :], h_hi[:, JT - 1, :].bitcast(F32), ALU.subtract
                                    ).then_inc(h_ready, 1)

            def ctx_v(n, s_, stores):
                dve.wait_ge(ctx_half, n + 1)
                if stores is not None:
                    dve.wait_ge(stored[s_], stores)
                nc.vector.tensor_tensor(stage[:, s_, 0:TC], bank(s_)[:, 0:TC], evac[:, s_, TC:2 * TC], ALU.add
                                        ).then_inc(ctx_freed, 1)

            for n in range(2):
                ctx_v(n, n, None)
            with dve.Fori(1, 4) as i:
                for s_ in range(2):
                    ctx_v(2 * i + s_, s_, 16 * i)

            def ctx_k_sum(k, s_):
                dve.wait_ge(ctx_half, N_KC + k + 1)
                nc.vector.tensor_tensor(evac[:, s_, 0:TC], bank(s_)[:, 0:TC], evac[:, s_, TC:2 * TC], ALU.add
                                        ).then_inc(ctx_freed, 1)

            def ctx_k_norm(k, s_, stores):
                dve.wait_ge(ctx_root, k + 1)
                nc.vector.reciprocal(evac[:, s_, 3 * TC:4 * TC], evac[:, s_, 3 * TC:4 * TC]).then_inc(ctx_recip, 1)
                dve.wait_ge(ctx_recip, k + 1)
                dve.wait_ge(stored[s_], stores)
                nc.vector.scalar_tensor_tensor(out=stage[:, s_, 0:TC], in0=evac[:, s_, 0:TC], scalar=k_gain,
                                               in1=evac[:, s_, 3 * TC:4 * TC], op0=ALU.mult, op1=ALU.mult
                                               ).then_inc(ctx_normed, 1)

            ctx_k_sum(0, 0)
            ctx_k_sum(1, 1)
            ctx_k_norm(0, 0, 16 * 4)
            with dve.Fori(1, 4) as i:
                ctx_k_sum(2 * i, 0)
                ctx_k_norm(2 * i - 1, 1, 16 * (3 + i))
                ctx_k_sum(2 * i + 1, 1)
                ctx_k_norm(2 * i, 0, 16 * (4 + i))
            ctx_k_norm(CT - 1, 1, 16 * 7)

            y = y_pad[:, HALO:HALO + T]
            acc = conv[:, CT - 1, :]

            def conv_tile(i):
                dve.wait_ge(psum_freed, 2 * i + 2)
                nc.vector.tensor_tensor(y, evac[:, 0, :], evac[:, 1, :], ALU.mult).then_inc(glu_used, 1)
                nc.vector.tensor_copy(tap_w[:], chan_par[:, bass.ds(i, 1), :].rearrange("p i k -> p (i k)")
                                      ).then_inc(taps_ready, 1)
                dve.wait_ge(taps_ready, i + 1)
                dve.wait_ge(glu_used, i + 1)
                nc.vector.tensor_scalar(acc, y_pad[:, 0:T], tap_w[:, 0:1], tap_w[:, CONV_K:CONV_K + 1], ALU.mult, ALU.add
                                        ).then_inc(tap_done, 1)
                for k in range(1, CONV_K):
                    dve.wait_ge(tap_done, i * (CONV_K - 1) + k)
                    last = k == CONV_K - 1
                    out = conv[:, bass.ds(i, 1), :].rearrange("p i t -> p (i t)") if last else acc
                    nc.vector.scalar_tensor_tensor(out=out, in0=y_pad[:, k:k + T], scalar=tap_w[:, k:k + 1], in1=acc,
                                                   op0=ALU.mult, op1=ALU.add).then_inc(conv_done if last else tap_done, 1)
                dve.wait_ge(conv_done, i + 1)

            with dve.Fori(0, CT) as i:
                conv_tile(i)

            dve.wait_ge(mean_done, 1)
            for i in range(CT):
                nc.vector.tensor_tensor(conv[:, i, :], conv[:, i, :], bank(4, 2), ALU.subtract).then_inc(centred, 1)
            dve.wait_ge(ln_root, 1)
            nc.vector.reciprocal(evac[:, 0, :], evac[:, 0, :]).then_inc(ln_recip, 1)
            dve.wait_ge(ln_recip, 1)
            for i in range(CT):
                nc.vector.tensor_tensor(conv[:, i, :], conv[:, i, :], evac[:, 0, :], ALU.mult).then_inc(ln_ready, 1)
            dve.wait_ge(ln_ready, CT)
            dve.sem_inc(gate_used, 1)

            with dve.Fori(0, 4) as i:
                for s_ in range(2):
                    dve.wait_ge(conv_used, 2 * i + s_ + 1)
                    dve.wait_ge(psum_freed, N_GC - N_U + 2 * i + s_ + 1)
                    dve.wait_ge(stored[s_], 16 * (CT + 4 + i))
                    nc.vector.tensor_tensor(stage[:, s_, :], evac[:, 0, :], evac[:, 1, :], ALU.mult
                                            ).then_inc(gate_used, 1)

            swap = [(q + 16) % 32 for q in range(32)]

            def rope(k, s_, first=False):
                dve.wait_ge(qk_scaled, k + 1)
                if not first:
                    dve.wait_ge(qk_roped, k)
                nc.vector.tensor_tensor(roped[:, s_, :], evac[:, s_, :], cos[:], ALU.mult).then_inc(qk_cos, 1)
                nc.vector.stream_shuffle(turned[:], evac[:, s_, :], swap).then_inc(qk_turned, 1)
                dve.wait_ge(qk_turned, 2 * k + 1)
                nc.vector.tensor_tensor(turned[:], turned[:], sin[:], ALU.mult).then_inc(qk_turned, 1)
                dve.wait_ge(qk_turned, 2 * k + 2)
                dve.wait_ge(qk_cos, k + 1)
                nc.vector.tensor_tensor(roped[:, s_, :], roped[:, s_, :], turned[:], ALU.add).then_inc(qk_roped, 1)

            def qk_norm(k, s_, stores):
                dve.wait_ge(qk_root, k + 1)
                nc.vector.reciprocal(rstd[:], rstd[:]).then_inc(qk_recip, 1)
                dve.wait_ge(qk_recip, k + 1)
                dve.wait_ge(stored[s_], stores)
                nc.vector.tensor_tensor(stage[:, s_, :], roped[:, s_, :], rstd[:], ALU.mult).then_inc(qk_done, 1)

            dve.wait_ge(rope_landed, 32)
            rope(0, 0, first=True)
            rope(1, 1)
            qk_norm(0, 0, 16 * (CT + 12))
            with dve.Fori(1, CT) as i:
                dve.wait_ge(qk_done, 2 * i - 1)
                rope(2 * i, 0)
                qk_norm(2 * i - 1, 1, 16 * (CT + 11 + i))
                dve.wait_ge(qk_done, 2 * i)
                rope(2 * i + 1, 1)
                qk_norm(2 * i, 0, 16 * (CT + 12 + i))
            qk_norm(2 * CT - 1, 1, 16 * (CT + 12 + 7))


def attention(nc, t, sem, Region, base, bank, ctx_kv_d, proj_d, o_all, p0_sum):
    r = Region(base)
    q_st = r.take("q_st", 2 * 2 * T, F32R)[:].rearrange("p (b m t) -> p b m t", b=2, m=2)
    k_hi = r.take("k_hi", 2 * 2 * KEYS, F32R)[:].rearrange("p (b m t) -> p b m t", b=2, m=2)
    k_lo = r.take("k_lo", 2 * 2 * KEYS, F32R)[:].rearrange("p (b m t) -> p b m t", b=2, m=2)
    v_hi = r.take("v_hi", 2 * KEYS, F32R)[:].rearrange("p (b t) -> p b t", b=2)
    v_lo = r.take("v_lo", 2 * KEYS, F32R)[:].rearrange("p (b t) -> p b t", b=2)
    q_raw = r.take("q_raw", 2 * T)[:].rearrange("p (m t) -> p m t", m=2)
    k_raw = r.take("k_raw", 2 * KEYS)[:].rearrange("p (m t) -> p m t", m=2)
    v_raw = r.take("v_raw", KEYS)
    prob = r.take("prob", 2 * 2 * KEYS)[:].rearrange("p (b m t) -> p b m t", b=2, m=2)
    diff = r.take("diff", 2 * KEYS)[:].rearrange("p (b t) -> p b t", b=2)
    QG = 2 * P
    dT_hi = r.take("dT_hi", 2 * KT * QG, F32R)[:].rearrange("p (b k q) -> p b k q", b=2, k=KT)
    dT_lo = r.take("dT_lo", 2 * KT * QG, F32R)[:].rearrange("p (b k q) -> p b k q", b=2, k=KT)
    ident = r.take("ident_b", P)
    top = r.take("top", 4)[:].rearrange("p (b m) -> p b m", b=2)
    neg_top = r.take("neg_top", 4)[:].rearrange("p (b m) -> p b m", b=2)
    p1_sum = r.take("p1_sum", 2)
    p1_inv = r.take("p1_inv", 2)
    map1_factor = r.take("map1_factor", 2)
    lam_rows = r.take("lam_rows", 4 * DH)[:].rearrange("p (k d) -> p k d", k=4)
    lam_dots = r.take("lam_dots", 2)
    lam_exp = r.take("lam_exp", 2)
    neg_lam = r.take("neg_lam", 1)
    ones_row = r.take("ones_row", P)
    lam_tmp = r.take("lam_tmp", 2 * DH)[:].rearrange("p (k d) -> p k d", k=2)
    assert r.at <= o_all_start(nc), r.at

    ROUNDS = ((0, 4), (4, 8), (8, 10))
    V_STEPS = (3, 5, 7)
    V_ROUNDS = len(ROUNDS)

    def use6(s_, second):
        return V_ROUNDS + 2 * s_ + second

    def use7(h, st):
        last = isinstance(h, int) and h == HEADS - 1
        return (TT + V_ROUNDS) * h + st + (0 if last else sum(v <= st for v in V_STEPS))

    def use7_v(h, rd):
        return (TT + V_ROUNDS) * h + V_STEPS[rd] + rd

    def ahead(h, st, by):
        return (h, st + by) if st + by < TT else (h + 1, st + by - TT)

    q_landed, k_landed, v_landed, lam_landed = (sem(n) for n in ("q_landed", "k_landed", "v_landed", "lam_landed"))
    id_ready = sem("id_ready")
    ones_ready = sem("ones_ready")
    lam_step = sem("lam_step")
    lam_spread = sem("lam_spread")
    lam_ready = sem("lam_ready")
    k_rounded = sem("k_rounded")
    q_rounded = sem("q_rounded")
    k_split = sem("k_split")
    q_split = sem("q_split")
    v_turned = sem("v_turned")
    scores_done = [sem(f"scores_done{m}") for m in range(2)]
    top_found = [sem(f"top_found{m}") for m in range(2)]
    top_ready = [sem(f"top_ready{m}") for m in range(2)]
    exp_done = [sem(f"exp_done{m}") for m in range(2)]
    inv_ready = sem("inv_ready")
    factor_ready = sem("factor_ready")
    diff_ready = sem("diff_ready")
    turned6, hi6, free6 = sem("turned6"), sem("hi6"), sem("free6")
    turned7, hi7, free7 = sem("turned7"), sem("hi7"), sem("free7")
    pv_done = sem("pv_done")
    o_copied = sem("o_copied")
    v_read = sem("v_read")

    with nc.Block(name="attention") as block:

        @block.sync
        def _(sp):
            for k, name in enumerate(("lam_q1", "lam_k1", "lam_q2", "lam_k2")):
                sp.dma_start(lam_rows[0:1, k, :], t[name]).then_inc(lam_landed, 16)

            def load_head(h, first=False):
                row_k = (N_K - N_GA) * P + h * P
                if not first:
                    sp.wait_ge(k_split, 2 * h)
                for half in range(2):
                    dst = k_raw[half * DH:(half + 1) * DH]
                    sp.dma_start(dst[:, :, 0:TC], ctx_kv_d[bass.ds(N_KC * P + h * P, P), :]
                                 .rearrange("(m p) t -> p m t", m=2)).then_inc(k_landed, 16)
                    sp.dma_start(dst[:, :, TC:], proj_d[bass.ds(row_k, P), :]
                                 .rearrange("(m p) t -> p m t", m=2)).then_inc(k_landed, 16)
                if not first:
                    sp.wait_ge(q_split, 2 * h)
                for half in range(2):
                    sp.dma_start(q_raw[half * DH:(half + 1) * DH], proj_d[bass.ds((N_Q - N_GA) * P + h * P, P), :]
                                 .rearrange("(m p) t -> p m t", m=2)).then_inc(q_landed, 16)
                if not first:
                    sp.wait_ge(v_read, h)
                sp.dma_start(v_raw[:, 0:TC], ctx_kv_d[bass.ds(h * P, P), :]).then_inc(v_landed, 16)
                sp.dma_start(v_raw[:, TC:], proj_d[bass.ds((N_V - N_GA) * P + h * P, P), :]).then_inc(v_landed, 16)

            load_head(0, first=True)
            with sp.Fori(1, HEADS) as h:
                load_head(h)

        @block.tensor
        def _(pe):
            pe.wait_ge(lam_step, 2)
            pe.wait_ge(ones_ready, 1)
            pe.matmul(bank(7)[:, 0:2], ones_row[0:1, :], lam_dots[0:1, :], start=True, stop=True).then_inc(lam_spread, 1)

            def turn_v(h, rd, to, turned):
                k0, k1 = ROUNDS[rd]
                for k in range(k0, k1):
                    mm = pe.transpose(bank(to)[:, (k - k0) * P:(k - k0 + 1) * P], v_raw[:, k * P:(k + 1) * P], ident[:])
                mm.then_inc(turned, 1)

            def scores(h, st, b, m, s_, first=False):
                if st == 0 and m == 0:
                    pe.wait_ge(k_split, 2 * (h + 1))
                    pe.wait_ge(q_split, 2 * (h + 1))
                if not first:
                    pe.wait_ge(exp_done[m], s_)
                q = q_st[:, b, m, st * P:(st + 1) * P]
                for c0 in range(0, KEYS, BANK):
                    c1 = min(c0 + BANK, KEYS)
                    out = bank(3 * m, 3)[:, c0:c1]
                    pe.matmul(out, q, k_hi[:, b, m, c0:c1], start=True, stop=False)
                    mm = pe.matmul(out, q, k_lo[:, b, m, c0:c1], start=False, stop=True)
                mm.then_inc(scores_done[m], 1)

            def turn_diff(h, st, s_, rd):
                if rd == 0:
                    pe.wait_ge(diff_ready, s_ + 1)
                if rd == 1:
                    pe.wait_ge(free7, use7(h, st) + 1)
                    if st % 2 == 0:
                        pe.wait_ge(o_copied, 4 * h + st // 2 + 1)
                else:
                    pe.wait_ge(free6, use6(s_, rd // 2))
                k0, k1 = ROUNDS[rd]
                for k in range(k0, k1):
                    mm = pe.transpose(bank(7 if rd == 1 else 6)[:, (k - k0) * P:(k - k0 + 1) * P],
                                      diff[:, st % 2, k * P:(k + 1) * P], ident[:])
                mm.then_inc(turned7 if rd == 1 else turned6, 1)

            def product_v(h, st, b, s_, k0, k1):
                g = st // 2 % 2
                if k0 == 0:
                    pe.wait_ge(free7, use7(h, st) + 2)
                    pe.wait_ge(free6, use6(s_, 0) + 1)
                for k in range(k0, k1):
                    if k == ROUNDS[2][0]:
                        pe.wait_ge(free6, use6(s_, 1) + 1)
                    vh, vl = v_hi[:, b, k * P:(k + 1) * P], v_lo[:, b, k * P:(k + 1) * P]
                    mm = split_matmuls(pe, bank(7)[:, 0:QG], vh, vl, dT_hi[:, g, k, :], dT_lo[:, g, k, :],
                                       k == 0, k == KT - 1)
                if k1 == KT:
                    mm.then_inc(pv_done, 1)

            pe.wait_ge(id_ready, 2)
            pe.wait_ge(v_landed, 32)
            for rd in range(3):
                if rd:
                    pe.wait_ge(free6, rd)
                turn_v(0, rd, 6, turned6)
            pe.sem_inc(pv_done, 2)
            scores(0, 0, 0, 0, 0, first=True)
            scores(0, 0, 0, 1, 0, first=True)
            scores(0, 1, 0, 0, 1)
            scores(0, 1, 0, 1, 1)
            scores(0, 2, 0, 0, 2)
            turn_diff(0, 0, 0, 0)

            def head(h, b, last=False):
                for st in range(TT):
                    s_ = TT * h + st
                    if st % 2:
                        turn_diff(h, st, s_, 0)
                    if not last and st in V_STEPS:
                        rd = V_STEPS.index(st)
                        if rd == 0:
                            pe.wait_ge(v_landed, 32 * (h + 2))
                        pe.wait_ge(free7, use7_v(h, rd) + 1)
                        turn_v(h + 1, rd, 7, turned7)
                    if not last or st + 2 < TT:
                        h2, st2 = ahead(h, st, 2)
                        scores(h2, st2, b if st + 2 < TT else 1 - b, 1, s_ + 2)
                    turn_diff(h, st, s_, 1)
                    turn_diff(h, st, s_, 2)
                    if not last or st + 3 < TT:
                        h3, st3 = ahead(h, st, 3)
                        scores(h3, st3, b if st + 3 < TT else 1 - b, 0, s_ + 3)
                    if st % 2:
                        product_v(h, st, b, s_, 0, KT // 2)
                        if not last or st + 1 < TT:
                            turn_diff(*ahead(h, st, 1), s_ + 1, 0)
                        product_v(h, st, b, s_, KT // 2, KT)

            head(0, 0)
            with pe.Fori(0, HEADS // 2 - 1) as i:
                head(2 * i + 1, 1)
                head(2 * i + 2, 0)
            head(HEADS - 1, 1, last=True)

        @block.scalar
        def _(act):
            act.sem_inc(o_copied, 1)
            act.preload_act_table(ACT.Exp)
            act.wait_ge(lam_spread, 1)
            nc.scalar.activation(lam_exp[:], bank(7)[:, 0:2], ACT.Exp).then_inc(lam_step, 1)

            def round_k(h, b, m):
                if m == 0:
                    act.wait_ge(k_landed, 64 * (h + 1))
                nc.scalar.activation(k_hi[:, b, m, :], k_raw[:, m, :], ACT.Copy).then_inc(k_rounded, 1)

            def round_q(h, b):
                act.wait_ge(q_landed, 32 * (h + 1))
                nc.scalar.activation(q_st[:, b], q_raw[:], ACT.Copy).then_inc(q_rounded, 1)

            def v_high(rd, b, frm, done):
                k0, k1 = ROUNDS[rd]
                nc.scalar.activation(v_hi[:, b, k0 * P:k1 * P], bank(frm)[:, 0:(k1 - k0) * P], ACT.Copy).then_inc(done, 1)

            def exp(st, m, s_, first=False):
                act.wait_ge(top_ready[m], s_ + 1)
                if not first:
                    act.wait_ge(diff_ready, s_ - 1)
                row_sum = p1_sum[:, st % 2:st % 2 + 1] if m else p0_sum[:, bass.ds(s_, 1)]
                nc.scalar.activation(prob[:, st % 2, m, :], bank(3 * m, 3)[:, 0:KEYS], ACT.Exp, scale=SCALE,
                                     bias=neg_top[:, st % 2, m:m + 1], accum_out=row_sum).then_inc(exp_done[m], 1)

            def diff_high(h, st, s_, rd):
                if rd == 1:
                    act.wait_ge(turned7, use7(h, st) + 1)
                else:
                    act.wait_ge(turned6, use6(s_, rd // 2) + 1)
                if rd == 0 and st % 2 == 0:
                    act.wait_ge(pv_done, 4 * h + st // 2 + 1)
                k0, k1 = ROUNDS[rd]
                nc.scalar.activation(dT_hi[:, st // 2 % 2, k0:k1, (st % 2) * P:(st % 2 + 1) * P],
                                     bank(7 if rd == 1 else 6)[:, 0:(k1 - k0) * P].rearrange("p (k q) -> p k q", q=P),
                                     ACT.Copy).then_inc(hi7 if rd == 1 else hi6, 1)

            def copy_o(h, st):
                act.wait_ge(pv_done, 4 * h + st // 2 + 3)
                nc.scalar.activation(o_all[:, bass.ds(h, 1), (st - 1) * P:(st + 1) * P].rearrange("p h t -> p (h t)"),
                                     bank(7)[:, 0:QG], ACT.Copy).then_inc(o_copied, 1)

            round_k(0, 0, 0)
            round_k(0, 0, 1)
            round_q(0, 0)
            for rd in range(3):
                act.wait_ge(turned6, rd + 1)
                v_high(rd, 0, 6, hi6)
            exp(0, 0, 0, first=True)
            exp(0, 1, 0, first=True)
            exp(1, 0, 1, first=True)

            def head(h, b, first=False, last=False):
                for st in range(TT):
                    s_ = TT * h + st
                    if not last or st + 1 < TT:
                        exp(st + 1, 1, s_ + 1, first=first and st == 0)
                    diff_high(h, st, s_, 0)
                    if not last and st in V_STEPS:
                        rd = V_STEPS.index(st)
                        act.wait_ge(turned7, use7_v(h, rd) + 1)
                        v_high(rd, 1 - b, 7, hi7)
                    if not last or st + 2 < TT:
                        exp(st + 2, 0, s_ + 2)
                    if st % 2 == 0:
                        if st:
                            copy_o(h, st - 1)
                        elif not first:
                            copy_o(h - 1, TT - 1)
                    diff_high(h, st, s_, 1)
                    diff_high(h, st, s_, 2)
                    if not last and st < 2:
                        round_k(h + 1, 1 - b, st)
                    if not last and st == 2:
                        round_q(h + 1, 1 - b)

            head(0, 0, first=True)
            with act.Fori(0, HEADS // 2 - 1) as i:
                head(2 * i + 1, 1)
                head(2 * i + 2, 0)
            head(HEADS - 1, 1, last=True)
            copy_o(HEADS - 1, TT - 1)

        @block.gpsimd
        def _(pool):
            pool.memset(ident[:], 0.0).then_inc(id_ready, 1)
            pool.wait_ge(id_ready, 1)
            pool.affine_select(out=ident[:], in_=ident[:], compare_op=ALU.not_equal, fill=1.0, base=0,
                               pattern=[[-1, P]], channel_multiplier=1).then_inc(id_ready, 1)

            def low_k(h, b, m):
                pool.wait_ge(k_rounded, 2 * h + m + 1)
                pool.tensor_tensor(k_lo[:, b, m, :], k_raw[:, m, :], k_hi[:, b, m, :].bitcast(F32), ALU.subtract
                                   ).then_inc(k_split, 1)

            def low_q(h, b, m):
                pool.wait_ge(q_rounded, h + 1)
                pool.tensor_tensor(q_st[DH:P, b, m, :], q_raw[DH:P, m, :], q_st[DH:P, b, m, :].bitcast(F32), ALU.subtract
                                   ).then_inc(q_split, 1)

            def split_low(h, b):
                for m in range(2):
                    low_k(h, b, m)
                pool.wait_ge(k_split, 2 * (h + 1))
                for m in range(2):
                    low_q(h, b, m)
                pool.wait_ge(q_split, 2 * (h + 1))

            with pool.Fori(0, HEADS // 2) as i:
                for b in range(2):
                    split_low(2 * i + b, b)

        @block.vector
        def _(dve):
            nc.vector.memset(ones_row[0:1, :], 1.0).then_inc(ones_ready, 1)
            dve.sem_inc(free7, 1)
            dve.wait_ge(lam_landed, 64)
            for k in range(2):
                nc.vector.tensor_tensor(lam_tmp[0:1, k, :], lam_rows[0:1, 2 * k, :], lam_rows[0:1, 2 * k + 1, :], ALU.mult
                                        ).then_inc(lam_ready, 1)
            dve.wait_ge(lam_ready, 2)
            for k in range(2):
                nc.vector.tensor_reduce(lam_dots[0:1, k:k + 1], lam_tmp[0:1, k, :], AXX, ALU.add).then_inc(lam_step, 1)
            dve.wait_ge(lam_step, 3)
            nc.vector.scalar_tensor_tensor(out=neg_lam[:], in0=lam_exp[:, 0:1], scalar=LAM_INIT, in1=lam_exp[:, 1:2],
                                           op0=ALU.add, op1=ALU.subtract).then_inc(lam_ready, 1)
            dve.wait_ge(lam_ready, 3)
            nc.vector.tensor_scalar(neg_lam[:], neg_lam[:], -1.0, None, ALU.mult).then_inc(lam_ready, 1)
            dve.wait_ge(lam_ready, 4)

            def v_low(rd, b, frm, done):
                k0, k1 = ROUNDS[rd]
                part = slice(k0 * P, k1 * P)
                nc.vector.tensor_tensor(v_lo[:, b, part], bank(frm)[:, 0:(k1 - k0) * P], v_hi[:, b, part].bitcast(F32),
                                        ALU.subtract).then_inc(done, 1)
                if rd == 2:
                    dve.sem_inc(v_read, 1)

            def find_top(st, m, s_):
                dve.wait_ge(scores_done[m], s_ + 1)
                nc.vector.tensor_reduce(top[:, st % 2, m:m + 1], bank(3 * m, 3)[:, 0:KEYS], AXX, ALU.max
                                        ).then_inc(top_found[m], 1)

            def negate_top(st, m, s_):
                dve.wait_ge(top_found[m], s_ + 1)
                nc.vector.tensor_scalar(neg_top[:, st % 2, m:m + 1], top[:, st % 2, m:m + 1], -SCALE,
                                        0.0 if m else -P0_DOWN * math.log(2.0), ALU.mult, ALU.add
                                        ).then_inc(top_ready[m], 1)

            def invert(st, s_):
                dve.wait_ge(exp_done[1], s_ + 1)
                nc.vector.reciprocal(p1_inv[:, st % 2:st % 2 + 1], p1_sum[:, st % 2:st % 2 + 1]).then_inc(inv_ready, 1)

            def factor(st, s_):
                dve.wait_ge(inv_ready, s_ + 1)
                dve.wait_ge(exp_done[0], s_ + 1)
                nc.vector.scalar_tensor_tensor(out=map1_factor[:, st % 2:st % 2 + 1], in0=p0_sum[:, bass.ds(s_, 1)],
                                               scalar=neg_lam[:], in1=p1_inv[:, st % 2:st % 2 + 1],
                                               op0=ALU.mult, op1=ALU.mult).then_inc(factor_ready, 1)

            def difference(st, s_):
                dve.wait_ge(factor_ready, s_ + 1)
                nc.vector.scalar_tensor_tensor(out=diff[:, st % 2, :], in0=prob[:, st % 2, 1, :],
                                               scalar=map1_factor[:, st % 2:st % 2 + 1], in1=prob[:, st % 2, 0, :],
                                               op0=ALU.mult, op1=ALU.add).then_inc(diff_ready, 1)

            def diff_low(h, st, s_, rd):
                if rd == 1:
                    dve.wait_ge(hi7, use7(h, st) + 1)
                else:
                    dve.wait_ge(hi6, use6(s_, rd // 2) + 1)
                k0, k1 = ROUNDS[rd]
                at = (slice(None), st // 2 % 2, slice(k0, k1), slice((st % 2) * P, (st % 2 + 1) * P))
                nc.vector.tensor_tensor(dT_lo[at], bank(7 if rd == 1 else 6)[:, 0:(k1 - k0) * P]
                                        .rearrange("p (k q) -> p k q", q=P), dT_hi[at].bitcast(F32), ALU.subtract
                                        ).then_inc(free7 if rd == 1 else free6, 1)

            for rd in range(3):
                dve.wait_ge(hi6, rd + 1)
                v_low(rd, 0, 6, free6)
            for m in range(2):
                find_top(0, m, 0)
                negate_top(0, m, 0)
            find_top(1, 0, 1)
            negate_top(1, 0, 1)
            invert(0, 0)
            factor(0, 0)
            difference(0, 0)
            find_top(1, 1, 1)
            negate_top(1, 1, 1)

            def head(h, b, last=False):
                for st in range(TT):
                    s_ = TT * h + st
                    nxt = not last or st + 1 < TT
                    front = not last or st + 2 < TT
                    if front:
                        find_top(st + 2, 0, s_ + 2)
                    if nxt:
                        invert(st + 1, s_ + 1)
                    if front:
                        negate_top(st + 2, 0, s_ + 2)
                    if nxt:
                        factor(st + 1, s_ + 1)
                    diff_low(h, st, s_, 0)
                    if not last and st in V_STEPS:
                        rd = V_STEPS.index(st)
                        dve.wait_ge(hi7, use7_v(h, rd) + 1)
                        v_low(rd, 1 - b, 7, free7)
                    if nxt:
                        difference(st + 1, s_ + 1)
                    if st % 2:
                        diff_low(h, st, s_, 1)
                    if front:
                        find_top(st + 2, 1, s_ + 2)
                        negate_top(st + 2, 1, s_ + 2)
                    if st % 2 == 0:
                        diff_low(h, st, s_, 1)
                    diff_low(h, st, s_, 2)

            head(0, 0)
            with dve.Fori(0, HEADS // 2 - 1) as i:
                head(2 * i + 1, 1)
                head(2 * i + 2, 0)
            head(HEADS - 1, 1, last=True)


def o_all_start(nc):
    return nc.sbuf_usable_end // 32 * 32 - HEADS * T * 4 - HEADS * TT * 4


def output(nc, t, sem, Region, base, bank, proj_d, gate_d, o_all, p0_sum):
    GROUPS = 8
    GT = 4
    RING = 4
    CONV_T = CONV_W // P
    r = Region(base)
    m_hi = r.take("m_hi", JT * T, F32R)[:].rearrange("p (k t) -> p k t", k=JT)
    lo_at = r.at
    m_lo = r.take("m_lo", JT * T, F32R)[:].rearrange("p (k t) -> p k t", k=JT)
    mixed = Region(lo_at).take("mixed", JT * T)[:].rearrange("p (k t) -> p k t", k=JT)
    o_sq = Region(base + CONV_T * T * 4).take("o_sq", HEADS * T)[:].rearrange("p (h t) -> p h t", h=HEADS)
    wo_raw = r.take("wo_raw", RING * BANK)[:].rearrange("p (s n) -> p s n", s=RING)
    wo_hi = r.take("wo_hi", RING * BANK, F32R)[:].rearrange("p (s n) -> p s n", s=RING)
    wo_lo = r.take("wo_lo", RING * BANK, F32R)[:].rearrange("p (s n) -> p s n", s=RING)
    gate = r.take("gate", D)
    xy = r.take("xy", GT * BANK)[:].rearrange("p (s n) -> p s n", s=GT)
    tmp_at = r.at
    tmp = r.take("tmp", 2 * BANK)[:].rearrange("p (s n) -> p s n", s=2)
    diag = Region(tmp_at).take("diag", TT * P)[:].rearrange("p (t q) -> p t q", t=TT)
    ident = r.take("ident_c", P)
    ones = r.take("ones_c", P)
    root = r.take("root", HEADS * TT)
    no_overflow = r.take("no_overflow", HEADS * TT)
    head_gain = r.take("head_gain", 1)
    p0_sq = r.take("p0_sq", HEADS * TT)
    assert r.at <= o_all_start(nc), r.at

    gain_landed = sem("gain_landed")
    gate_landed = sem("gate_landed")
    mix_landed = [sem(f"mix_landed{k}") for k in range(JT // 4)]
    wo_landed = [sem(f"wo_landed{k}") for k in range(RING)]
    wo_hi_ready = [sem(f"wo_hi_ready{k}") for k in range(RING)]
    wo_lo_ready = [sem(f"wo_lo_ready{k}") for k in range(RING)]
    wo_used = [sem(f"wo_used{k}") for k in range(RING)]
    id2_ready = sem("id2_ready")
    const_ready = sem("const_ready")
    o_squared = sem("o_squared")
    o_bounded = sem("o_bounded")
    o_summed = sem("o_summed")
    o_root = sem("o_root")
    o_recip = sem("o_recip")
    diag_ready = sem("diag_ready")
    spread = sem("spread")
    o_normed = sem("o_normed")
    mix_gated = sem("mix_gated")
    mix_rounded = sem("mix_rounded")
    mix_ready = sem("mix_ready")
    sum_done = sem("sum_done")
    sum_freed = sem("sum_freed")
    y_done = sem("y_done")
    xo_landed = sem("xo_landed")
    out_stored = sem("out_stored")

    x_v = t["x"].rearrange("b (g s p) d -> p (b g) s d", p=P, s=GT)
    out_v = t["out"].rearrange("b (g s p) d -> p (b g) s d", p=P, s=GT)

    def w_row(k):
        return (ATT_W + k * P, (N_GC - N_GA + k) * P) if k < CONV_T else ((k - CONV_T) * P, (k - CONV_T) * P)

    with nc.Block(name="output") as block:

        @block.sync
        def _(sp):
            def columns(cb):
                return bass.ds((cb + 1) * BANK - BANK, BANK)

            def load_w(n4, k, cb, first=False):
                if not first:
                    sp.wait_ge(wo_lo_ready[k % RING], n4)
                row = w_row(k)[0]
                sp.dma_start(wo_raw[:, k % RING, :], t["w_out"][0, row:row + P, columns(cb)]
                             ).then_inc(wo_landed[k % RING], 16)

            def group(g, half, cb, first=False):
                uses = [4 * g + q for q in range(JT // RING)]
                if not isinstance(g, int):
                    uses = [sp.snap(u) for u in uses]
                for k in range(JT):
                    load_w(uses[k // RING], k, cb, first and k < RING)
                    if first and 0 <= k - RING + 1 < 4:
                        for kk in range(4 * (k - RING + 1), 4 * (k - RING + 2)):
                            row = w_row(kk)[1]
                            sp.dma_start(mixed[:, kk, :], proj_d[row:row + P, :]).then_inc(mix_landed[kk // 4], 16)
                    if k == 4 and not first:
                        sp.wait_ge(y_done, 4 * g)
                        last_cb = cb if half else cb - 1
                        sp.dma_start(out_v[:, 1 - half, :, columns(last_cb)], xy[:]).then_inc(out_stored, 16)
                    if k == 8:
                        if first:
                            sp.dma_start(gate[:], gate_d.to_broadcast([P, D])).then_inc(gate_landed, 16)
                        else:
                            sp.wait_ge(out_stored, 16 * g)
                        sp.dma_start(xy[:], x_v[:, half, :, columns(cb)]).then_inc(xo_landed, 16)

            sp.dma_start(head_gain[:], t["sub_norm_g"].rearrange("l d -> d l")).then_inc(gain_landed, 16)
            group(0, 0, 0, first=True)
            group(1, 1, 0)
            with sp.Fori(1, GROUPS // 2) as cb:
                for half in range(2):
                    group(2 * cb + half, half, cb)
            sp.wait_ge(y_done, GT * GROUPS)
            sp.dma_start(out_v[:, 1, :, D - BANK:D], xy[:]).then_inc(out_stored, 16)
            sp.wait_ge(out_stored, 16 * GROUPS)

        @block.gpsimd
        def _(pool):
            pool.memset(ident[:], 0.0).then_inc(id2_ready, 1)
            pool.wait_ge(id2_ready, 1)
            pool.affine_select(out=ident[:], in_=ident[:], compare_op=ALU.not_equal, fill=1.0, base=0,
                               pattern=[[-1, P]], channel_multiplier=1).then_inc(id2_ready, 1)
            with pool.Fori(0, GROUPS * JT // RING) as n:
                for s_ in range(RING):
                    pool.wait_ge(wo_hi_ready[s_], n + 1)
                    pool.tensor_tensor(wo_lo[:, s_, :], wo_raw[:, s_, :], wo_hi[:, s_, :].bitcast(F32), ALU.subtract
                                       ).then_inc(wo_lo_ready[s_], 1)

        @block.tensor
        def _(pe):
            pe.wait_ge(const_ready, 1)
            for h in range(HEADS):
                pe.wait_ge(o_squared, h + 1)
                for tt in range(TT):
                    mm = pe.matmul(bank(4)[:, h * TT + tt:h * TT + tt + 1], o_sq[:, h, tt * P:(tt + 1) * P], ones[:, 0:1],
                                   start=True, stop=True, skip_group_check=True)
            mm.then_inc(o_summed, 1)

            def spread_norm(h):
                pe.wait_ge(diag_ready, h + 1)
                if h >= 2:
                    pe.wait_ge(o_normed, h - 1)
                for tt in range(TT):
                    b = 4 + 2 * (h % 2) + tt // 4
                    mm = pe.matmul(bank(b)[:, (tt % 4) * P:(tt % 4 + 1) * P], ones[:], diag[:, tt, :],
                                   start=True, stop=True, skip_group_check=True)
                mm.then_inc(spread, 1)

            def group(g, half, first=False):
                for k in range(JT):
                    if first and k >= CONV_T:
                        if k == CONV_T:
                            spread_norm(0)
                        if k + 1 < JT:
                            spread_norm(k + 1 - CONV_T)
                    if first:
                        pe.wait_ge(mix_ready, k + 1)
                    n = 4 * g + k // RING + 1
                    s_ = k % RING
                    pe.wait_ge(wo_hi_ready[s_], n)
                    pe.wait_ge(wo_lo_ready[s_], n)
                    for q in range(GT):
                        if k == 0 and not first:
                            if isinstance(g, int):
                                pass
                            else:
                                pe.wait_ge(sum_freed, 4 * g - 8 + q + 1)
                        tok = slice((half * GT + q) * P, (half * GT + q + 1) * P)
                        mm = split_matmuls(pe, bank(half * GT + q), m_hi[:, k, tok], m_lo[:, k, tok],
                                           wo_hi[:, s_, :], wo_lo[:, s_, :], k == 0, k == JT - 1)
                        if k == JT - 1:
                            mm.then_inc(sum_done, 1)
                    if k < JT - 1:
                        mm.then_inc(wo_used[s_], 1)
                    else:
                        pe.wait_ge(sum_done, 4 * g + GT)
                        pe.sem_inc(wo_used[s_], 1)

            group(0, 0, first=True)
            pe.wait_ge(o_normed, HEADS)
            group(1, 1)
            with pe.Fori(1, GROUPS // 2) as cb:
                for half in range(2):
                    group(2 * cb + half, half)

        @block.scalar
        def _(act):
            for h in range(HEADS):
                act.wait_ge(o_bounded, h + 1)
                nc.scalar.activation(o_sq[:, h, :], o_sq[:, h, :], ACT.Square, scale=O_DOWN).then_inc(o_squared, 1)

            def round_w(g, k, first=False):
                s_ = k % RING
                n = 4 * g + k // RING
                act.wait_ge(wo_landed[s_], 16 * (n + 1))
                if not (first and k < RING):
                    act.wait_ge(wo_used[s_], n)
                nc.scalar.activation(wo_hi[:, s_, :], wo_raw[:, s_, :], ACT.Copy).then_inc(wo_hi_ready[s_], 1)

            def round_mix(k):
                nc.scalar.activation(m_hi[:, k, :], mixed[:, k, :], ACT.Copy).then_inc(mix_rounded, 1)

            for k in range(CONV_T):
                if k == RING:
                    act.wait_ge(o_recip, 3)
                    nc.scalar.activation(root[:], root[:], ACT.Sqrt, scale=1.0 / P).then_inc(o_root, 1)
                round_w(0, k, first=True)
                act.wait_ge(mix_landed[k // 4], 16 * 4)
                round_mix(k)
            for k in range(CONV_T, JT):
                round_w(0, k, first=True)
                act.wait_ge(mix_gated, k - CONV_T + 1)
                round_mix(k)
            for k in range(JT):
                round_w(1, k)
            with act.Fori(1, GROUPS // 2) as cb:
                for half in range(2):
                    for k in range(JT):
                        round_w(2 * cb + half, k)

        @block.vector
        def _(dve):
            nc.vector.memset(ones[:], 1.0).then_inc(const_ready, 1)
            nc.vector.tensor_tensor(p0_sq[:], p0_sum[:], p0_sum[:], ALU.mult).then_inc(const_ready, 1)
            for h in range(HEADS):
                nc.vector.tensor_scalar(o_sq[:, h, :], o_all[:, h, :], O_BOUND, -O_BOUND, ALU.min, ALU.max
                                        ).then_inc(o_bounded, 1)

            def low_mix(k):
                dve.wait_ge(mix_rounded, k + 1)
                nc.vector.tensor_tensor(m_lo[:, k, :], mixed[:, k, :], m_hi[:, k, :].bitcast(F32), ALU.subtract
                                        ).then_inc(mix_ready, 1)

            for k in range(RING):
                low_mix(k)
            dve.wait_ge(gain_landed, 16)
            nc.vector.tensor_scalar(head_gain[:], head_gain[:], (1.0 - LAM_INIT) * O_DOWN, None, ALU.mult
                                    ).then_inc(o_recip, 1)
            dve.wait_ge(const_ready, 2)
            dve.wait_ge(o_summed, 1)
            nc.vector.scalar_tensor_tensor(out=no_overflow[:], in0=p0_sq[:], scalar=SQ_OVERFLOW,
                                           in1=bank(4)[:, 0:HEADS * TT], op0=ALU.mult, op1=ALU.is_gt).then_inc(o_recip, 1)
            nc.vector.scalar_tensor_tensor(out=root[:], in0=p0_sq[:], scalar=P * EPS * O_DOWN ** 2,
                                           in1=bank(4)[:, 0:HEADS * TT], op0=ALU.mult, op1=ALU.add).then_inc(o_recip, 1)
            dve.wait_ge(o_root, 1)
            nc.vector.reciprocal(root[:], root[:]).then_inc(o_recip, 1)
            dve.wait_ge(o_recip, 4)
            nc.vector.tensor_tensor(root[:], root[:], no_overflow[:], ALU.mult).then_inc(o_recip, 1)
            dve.wait_ge(o_recip, 5)
            dve.wait_ge(id2_ready, 2)

            def spread_diag(h):
                if h >= 1:
                    dve.wait_ge(spread, h)
                nc.vector.tensor_tensor(diag[:], ident[:].unsqueeze(1).to_broadcast([P, TT, P]),
                                        root[:, h * TT:(h + 1) * TT].unsqueeze(2).to_broadcast([P, TT, P]), ALU.mult
                                        ).then_inc(diag_ready, 1)

            spread_diag(0)
            for k in range(RING, CONV_T):
                low_mix(k)
            for h in range(HEADS):
                if h + 1 < HEADS:
                    spread_diag(h + 1)
                k = CONV_T + h
                dve.wait_ge(spread, h + 1)
                nc.vector.scalar_tensor_tensor(out=o_all[:, h, :], in0=o_all[:, h, :], scalar=head_gain[:],
                                               in1=bank(4 + 2 * (h % 2), 2), op0=ALU.mult, op1=ALU.mult
                                               ).then_inc(o_normed, 1)
                dve.wait_ge(o_normed, h + 1)
                dve.wait_ge(mix_landed[k // 4], 16 * 4)
                nc.vector.tensor_tensor(mixed[:, k, :], mixed[:, k, :], o_all[:, h, :], ALU.mult).then_inc(mix_gated, 1)
                low_mix(k)

            def result(g, half, cb):
                for q in range(GT):
                    dve.wait_ge(sum_done, 4 * g + q + 1)
                    if q == 0:
                        dve.wait_ge(xo_landed, 16 * (g + 1))
                    nc.vector.tensor_tensor(tmp[:, q % 2, :], bank(half * GT + q), gate[:, bass.ds(cb * BANK, BANK)], ALU.mult
                                            ).then_inc(sum_freed, 1)
                    dve.wait_ge(sum_freed, 4 * g + q + 1)
                    nc.vector.tensor_tensor(xy[:, q, :], xy[:, q, :], tmp[:, q % 2, :], ALU.add).then_inc(y_done, 1)

            dve.wait_ge(gate_landed, 16)
            with dve.Fori(0, GROUPS // 2) as cb:
                for half in range(2):
                    result(2 * cb + half, half, cb)


_INS = ["x", "c", "ctx", "c_ctx", "w_ada", "b_ada", "norm_g", "w_in", "q_norm_g", "k_norm_g", "lam_q1", "lam_k1",
        "lam_q2", "lam_k2", "sub_norm_g", "conv_w", "conv_b", "conv_ln_g", "conv_ln_b", "w_out"]


def kernel(**inputs):
    import concourse.bacc as _bacc
    from concourse.bass_utils import run_bass_kernel_spmd as _run

    nc = _bacc.Bacc("TRN2", target_bir_lowering=False, num_devices=1)
    cos, sin = rope_tables()
    arrays, tensors = {}, {}
    for name in _INS + ["rope_cos", "rope_sin"]:
        a = {"rope_cos": cos, "rope_sin": sin}.get(name)
        if a is None:
            a = np.ascontiguousarray(inputs[name])
        arrays[f"in_{name}_dram"] = a
        tensors[name] = nc.dram_tensor(f"in_{name}_dram", a.shape, mybir.dt.from_np(a.dtype), kind="ExternalInput").ap()
    tensors["out"] = nc.dram_tensor("out_0_dram", (1, T, D), F32, kind="ExternalOutput").ap()
    with nc.allow_non_contiguous_dma(reason="gains of 64 or 128 channels, one per partition"):
        build(nc, tensors)
    r = _run(nc, [arrays], core_ids=[0])
    return r.results[0]["out_0_dram"]
```

```python
from contextlib import ExitStack
import math

import numpy as np

import concourse.bass as bass
from concourse import mybir

F32 = mybir.dt.float32
F32R = mybir.dt.float32r
ALU = mybir.AluOpType
ACT = mybir.ActivationFunctionType
AXX = mybir.AxisListType.X

P = 128
D = 2048
JT = D // P
T = 1024
TC = 256
TT = T // P
HEADS = 8
DH = 64
ATT_W = 1024
CONV_W = 1024
CONV_K = 31
HALO = CONV_K // 2
GRID_W = 64
ROPE_BASE = 10000.0
EPS = 1e-6
Q0, K0, V0, GA0, U0 = 0, 1024, 2048, 3072, 4096
GC0 = U0 + 2 * CONV_W
CT = 8
CH = 4
JC = JT // CH
KEYS = TC + T
KT = KEYS // P
SCALE = 1.0 / math.sqrt(DH)
LAM_INIT = 0.8 - 0.6 * math.exp(-0.3 * 0)
BANK = 512
P0_DOWN = 11
O_BOUND = 2.0 ** 65
O_DOWN = 2.0 ** -20
SQ_OVERFLOW = 2.0 ** 128 * O_DOWN ** 2

N_VC, N_KC, N_U, N_GA, N_GC, N_K, N_Q, N_V, N_END = 0, 8, 16, 32, 40, 48, 56, 64, 72


ROTARY_AT = (2 * JT * T + 3 * JT * P) * 4


def rope_tables():
    tok = np.arange(T)
    nf = DH // 4
    inv = ROPE_BASE ** (-np.arange(nf, dtype=np.float32) / np.float32(nf))
    row = (tok // GRID_W).astype(np.float32)[:, None] * inv.astype(np.float32)
    col = (tok % GRID_W).astype(np.float32)[:, None] * inv.astype(np.float32)
    ang = np.concatenate([row, row, col, col], axis=-1).astype(np.float32)
    sign = np.concatenate([-np.ones(nf), np.ones(nf)] * 2).astype(np.float32)
    cos = np.cos(ang).T
    sin = (np.sin(ang) * sign).T
    return (np.ascontiguousarray(np.concatenate([cos, cos]).astype(np.float32)),
            np.ascontiguousarray(np.concatenate([sin, sin]).astype(np.float32)))


class RawHead:
    pass


def split_matmuls(pe, out, w_hi, w_lo, x_hi, x_lo, start, stop):
    pe.matmul(out, w_hi, x_hi, start=start, stop=False)
    pe.matmul(out, w_hi, x_lo, start=False, stop=False)
    return pe.matmul(out, w_lo, x_hi, start=False, stop=stop)


def build(nc, t):
    with ExitStack() as ctx:
        sem_names = []

        def sem(name):
            sem_names.append(name)
            return ctx.enter_context(nc.semaphore(name))

        base = (nc.sbuf_base + 31) // 32 * 32
        limit = nc.sbuf_usable_end // 32 * 32

        class Region:
            def __init__(self, start):
                self.at = start

            def take(self, name, cols, dtype=F32):
                h = nc.alloc_sbuf_tensor_at(name, [P, cols], dtype, offset=self.at)
                self.at += (cols * 4 + 31) // 32 * 32
                assert self.at <= limit, (name, self.at, limit)
                return h

        o_all = Region(limit - HEADS * T * 4).take("o_all", HEADS * T)[:].rearrange("p (h t) -> p h t", h=HEADS)

        p0_sum = Region(o_all_start(nc)).take("p0_sum", HEADS * TT)

        psum = ctx.enter_context(nc.psum_tensor("psum", [P, 8 * BANK], F32))

        def bank(b, n=1):
            return psum[:, b * BANK:(b + n) * BANK]

        ctx_kv_d = nc.dram_tensor("ctx_kv", [(N_U - N_VC) * P, TC], F32, kind="Internal").ap()
        proj_d = nc.dram_tensor("proj", [(N_END - N_GA) * P, T], F32, kind="Internal").ap()
        gate_d = nc.dram_tensor("gate_row", [1, D], F32, kind="Internal").ap()

        r = Region(base + ROTARY_AT)
        raw = RawHead()
        raw.k = r.take("k_raw", 2 * KEYS)[:].rearrange("p (m t) -> p m t", m=2)
        raw.q = r.take("q_raw", 2 * T)[:].rearrange("p (m t) -> p m t", m=2)
        raw.end = r.at
        raw.k_landed, raw.q_landed = sem("k_landed"), sem("q_landed")

        def load_k(sp, h):
            for half in range(2):
                dst = raw.k[half * DH:(half + 1) * DH]
                sp.dma_start(dst[:, :, 0:TC], ctx_kv_d[bass.ds(N_KC * P + h * P, P), :]
                             .rearrange("(m p) t -> p m t", m=2)).then_inc(raw.k_landed, 16)
                sp.dma_start(dst[:, :, TC:], proj_d[bass.ds((N_K - N_GA) * P + h * P, P), :]
                             .rearrange("(m p) t -> p m t", m=2)).then_inc(raw.k_landed, 16)

        def load_q(sp, h):
            for half in range(2):
                sp.dma_start(raw.q[half * DH:(half + 1) * DH], proj_d[bass.ds((N_Q - N_GA) * P + h * P, P), :]
                             .rearrange("(m p) t -> p m t", m=2)).then_inc(raw.q_landed, 16)

        projections(nc, t, sem, Region, base, bank, ctx_kv_d, proj_d, gate_d, load_k, load_q)
        attention(nc, t, sem, Region, base, bank, ctx_kv_d, proj_d, o_all, p0_sum, raw, load_k, load_q)
        output(nc, t, sem, Region, base, bank, proj_d, gate_d, o_all, p0_sum)


def projections(nc, t, sem, Region, base, bank, ctx_kv_d, proj_d, gate_d, load_k, load_q):
    r = Region(base)
    h_hi = r.take("h_hi", JT * T, F32R)[:].rearrange("p (j t) -> p j t", j=JT)
    lo_at = r.at
    h_lo = r.take("h_lo", JT * T, F32R)[:].rearrange("p (j t) -> p j t", j=JT)
    w_raw = r.take("w_raw", JT * P)[:].rearrange("p (c j n) -> p c j n", c=CH, n=P)
    w_hi = r.take("w_hi", JT * P, F32R)[:].rearrange("p (c j n) -> p c j n", c=CH, n=P)
    w_lo = r.take("w_lo", JT * P, F32R)[:].rearrange("p (c j n) -> p c j n", c=CH, n=P)
    shared_at = r.at
    assert shared_at == base + ROTARY_AT
    hc = r.take("hc", JT * 2 * TC, F32R)[:].rearrange("p (j t) -> p j t", j=JT)
    late_at = r.at
    stage = r.take("stage", 2 * T)[:].rearrange("p (s t) -> p s t", s=2)
    evac = r.take("evac", 2 * T)[:].rearrange("p (s t) -> p s t", s=2)
    y_pad = r.take("y_pad", T + 2 * HALO + 2)
    n_par = CONV_K + 3
    chan_par = r.take("chan_par", CT * n_par)[:].rearrange("p (i k) -> p i k", i=CT)
    tap_w = r.take("tap_w", n_par)
    block_ones = r.take("block_ones", P)
    mean_ones = r.take("mean_ones", P)
    eps_col, q_gain, k_gain = (r.take(name, 1)[:] for name in ("eps_col", "q_gain", "k_gain"))
    mod = r.take("mod", 4 * JT)[:].rearrange("p (k j v) -> p k j v", k=2, v=2)

    c_act = r.take("c_act", 2 * JT)[:].rearrange("p (j v) -> p j v", v=2)

    GATE_RING = 3
    gate_w = Region(base + 2 * JT * T * 4).take("gate_w", GATE_RING * JC * BANK)[:].rearrange(
        "p (s j n) -> p s j n", s=GATE_RING, n=BANK)
    gate_row = stage.rearrange("p s t -> p (s t)")
    xT = Region(lo_at).take("xT", JT * T)[:].rearrange("p (j t) -> p j t", j=JT)
    s = Region(base)
    ada_w = s.take("ada_w", CH * JC * BANK)[:].rearrange("p (c j n) -> p c j n", c=CH, n=BANK)
    ada_lo = Region(base).take("ada_lo", CH * JC * BANK, F32R)[:].rearrange("p (c j n) -> p c j n", c=CH, n=BANK)
    x_tok = s.take("x_tok", 2 * D)[:].rearrange("p (s d) -> p s d", s=2)
    x_sq = s.take("x_sq", D)
    chan_rows = s.take("chan_rows", CONV_W)
    ident = s.take("ident", P)
    c_col = s.take("c_col", 2 * JT)[:].rearrange("p (v j) -> p v j", v=2)
    c_split = s.take("c_split", 4 * JT, F32R)[:].rearrange("p (j v) -> p j v", v=4)
    pair_sum = s.take("pair_sum", 2)
    ln_x = s.take("ln_x", 3 * (TT + 2))[:].rearrange("p (k t) -> p k t", k=3)
    g_col = s.take("g_col", JT)
    b_col = s.take("b_col", 2 * JT)[:].rearrange("p (k j) -> p k j", k=2)
    assert s.at <= lo_at
    s = Region(shared_at)
    ada_rows = s.take("ada_rows", 2 * D)
    ada_hi = s.take("ada_hi", 2 * JC * BANK, F32R)[:].rearrange("p (s j n) -> p s j n", s=2, n=BANK)
    s = Region(late_at)
    xcT = s.take("xcT", JT * TC)[:].rearrange("p (j t) -> p j t", j=JT)
    conv = Region(shared_at).take("conv", CT * T)[:].rearrange("p (i t) -> p i t", i=CT)
    s = Region(shared_at)
    cos = s.take("cos", T)
    sin = s.take("sin", T)
    sq = s.take("sq", 2 * T)[:].rearrange("p (s t) -> p s t", s=2)
    roped = s.take("roped", 2 * T)[:].rearrange("p (s t) -> p s t", s=2)
    turned = s.take("turned", T)
    rstd = s.take("rstd", T)

    ada_v = t["w_ada"].rearrange("l (p j) n -> p (l j) n", p=P)
    w_v = t["w_in"].rearrange("l (p j) n -> p (l j) n", p=P)

    par_landed = sem("par_landed")
    ada_landed = [sem(f"ada_landed{c}") for c in range(CH)]
    ada_used = [sem(f"ada_used{c}") for c in range(CH)]
    ada_hi_ready = sem("ada_hi_ready")
    ada_lo_ready = sem("ada_lo_ready")
    ident_ready = sem("ident_ready")
    c_ready = sem("c_ready")
    rows_ready = sem("rows_ready")
    cols_done = sem("cols_done")
    mod_ready = sem("mod_ready")
    x_landed = [sem(f"x_landed{p}") for p in range(2)]
    x_squared = sem("x_squared")
    x_root = sem("x_root")
    recip_done = sem("recip_done")
    x_normed = sem("x_normed")
    x_turned = sem("x_turned")
    xT_by_act = sem("xT_by_act")
    xT_by_dve = sem("xT_by_dve")
    modulated = sem("modulated")
    rounded = sem("rounded")
    hc_ready = sem("hc_ready")
    h_ready = sem("h_ready")
    par_done = sem("par_done")
    mod_step = sem("mod_step")
    gate_row_ready = sem("gate_row_ready")
    gate_stored = sem("gate_stored")
    w_landed = [sem(f"w_landed{c}") for c in range(CH)]
    w_hi_ready = [sem(f"w_hi_ready{c}") for c in range(CH)]
    w_lo_ready = [sem(f"w_lo_ready{c}") for c in range(CH)]
    w_used = [sem(f"w_used{c}") for c in range(CH)]
    tile_done = w_used[CH - 1]
    ctx_half = sem("ctx_half")
    ctx_freed = sem("ctx_freed")
    psum_freed = sem("psum_freed")
    ctx_squared = sem("ctx_squared")
    ctx_summed = sem("ctx_summed")
    ctx_root = sem("ctx_root")
    ctx_normed = sem("ctx_normed")
    stored = [sem(f"stored{p}") for p in range(2)]
    glu_in = sem("glu_in")
    glu_used = sem("glu_used")
    conv_done = sem("conv_done")
    mean_done = sem("mean_done")
    centred = sem("centred")
    ln_squared = sem("ln_squared")
    ln_sq_used = sem("ln_sq_used")
    ln_root = sem("ln_root")
    ln_ready = sem("ln_ready")
    taps_ready = sem("taps_ready")
    tap_done = sem("tap_done")
    gate_used = sem("gate_used")
    eps_ready = sem("eps_ready")
    rope_landed = sem("rope_landed")
    conv_used = sem("conv_used")
    qk_scaled = sem("qk_scaled")
    qk_cos = sem("qk_cos")
    qk_turned = sem("qk_turned")
    qk_roped = sem("qk_roped")
    qk_summed = sem("qk_summed")
    qk_root = sem("qk_root")
    qk_done = sem("qk_done")

    N_PAR = 11
    MOD_BLOCKS = 2 * D // BANK
    ADA_BLOCKS = 3 * D // BANK
    GATE_BANKS = (7, 2, 3, 4)

    gate_chunks = [(m, MOD_BLOCKS + m // CH, m % CH, (m + 2) % GATE_RING) for m in range((ADA_BLOCKS - MOD_BLOCKS) * CH)]
    X_TILES = TT + 2

    with nc.Block(name="projections") as block:

        @block.sync
        def _(sp):
            sp.dma_start(c_col[:, 0, :], t["c"].rearrange("l (p j) -> (l p) j", p=P)).then_inc(c_ready, 16)
            sp.dma_start(c_col[:, 1, :], t["c_ctx"].rearrange("(p j) -> p j", p=P)).then_inc(c_ready, 16)

            def load_ada(nb, first=False):
                for c in range(CH):
                    if not first:
                        sp.wait_ge(ada_used[c], nb)
                    sp.dma_start(ada_w[:, c], ada_v[:, c * JC:(c + 1) * JC, bass.ds(nb * BANK, BANK)]
                                 ).then_inc(ada_landed[c], 16)

            load_ada(0, first=True)
            sp.dma_start(g_col[:], t["norm_g"].rearrange("l (p j) -> (l p) j", p=P)).then_inc(par_landed, 16)
            for k in range(2):
                sp.dma_start(b_col[:, k, :], t["b_ada"][:, k * D:(k + 1) * D].rearrange("l (p j) -> (l p) j", p=P)
                             ).then_inc(par_landed, 16)
            sp.dma_start(chan_rows[0:CONV_K, :], t["conv_w"].rearrange("l k n -> (l k) n")).then_inc(par_landed, 16)
            for k, name in enumerate(("conv_b", "conv_ln_g", "conv_ln_b")):
                sp.dma_start(chan_rows[CONV_K + k:CONV_K + k + 1, :], t[name]).then_inc(par_landed, 16)
            for m in range(2):
                sp.dma_start(q_gain[m * DH:(m + 1) * DH, :], t["q_norm_g"].rearrange("l d -> d l")).then_inc(par_landed, 16)
                sp.dma_start(k_gain[m * DH:(m + 1) * DH, :], t["k_norm_g"].rearrange("l d -> d l")).then_inc(par_landed, 16)

            with sp.Fori(1, MOD_BLOCKS) as nb:
                load_ada(nb)

            def load_w(n, col, first=False):
                for c in range(CH):
                    if not first:
                        sp.wait_ge(w_lo_ready[c], n)
                    sp.dma_start(w_raw[:, c], w_v[:, c * JC:(c + 1) * JC, bass.ds(col, P)]
                                 ).then_inc(w_landed[c], 16)

            def store_ctx(n, par, ready, count):
                sp.wait_ge(ready, count)
                sp.dma_start(ctx_kv_d[bass.ds(n * P, P), :], stage[:, par, 0:TC]).then_inc(stored[par], 16)

            def store(n, par):
                sp.dma_start(proj_d[bass.ds((n - N_GA) * P, P), :], stage[:, par, :]).then_inc(stored[par], 16)

            def store_after_act(n, par):
                sp.wait_ge(psum_freed, n - N_U + 1)
                store(n, par)

            def store_gc(n, par):
                sp.wait_ge(gate_used, n - N_GC + 2)
                store(n, par)

            def store_qk(n, par):
                sp.wait_ge(qk_done, n - N_K + 1)
                store(n, par)

            for m, nb, c, slot in gate_chunks:
                if m < GATE_RING:
                    sp.wait_ge(ada_used[c], nb)
                else:
                    _, nb0, c0, _ = gate_chunks[m - GATE_RING]
                    sp.wait_ge(ada_used[c0], nb0 + 1)
                sp.dma_start(gate_w[:, slot], ada_v[:, c * JC:(c + 1) * JC, nb * BANK:(nb + 1) * BANK]
                             ).then_inc(ada_landed[c], 16)
            _, nb0, c0, _ = gate_chunks[-GATE_RING]
            sp.wait_ge(ada_used[c0], nb0 + 1)
            load_w(0, V0, first=True)
            sp.wait_ge(gate_row_ready, ADA_BLOCKS - MOD_BLOCKS)
            sp.dma_start(gate_d, gate_row[0:1, :]).then_inc(gate_stored, 16)

            load_w(1, V0 + P)
            with sp.Fori(1, 4) as i:
                for s_ in range(2):
                    load_w(2 * i + s_, V0 + (2 * i + s_) * P)
                    store_ctx(2 * i + s_ - 2, s_, ctx_freed, 2 * i + s_ - 1)
            for s_ in range(2):
                load_w(N_KC + s_, K0 + s_ * P)
                store_ctx(N_KC + s_ - 2, s_, ctx_freed, N_KC + s_ - 1)
            load_w(N_KC + 2, K0 + 2 * P)
            load_w(N_KC + 3, K0 + 3 * P)
            store_ctx(N_KC, 0, ctx_normed, 1)
            with sp.Fori(2, 4) as i:
                for s_ in range(2):
                    load_w(N_KC + 2 * i + s_, K0 + (2 * i + s_) * P)
                    store_ctx(N_KC + 2 * i + s_ - 3, 1 - s_, ctx_normed, 2 * i + s_ - 2)
            for s_ in range(2):
                load_w(N_U + s_, U0 + s_ * CONV_W)
                store_ctx(N_U + s_ - 3, 1 - s_, ctx_normed, CT + s_ - 2)
            store_ctx(N_U - 1, 1, ctx_normed, CT)
            with sp.Fori(1, CT) as i:
                for s_ in range(2):
                    load_w(N_U + 2 * i + s_, U0 + i * P + s_ * CONV_W)
            for n0, col0, last_store, own_store in ((N_GA, GA0, None, store_after_act),
                                                    (N_GC, GC0, store_after_act, store_gc),
                                                    (N_K, K0, store_gc, store_qk),
                                                    (N_Q, Q0, store_qk, store_qk),
                                                    (N_V, V0, store_qk, store_after_act)):
                for s_ in range(2):
                    load_w(n0 + s_, col0 + s_ * P)
                    if last_store:
                        last_store(n0 + s_ - 2, s_)
                if n0 == N_K:
                    sp.wait_ge(conv_used, CT)
                    sp.dma_start(cos[:], t["rope_cos"]).then_inc(rope_landed, 16)
                    sp.dma_start(sin[:], t["rope_sin"]).then_inc(rope_landed, 16)
                with sp.Fori(1, CT // 2) as i:
                    for s_ in range(2):
                        load_w(n0 + 2 * i + s_, col0 + (2 * i + s_) * P)
                        own_store(n0 + 2 * i + s_ - 2, s_)
            sp.wait_ge(qk_done, 2 * CT)
            for par in range(2):
                sp.wait_ge(stored[par], 16 * ((N_U - N_VC) + (N_V - N_GA)) // 2)
            load_k(sp, 0)
            load_q(sp, 0)
            for s_ in range(2):
                store_after_act(N_END - 2 + s_, s_)
            for par in range(2):
                sp.wait_ge(stored[par], 16 * ((N_U - N_VC) + (N_END - N_GA)) // 2)

        @block.gpsimd
        def _(pool):
            pool.memset(ident[:], 0.0).then_inc(ident_ready, 1)
            pool.wait_ge(ident_ready, 1)
            pool.affine_select(out=ident[:], in_=ident[:], compare_op=ALU.not_equal, fill=1.0, base=0,
                               pattern=[[-1, P]], channel_multiplier=1).then_inc(ident_ready, 1)

            xl = t["x"].rearrange("b t d -> (b t) d")
            xc = t["ctx"].rearrange("b t d -> (b t) d")
            for k in range(2):
                pool.dma_start(x_tok[:, k], xl[k * P:(k + 1) * P, :]).then_inc(x_landed[k], 16)
            with pool.Fori(1, TT // 2) as i:
                for k in range(2):
                    pool.wait_ge(x_turned, 8 * i + 4 * k - 4)
                    pool.dma_start(x_tok[:, k], xl[bass.ds((2 * i + k) * P, P), :]).then_inc(x_landed[k], 16)
            for k in range(2):
                pool.wait_ge(x_turned, 4 * (TT + k - 1))
                pool.dma_start(x_tok[:, k], xc[k * P:(k + 1) * P, :]).then_inc(x_landed[k], 16)

            with pool.Fori(0, N_END) as n:
                for c in range(CH):
                    pool.wait_ge(w_hi_ready[c], n + 1)
                    pool.tensor_tensor(w_lo[:, c], w_raw[:, c], w_hi[:, c].bitcast(F32), ALU.subtract
                                       ).then_inc(w_lo_ready[c], 1)

        @block.tensor
        def _(pe):
            def ada_block(nb, s_, first=False):
                for c in range(CH):
                    pe.wait_ge(ada_lo_ready, CH * nb + c + 1)
                    if c == 0 and not first:
                        pe.wait_ge(rows_ready, nb - 1)
                    for j in range(JC):
                        jj = c * JC + j
                        pe.matmul(bank(s_)[0:4, :], c_split[:, jj, :], ada_hi[:, c % 2, j, :], start=(jj == 0), stop=False)
                        mm = pe.matmul(bank(s_)[0:4, :], c_split[:, jj, :], ada_lo[:, c, j, :], start=False,
                                       stop=(jj == JT - 1))
                    mm.then_inc(ada_used[c], 1)

            def turn_x(i, k, first=False):
                pe.wait_ge(x_normed, i + 1)
                if not first:
                    pe.wait_ge(xT_by_act, 2 * i)
                    pe.wait_ge(xT_by_dve, 2 * i)
                xv = x_tok[:, k, :].rearrange("p (c j) -> p j c", j=JT)
                for b in range(4):
                    for j in range(4):
                        mm = pe.transpose(bank(2 + b)[:, j * P:(j + 1) * P], xv[:, 4 * b + j, :], ident[:])
                    mm.then_inc(x_turned, 1)

            pe.wait_ge(c_ready, 32 + 3)
            ada_block(0, 0, first=True)
            pe.wait_ge(ident_ready, 2)
            turn_x(0, 0, first=True)
            ada_block(1, 1, first=True)
            turn_x(1, 1)
            pe.wait_ge(par_landed, 16 * N_PAR)
            for i in range(CT):
                mm = pe.matmul(bank(6)[:, i * n_par:(i + 1) * n_par], chan_rows[0:n_par, i * P:(i + 1) * P],
                               ident[0:n_par, 0:n_par], start=True, stop=True)
            mm.then_inc(cols_done, 1)
            with pe.Fori(1, 3) as i:
                for s_ in range(2):
                    ada_block(2 * i + s_, s_)
                    turn_x(2 * i + s_, s_)

            def to_columns(k):
                for j in range(JT):
                    rows = ada_rows[0:4, k * D:(k + 1) * D].rearrange("v (c j) -> v j c", j=JT)[:, j, :]
                    mm = pe.matmul(bank(6)[:, 2 * (k * JT + j):2 * (k * JT + j) + 2], rows, pair_sum[0:4, :],
                                   start=True, stop=True)
                return mm

            pe.wait_ge(rows_ready, MOD_BLOCKS // 2)
            pe.wait_ge(par_done, 1)
            to_columns(0)
            for i in range(MOD_BLOCKS - 2, MOD_BLOCKS):
                ada_block(i, i % 2)
                turn_x(i, i % 2)
            pe.wait_ge(rows_ready, MOD_BLOCKS)
            to_columns(1).then_inc(cols_done, 1)
            turn_x(TT, 0)

            for m, nb, c, slot in gate_chunks:
                if m == CH:
                    turn_x(TT + 1, 1)
                    pe.wait_ge(xT_by_act, 2 * X_TILES)
                    pe.wait_ge(xT_by_dve, 2 * X_TILES)
                pe.wait_ge(ada_landed[c], 16 * (nb + 1))
                for j in range(JC):
                    mm = pe.matmul(bank(GATE_BANKS[nb - MOD_BLOCKS])[0:2, :], c_act[:, c * JC + j, :], gate_w[:, slot, j, :],
                                   start=(c == 0 and j == 0), stop=(c == CH - 1 and j == JC - 1))
                mm.then_inc(ada_used[c], 1)

            def ctx_tile(n, s_, head=False, second=False):
                if not (head or second):
                    pe.wait_ge(ctx_freed, n - 1)
                for c in range(CH):
                    pe.wait_ge(w_hi_ready[c], n + 1)
                    pe.wait_ge(w_lo_ready[c], n + 1)
                    for j in range(JC):
                        jj = c * JC + j
                        if head:
                            pe.wait_ge(hc_ready, jj + 1)
                        pe.matmul(bank(s_), w_hi[:, c, j, :], hc[:, jj, :], start=(jj == 0), stop=False,
                                  skip_group_check=True)
                        mm = pe.matmul(bank(s_)[:, 0:TC], w_lo[:, c, j, :], hc[:, jj, 0:TC], start=False,
                                       stop=(jj == JT - 1), skip_group_check=True)
                    mm.then_inc(w_used[c], 1)

            def ctx_sums(k, par):
                pe.wait_ge(ctx_squared, k + 1)
                pe.matmul(bank(4 + par)[:, 0:TC], block_ones[:], evac[:, par, 512:512 + TC], start=True, stop=True
                          ).then_inc(ctx_summed, 1)

            ctx_tile(0, 0, head=True)
            ctx_tile(1, 1, second=True)
            with pe.Fori(1, 4) as i:
                for s_ in range(2):
                    ctx_tile(2 * i + s_, s_)
            ctx_tile(N_KC, 0)
            ctx_tile(N_KC + 1, 1)
            ctx_sums(0, 0)
            with pe.Fori(1, 4) as i:
                for s_ in range(2):
                    ctx_tile(N_KC + 2 * i + s_, s_)
                    ctx_sums(2 * i + s_ - 1, (s_ + 1) % 2)

            def tile(n, s_):
                for c in range(CH):
                    pe.wait_ge(w_hi_ready[c], n + 1)
                    pe.wait_ge(w_lo_ready[c], n + 1)
                    for j in range(JC):
                        jj = c * JC + j
                        for w, x, last in ((w_hi, h_hi, False), (w_hi, h_lo, False), (w_lo, h_hi, jj == JT - 1)):
                            for hf in range(2):
                                mm = pe.matmul(bank(2 * s_ + hf), w[:, c, j, :], x[:, jj, hf * BANK:(hf + 1) * BANK],
                                               start=(jj == 0 and w is w_hi and x is h_hi), stop=last)
                    mm.then_inc(w_used[c], 1)

            pe.wait_ge(h_ready, JT)
            pe.wait_ge(ctx_freed, N_U)
            tile(N_U, 0)
            ctx_sums(CT - 1, 1)
            tile(N_U + 1, 1)

            def pair(n):
                for s_ in range(2):
                    pe.wait_ge(psum_freed, n + s_ - N_U - 1)
                    tile(n + s_, s_)

            with pe.Fori(1, CT) as i:
                pair(N_U + 2 * i)
            pair(N_GA)
            pe.wait_ge(ctx_root, CT)
            for i in range(CT):
                pe.wait_ge(conv_done, i + 1)
                for hf in range(2):
                    mm = pe.matmul(bank(4 + hf), mean_ones[:], conv[:, i, hf * BANK:(hf + 1) * BANK],
                                   start=(i == 0), stop=(i == CT - 1))
            mm.then_inc(mean_done, 1)
            pair(N_GA + 2)
            for i in range(CT):
                pe.wait_ge(ln_squared, i + 1)
                for hf in range(2):
                    mm = pe.matmul(bank(6 + hf), mean_ones[:], evac[:, i % 2, hf * BANK:(hf + 1) * BANK],
                                   start=(i == 0), stop=(i == CT - 1))
                mm.then_inc(ln_sq_used, 1)
            with pe.Fori(2, 4) as i:
                pair(N_GA + 2 * i)
            with pe.Fori(0, 4) as i:
                pair(N_GC + 2 * i)

            def qk_sums(k, par):
                pe.wait_ge(psum_freed, N_K - N_U + k + 1)
                for hf in range(2):
                    mm = pe.matmul(bank(4 + hf), block_ones[:], sq[:, par, hf * BANK:(hf + 1) * BANK],
                                   start=True, stop=True)
                mm.then_inc(qk_summed, 1)

            pair(N_K)
            qk_sums(0, 0)
            with pe.Fori(1, CT) as i:
                for s_ in range(2):
                    n = N_K + 2 * i + s_
                    pe.wait_ge(psum_freed, n - N_U - 1)
                    tile(n, s_)
                    pe.wait_ge(qk_root, 2 * i + s_ - 1)
                    qk_sums(2 * i + s_ - 1, (s_ + 1) % 2)
            pe.wait_ge(psum_freed, N_V - N_U - 1)
            tile(N_V, 0)
            pe.wait_ge(qk_root, 2 * CT - 1)
            qk_sums(2 * CT - 1, 1)
            pe.wait_ge(psum_freed, N_V - N_U)
            tile(N_V + 1, 1)
            with pe.Fori(1, 4) as i:
                pair(N_V + 2 * i)

        @block.scalar
        def _(act):
            act.wait_ge(c_ready, 32)
            nc.scalar.activation(c_act[:].rearrange("p j v -> p v j"), c_col[:], ACT.Silu).then_inc(c_ready, 1)
            act.wait_ge(c_ready, 32 + 1)
            nc.scalar.activation(c_split[:, :, 0:2], c_act[:], ACT.Copy).then_inc(c_ready, 1)
            act.preload_act_table(ACT.Sqrt)
            act.wait_ge(eps_ready, 1)

            def norm_tile(i, k, half):
                act.wait_ge(x_landed[k], 16 * (half + 1))
                nc.scalar.activation(x_sq[:], x_tok[:, k, :], ACT.Square, accum_out=ln_x[:, 0, bass.ds(i, 1)]
                                     ).then_inc(x_squared, 1)
                act.wait_ge(x_squared, i + 1)
                nc.scalar.activation(ln_x[:, 1, bass.ds(i, 1)], ln_x[:, 0, bass.ds(i, 1)], ACT.Sqrt, scale=1.0 / D,
                                     bias=eps_col).then_inc(x_root, 1)

            def copy_xT(i, dst, col):
                for b in range(2):
                    act.wait_ge(x_turned, 4 * i + b + 1)
                    nc.scalar.activation(dst[:, 4 * b:4 * b + 4, bass.ds(col, P)],
                                         bank(2 + b).rearrange("p (j c) -> p j c", j=4), ACT.Copy).then_inc(xT_by_act, 1)

            def copy_rows(nb, s_):
                act.wait_ge(ada_used[CH - 1], nb + 1)
                nc.scalar.activation(ada_rows[0:4, bass.ds(nb * BANK, BANK)], bank(s_)[0:4, :], ACT.Copy
                                     ).then_inc(rows_ready, 1)

            def ada_high(nb, c, first=False):
                act.wait_ge(ada_landed[c], 16 * (nb + 1))
                if c >= 2:
                    act.wait_ge(ada_used[c - 2], nb + 1)
                elif not first:
                    act.wait_ge(ada_used[c + 2], nb)
                nc.scalar.activation(ada_hi[:, c % 2], ada_w[:, c], ACT.Copy).then_inc(ada_hi_ready, 1)

            def setup_step(n, k, half, first=False):
                norm_tile(n, k, half)
                ada_high(n, 0, first)
                ada_high(n, 1, first)
                if not first:
                    copy_rows(n - 1, 1 - k)
                    copy_xT(n - 1, xT, (n - 1) * P)
                ada_high(n, 2)
                ada_high(n, 3)

            setup_step(0, 0, 0, first=True)
            setup_step(1, 1, 0)
            with act.Fori(1, TT // 2) as i:
                for k in range(2):
                    setup_step(2 * i + k, k, i)
            copy_rows(TT - 1, 1)
            norm_tile(TT, 0, TT // 2)
            copy_xT(TT - 1, xT, (TT - 1) * P)
            norm_tile(TT + 1, 1, TT // 2)
            for k in range(2):
                copy_xT(TT + k, xcT, k * P)

            def split_w(n, first=False):
                for c in range(CH):
                    act.wait_ge(w_landed[c], 16 * (n + 1))
                    if not first:
                        act.wait_ge(w_used[c], n)
                    nc.scalar.activation(w_hi[:, c], w_raw[:, c], ACT.Copy).then_inc(w_hi_ready[c], 1)

            act.wait_ge(par_landed, 16 * N_PAR)
            for j in range(JT):
                act.wait_ge(modulated, j + 1)
                nc.scalar.activation(hc[:, j, 0:TC], xcT[:, j, :], ACT.Copy).then_inc(rounded, 1)
            for j in range(JT):
                act.wait_ge(modulated, JT + j + 1)
                nc.scalar.activation(h_hi[:, j, :], xT[:, j, :], ACT.Copy).then_inc(rounded, 1)
            act.wait_ge(ada_used[CH - 1], ADA_BLOCKS)
            split_w(0, first=True)
            act.wait_ge(hc_ready, JT)
            for q in range(ADA_BLOCKS - MOD_BLOCKS):
                nc.scalar.activation(gate_row[0:1, q * BANK:(q + 1) * BANK], bank(GATE_BANKS[q])[0:1, :], ACT.Copy
                                     ).then_inc(gate_row_ready, 1)

            def ctx_evac(n, s_, freed=True):
                act.wait_ge(tile_done, n + 1)
                if freed:
                    act.wait_ge(ctx_freed, n - 1)
                nc.scalar.activation(evac[:, s_, TC:2 * TC], bank(s_)[:, TC:2 * TC], ACT.Copy).then_inc(ctx_half, 1)

            for n in range(2):
                split_w(n + 1)
                ctx_evac(n, n, freed=False)
            with act.Fori(1, 4) as i:
                for s_ in range(2):
                    split_w(2 * i + s_ + 1)
                    ctx_evac(2 * i + s_, s_)

            def ctx_square(k, par):
                act.wait_ge(ctx_freed, N_KC + k + 1)
                nc.scalar.activation(evac[:, par, 2 * TC:3 * TC], evac[:, par, 0:TC], ACT.Square).then_inc(ctx_squared, 1)

            def ctx_sqrt(k, par):
                act.wait_ge(ctx_summed, k + 1)
                nc.scalar.activation(evac[:, par, 3 * TC:4 * TC], bank(4 + par)[:, 0:TC], ACT.Sqrt,
                                     scale=1.0 / DH, bias=eps_col).then_inc(ctx_root, 1)

            for k in range(2):
                split_w(N_KC + k + 1)
                ctx_evac(N_KC + k, k)
                ctx_square(k, k)
            ctx_sqrt(0, 0)
            with act.Fori(1, 4) as i:
                for s_ in range(2):
                    k = 2 * i + s_
                    split_w(N_KC + k + 1)
                    act.wait_ge(ctx_normed, k - 1)
                    ctx_evac(N_KC + k, s_)
                    ctx_square(k, s_)
                    ctx_sqrt(k - 1, (s_ + 1) % 2)

            def glu_value(n, i, first=False):
                split_w(n + 1)
                act.wait_ge(tile_done, n + 1)
                if not first:
                    act.wait_ge(glu_used, i)
                nc.scalar.activation(evac[:, 0, :], bank(0, 2), ACT.Copy).then_inc(psum_freed, 1)

            def glu_gate(n):
                split_w(n + 1)
                act.wait_ge(tile_done, n + 1)
                nc.scalar.activation(evac[:, 1, :], bank(2, 2), ACT.Sigmoid).then_inc(psum_freed, 1)

            split_w(N_U + 1)
            ctx_sqrt(CT - 1, 1)
            act.wait_ge(ctx_normed, CT)
            act.preload_act_table(ACT.Sigmoid)
            act.wait_ge(tile_done, N_U + 1)
            nc.scalar.activation(evac[:, 0, :], bank(0, 2), ACT.Copy).then_inc(psum_freed, 1)
            glu_gate(N_U + 1)
            with act.Fori(1, CT) as i:
                glu_value(N_U + 2 * i, i)
                glu_gate(N_U + 2 * i + 1)

            def to_stage(n, s_, count, func, last=False):
                if not last:
                    split_w(n + 1)
                act.wait_ge(tile_done, n + 1)
                act.wait_ge(stored[s_], count)
                nc.scalar.activation(stage[:, s_, :], bank(2 * s_, 2), func).then_inc(psum_freed, 1)

            act.preload_act_table(ACT.Silu)
            for k in range(4):
                to_stage(N_GA + k, k % 2, 16 * (CT + k // 2), ACT.Silu)
            for i in range(CT):
                act.wait_ge(centred, i + 1)
                if i >= 2:
                    act.wait_ge(ln_sq_used, i - 1)
                nc.scalar.activation(evac[:, i % 2, :], conv[:, i, :], ACT.Square).then_inc(ln_squared, 1)
            act.wait_ge(ln_sq_used, CT)
            nc.scalar.activation(evac[:, 0, :], bank(6, 2), ACT.Sqrt, bias=eps_col).then_inc(ln_root, 1)
            act.preload_act_table(ACT.Silu)
            with act.Fori(2, 4) as i:
                for s_ in range(2):
                    to_stage(N_GA + 2 * i + s_, s_, 16 * (CT + i), ACT.Silu)

            act.wait_ge(ln_ready, CT)

            def conv_gate(k, s_):
                split_w(N_GC + k + 1)
                act.wait_ge(gate_used, k + 1)
                par = chan_par[:, bass.ds(k, 1), :].rearrange("p i k -> p (i k)")
                nc.scalar.activation(evac[:, 1, :], conv[:, bass.ds(k, 1), :].rearrange("p i t -> p (i t)"), ACT.Silu,
                                     scale=par[:, CONV_K + 1:CONV_K + 2], bias=par[:, CONV_K + 2:CONV_K + 3]
                                     ).then_inc(conv_used, 1)
                act.wait_ge(tile_done, N_GC + k + 1)
                nc.scalar.activation(evac[:, 0, :], bank(2 * s_, 2), ACT.Silu).then_inc(psum_freed, 1)

            with act.Fori(0, 4) as i:
                for s_ in range(2):
                    conv_gate(2 * i + s_, s_)
            act.preload_act_table(ACT.Sqrt)

            def qk_evac(n, k, s_, gain):
                split_w(n + 1)
                act.wait_ge(tile_done, n + 1)
                nc.scalar.activation(evac[:, s_, :], bank(2 * s_, 2), ACT.Copy, scale=gain).then_inc(qk_scaled, 1)
                nc.scalar.activation(sq[:, s_, :], bank(2 * s_, 2), ACT.Square).then_inc(psum_freed, 1)

            def qk_sqrt(k):
                act.wait_ge(qk_summed, k + 1)
                nc.scalar.activation(rstd[:], bank(4, 2), ACT.Sqrt, scale=1.0 / DH, bias=eps_col).then_inc(qk_root, 1)

            act.wait_ge(gate_used, CT + 1)
            qk_evac(N_K, 0, 0, k_gain)
            qk_evac(N_K + 1, 1, 1, k_gain)
            qk_sqrt(0)

            def qk_pair(n, k, gain):
                for s_ in range(2):
                    act.wait_ge(qk_roped, k + s_ - 1)
                    act.wait_ge(qk_summed, k + s_ - 1)
                    qk_evac(n + s_, k + s_, s_, gain)
                    act.wait_ge(qk_done, k + s_ - 1)
                    qk_sqrt(k + s_ - 1)

            with act.Fori(1, 4) as i:
                qk_pair(N_K + 2 * i, 2 * i, k_gain)
            with act.Fori(4, 8) as i:
                qk_pair(N_K + 2 * i, 2 * i, q_gain)
            to_stage(N_V, 0, 16 * (CT + 16), ACT.Copy)
            act.wait_ge(qk_done, 2 * CT - 1)
            qk_sqrt(2 * CT - 1)
            to_stage(N_V + 1, 1, 16 * (CT + 16), ACT.Copy)
            with act.Fori(1, 3) as i:
                for s_ in range(2):
                    to_stage(N_V + 2 * i + s_, s_, 16 * (CT + 16 + i), ACT.Copy)
            to_stage(N_END - 2, 0, 16 * (CT + 19), ACT.Copy)
            to_stage(N_END - 1, 1, 16 * (CT + 19), ACT.Copy, last=True)

        @block.vector
        def _(dve):
            nc.vector.memset(eps_col, EPS).then_inc(eps_ready, 1)
            nc.vector.memset(mean_ones[:], 1.0 / CONV_W)
            nc.vector.memset(block_ones[0:DH, 0:DH], 1.0)
            nc.vector.memset(block_ones[0:DH, DH:P], 0.0)
            nc.vector.memset(block_ones[DH:P, 0:DH], 0.0)
            nc.vector.memset(block_ones[DH:P, DH:P], 1.0)
            nc.vector.memset(y_pad[:, 0:HALO], 0.0)
            nc.vector.memset(y_pad[:, HALO + T:], 0.0)
            dve.wait_ge(ident_ready, 2)
            nc.vector.tensor_tensor(pair_sum[0:4, :], ident[0:4, 0:2], ident[0:4, 2:4], ALU.add)

            def norm_tile(i, k):
                dve.wait_ge(x_root, i + 1)
                nc.vector.reciprocal(ln_x[:, 2, bass.ds(i, 1)], ln_x[:, 1, bass.ds(i, 1)]).then_inc(recip_done, 1)
                dve.wait_ge(recip_done, i + 1)
                nc.vector.tensor_scalar(x_tok[:, k, :], x_tok[:, k, :], ln_x[:, 2, bass.ds(i, 1)], None, ALU.mult
                                        ).then_inc(x_normed, 1)

            def copy_xT(i, dst, col):
                for b in range(2, 4):
                    dve.wait_ge(x_turned, 4 * i + b + 1)
                    nc.vector.tensor_copy(dst[:, 4 * b:4 * b + 4, bass.ds(col, P)],
                                          bank(2 + b).rearrange("p (j c) -> p j c", j=4)).then_inc(xT_by_dve, 1)

            def ada_low(nb, c):
                dve.wait_ge(ada_hi_ready, CH * nb + c + 1)
                nc.vector.tensor_tensor(ada_lo[:, c], ada_w[:, c], ada_hi[:, c % 2].bitcast(F32), ALU.subtract
                                        ).then_inc(ada_lo_ready, 1)

            def setup_step(n, k, first=False):
                norm_tile(n, k)
                ada_low(n, 0)
                ada_low(n, 1)
                if not first:
                    copy_xT(n - 1, xT, (n - 1) * P)
                ada_low(n, 2)
                ada_low(n, 3)

            dve.wait_ge(c_ready, 32 + 2)
            nc.vector.tensor_tensor(c_split[:, :, 2:4], c_act[:], c_split[:, :, 0:2].bitcast(F32), ALU.subtract
                                    ).then_inc(c_ready, 1)
            setup_step(0, 0, first=True)
            setup_step(1, 1)
            dve.wait_ge(cols_done, 1)
            nc.vector.tensor_copy(chan_par[:].rearrange("p i k -> p (i k)"), bank(6)[:, 0:CT * n_par]).then_inc(par_done, 1)
            with dve.Fori(1, TT // 2) as i:
                for k in range(2):
                    setup_step(2 * i + k, k)
            norm_tile(TT, 0)
            copy_xT(TT - 1, xT, (TT - 1) * P)
            norm_tile(TT + 1, 1)
            for k in range(2):
                copy_xT(TT + k, xcT, k * P)

            dve.wait_ge(cols_done, 2)
            cols = bank(6)[:, 0:4 * JT].rearrange("p (k j v) -> p k j v", k=2, v=2)
            for v in range(2):
                nc.vector.tensor_tensor(mod[:, 1, :, v], cols[:, 0, :, v], b_col[:, 0, :], ALU.add)
                nc.vector.tensor_tensor(mod[:, 0, :, v], cols[:, 1, :, v], b_col[:, 1, :], ALU.add).then_inc(mod_step, 1)
            dve.wait_ge(mod_step, 2)
            for v in range(2):
                nc.vector.scalar_tensor_tensor(out=mod[:, 0, :, v], in0=mod[:, 0, :, v], scalar=1.0, in1=g_col[:],
                                               op0=ALU.add, op1=ALU.mult).then_inc(mod_ready, 1)
            dve.wait_ge(mod_ready, 2)
            dve.wait_ge(xT_by_act, 2 * X_TILES)
            for j in range(JT):
                nc.vector.tensor_scalar(xcT[:, j, :], xcT[:, j, :], mod[:, 0, j, 1:2], mod[:, 1, j, 1:2], ALU.mult, ALU.add
                                        ).then_inc(modulated, 1)
            for j in range(JT):
                dve.wait_ge(rounded, j + 1)
                nc.vector.tensor_tensor(hc[:, j, TC:2 * TC], xcT[:, j, :], hc[:, j, 0:TC].bitcast(F32), ALU.subtract
                                        ).then_inc(hc_ready, 1)
            for j in range(JT):
                nc.vector.tensor_scalar(xT[:, j, :], xT[:, j, :], mod[:, 0, j, 0:1], mod[:, 1, j, 0:1], ALU.mult, ALU.add
                                        ).then_inc(modulated, 1)
                if j >= 1:
                    dve.wait_ge(rounded, JT + j)
                    nc.vector.tensor_tensor(h_lo[:, j - 1, :], xT[:, j - 1, :], h_hi[:, j - 1, :].bitcast(F32), ALU.subtract
                                            ).then_inc(h_ready, 1)
            dve.wait_ge(rounded, 2 * JT)
            nc.vector.tensor_tensor(h_lo[:, JT - 1, :], xT[:, JT - 1, :], h_hi[:, JT - 1, :].bitcast(F32), ALU.subtract
                                    ).then_inc(h_ready, 1)

            def ctx_v(n, s_, stores):
                dve.wait_ge(ctx_half, n + 1)
                if stores is not None:
                    dve.wait_ge(stored[s_], stores)
                nc.vector.tensor_tensor(stage[:, s_, 0:TC], bank(s_)[:, 0:TC], evac[:, s_, TC:2 * TC], ALU.add
                                        ).then_inc(ctx_freed, 1)

            dve.wait_ge(gate_stored, 16)
            for n in range(2):
                ctx_v(n, n, None)
            with dve.Fori(1, 4) as i:
                for s_ in range(2):
                    ctx_v(2 * i + s_, s_, 16 * i)

            def ctx_k_sum(k, s_):
                dve.wait_ge(ctx_half, N_KC + k + 1)
                nc.vector.tensor_tensor(evac[:, s_, 0:TC], bank(s_)[:, 0:TC], evac[:, s_, TC:2 * TC], ALU.add
                                        ).then_inc(ctx_freed, 1)

            def ctx_k_norm(k, s_, stores):
                dve.wait_ge(ctx_root, k + 1)
                nc.vector.reciprocal(evac[:, s_, 3 * TC:4 * TC], evac[:, s_, 3 * TC:4 * TC]).then_inc(recip_done, 1)
                dve.wait_ge(recip_done, X_TILES + k + 1)
                dve.wait_ge(stored[s_], stores)
                nc.vector.scalar_tensor_tensor(out=stage[:, s_, 0:TC], in0=evac[:, s_, 0:TC], scalar=k_gain,
                                               in1=evac[:, s_, 3 * TC:4 * TC], op0=ALU.mult, op1=ALU.mult
                                               ).then_inc(ctx_normed, 1)

            ctx_k_sum(0, 0)
            ctx_k_sum(1, 1)
            ctx_k_norm(0, 0, 16 * 4)
            with dve.Fori(1, 4) as i:
                ctx_k_sum(2 * i, 0)
                ctx_k_norm(2 * i - 1, 1, 16 * (3 + i))
                ctx_k_sum(2 * i + 1, 1)
                ctx_k_norm(2 * i, 0, 16 * (4 + i))
            ctx_k_norm(CT - 1, 1, 16 * 7)

            y = y_pad[:, HALO:HALO + T]
            acc = conv[:, CT - 1, :]

            def conv_tile(i):
                dve.wait_ge(psum_freed, 2 * i + 2)
                nc.vector.tensor_tensor(y, evac[:, 0, :], evac[:, 1, :], ALU.mult).then_inc(glu_used, 1)
                nc.vector.tensor_copy(tap_w[:], chan_par[:, bass.ds(i, 1), :].rearrange("p i k -> p (i k)")
                                      ).then_inc(taps_ready, 1)
                dve.wait_ge(taps_ready, i + 1)
                dve.wait_ge(glu_used, i + 1)
                nc.vector.tensor_scalar(acc, y_pad[:, 0:T], tap_w[:, 0:1], tap_w[:, CONV_K:CONV_K + 1], ALU.mult, ALU.add
                                        ).then_inc(tap_done, 1)
                for k in range(1, CONV_K):
                    dve.wait_ge(tap_done, i * (CONV_K - 1) + k)
                    last = k == CONV_K - 1
                    out = conv[:, bass.ds(i, 1), :].rearrange("p i t -> p (i t)") if last else acc
                    nc.vector.scalar_tensor_tensor(out=out, in0=y_pad[:, k:k + T], scalar=tap_w[:, k:k + 1], in1=acc,
                                                   op0=ALU.mult, op1=ALU.add).then_inc(conv_done if last else tap_done, 1)
                dve.wait_ge(conv_done, i + 1)

            with dve.Fori(0, CT) as i:
                conv_tile(i)

            dve.wait_ge(mean_done, 1)
            for i in range(CT):
                nc.vector.tensor_tensor(conv[:, i, :], conv[:, i, :], bank(4, 2), ALU.subtract).then_inc(centred, 1)
            dve.wait_ge(ln_root, 1)
            nc.vector.reciprocal(evac[:, 0, :], evac[:, 0, :]).then_inc(recip_done, 1)
            dve.wait_ge(recip_done, X_TILES + CT + 1)
            for i in range(CT):
                nc.vector.tensor_tensor(conv[:, i, :], conv[:, i, :], evac[:, 0, :], ALU.mult).then_inc(ln_ready, 1)
            dve.wait_ge(ln_ready, CT)
            dve.sem_inc(gate_used, 1)

            with dve.Fori(0, 4) as i:
                for s_ in range(2):
                    dve.wait_ge(conv_used, 2 * i + s_ + 1)
                    dve.wait_ge(psum_freed, N_GC - N_U + 2 * i + s_ + 1)
                    dve.wait_ge(stored[s_], 16 * (CT + 4 + i))
                    nc.vector.tensor_tensor(stage[:, s_, :], evac[:, 0, :], evac[:, 1, :], ALU.mult
                                            ).then_inc(gate_used, 1)

            swap = [(q + 16) % 32 for q in range(32)]

            def rope(k, s_, first=False):
                dve.wait_ge(qk_scaled, k + 1)
                if not first:
                    dve.wait_ge(qk_roped, k)
                nc.vector.tensor_tensor(roped[:, s_, :], evac[:, s_, :], cos[:], ALU.mult).then_inc(qk_cos, 1)
                nc.vector.stream_shuffle(turned[:], evac[:, s_, :], swap).then_inc(qk_turned, 1)
                dve.wait_ge(qk_turned, 2 * k + 1)
                nc.vector.tensor_tensor(turned[:], turned[:], sin[:], ALU.mult).then_inc(qk_turned, 1)
                dve.wait_ge(qk_turned, 2 * k + 2)
                dve.wait_ge(qk_cos, k + 1)
                nc.vector.tensor_tensor(roped[:, s_, :], roped[:, s_, :], turned[:], ALU.add).then_inc(qk_roped, 1)

            def qk_norm(k, s_, stores):
                dve.wait_ge(qk_root, k + 1)
                nc.vector.reciprocal(rstd[:], rstd[:]).then_inc(recip_done, 1)
                dve.wait_ge(recip_done, X_TILES + CT + 1 + k + 1)
                dve.wait_ge(stored[s_], stores)
                nc.vector.tensor_tensor(stage[:, s_, :], roped[:, s_, :], rstd[:], ALU.mult).then_inc(qk_done, 1)

            dve.wait_ge(rope_landed, 32)
            rope(0, 0, first=True)
            rope(1, 1)
            qk_norm(0, 0, 16 * (CT + 8))
            with dve.Fori(1, CT) as i:
                dve.wait_ge(qk_done, 2 * i - 1)
                rope(2 * i, 0)
                qk_norm(2 * i - 1, 1, 16 * (CT + 7 + i))
                dve.wait_ge(qk_done, 2 * i)
                rope(2 * i + 1, 1)
                qk_norm(2 * i, 0, 16 * (CT + 8 + i))
            qk_norm(2 * CT - 1, 1, 16 * (CT + 8 + 7))


def attention(nc, t, sem, Region, base, bank, ctx_kv_d, proj_d, o_all, p0_sum, raw, load_k, load_q):
    r = Region(base)
    q_st = r.take("q_st", 2 * 2 * T, F32R)[:].rearrange("p (b m t) -> p b m t", b=2, m=2)
    k_hi = r.take("k_hi", 2 * 2 * KEYS, F32R)[:].rearrange("p (b m t) -> p b m t", b=2, m=2)
    k_lo = r.take("k_lo", 2 * 2 * KEYS, F32R)[:].rearrange("p (b m t) -> p b m t", b=2, m=2)
    v_hi = r.take("v_hi", 2 * KEYS, F32R)[:].rearrange("p (b t) -> p b t", b=2)
    v_lo = r.take("v_lo", 2 * KEYS, F32R)[:].rearrange("p (b t) -> p b t", b=2)
    q_raw, k_raw = raw.q, raw.k
    v_raw = r.take("v_raw", KEYS)
    prob = r.take("prob", 2 * 2 * KEYS)[:].rearrange("p (b m t) -> p b m t", b=2, m=2)
    diff = r.take("diff", 2 * KEYS)[:].rearrange("p (b t) -> p b t", b=2)
    QG = 2 * P
    dT_hi = r.take("dT_hi", 2 * KT * QG, F32R)[:].rearrange("p (b k q) -> p b k q", b=2, k=KT)
    dT_lo = r.take("dT_lo", 2 * KT * QG, F32R)[:].rearrange("p (b k q) -> p b k q", b=2, k=KT)
    assert r.at <= base + ROTARY_AT
    r = Region(raw.end)
    ident = r.take("ident_b", P)
    top = r.take("top", 4)[:].rearrange("p (b m) -> p b m", b=2)
    neg_top = r.take("neg_top", 4)[:].rearrange("p (b m) -> p b m", b=2)
    p1_sum = r.take("p1_sum", 2)
    p1_inv = r.take("p1_inv", 2)
    map1_factor = r.take("map1_factor", 2)
    lam_rows = r.take("lam_rows", 4 * DH)[:].rearrange("p (k d) -> p k d", k=4)
    lam_dots = r.take("lam_dots", 2)
    lam_exp = r.take("lam_exp", 2)
    neg_lam = r.take("neg_lam", 1)
    ones_row = r.take("ones_row", P)
    lam_tmp = r.take("lam_tmp", 2 * DH)[:].rearrange("p (k d) -> p k d", k=2)
    assert r.at <= o_all_start(nc), r.at

    ROUNDS = ((0, 4), (4, 8), (8, 10))
    V_STEPS = (3, 5, 7)
    V_ROUNDS = len(ROUNDS)

    SHARE = 6 * P

    def use6(s_, second):
        return V_ROUNDS + 2 * s_ + second

    def use7(h, st):
        last = isinstance(h, int) and h == HEADS - 1
        return (TT + V_ROUNDS) * h + st + (0 if last else sum(v <= st for v in V_STEPS))

    def use7_v(h, rd):
        return (TT + V_ROUNDS) * h + V_STEPS[rd] + rd

    def ahead(h, st, by):
        return (h, st + by) if st + by < TT else (h + 1, st + by - TT)

    q_landed, k_landed = raw.q_landed, raw.k_landed
    v_landed, lam_landed = sem("v_landed"), sem("lam_landed")
    id_ready = sem("id_ready")
    ones_ready = sem("ones_ready")
    lam_step = sem("lam_step")
    lam_spread = sem("lam_spread")
    lam_ready = sem("lam_ready")
    k_rounded = sem("k_rounded")
    q_rounded = sem("q_rounded")
    k_split = sem("k_split")
    q_split = sem("q_split")
    v_turned = sem("v_turned")
    scores_done = [sem(f"scores_done{m}") for m in range(2)]
    top_found = [sem(f"top_found{m}") for m in range(2)]
    top_ready = [sem(f"top_ready{m}") for m in range(2)]
    exp_done = [sem(f"exp_done{m}") for m in range(2)]
    inv_ready = sem("inv_ready")
    factor_ready = sem("factor_ready")
    rest_ready = sem("rest_ready")
    diff_ready = sem("diff_ready")
    turned6, hi6, free6 = sem("turned6"), sem("hi6"), sem("free6")
    turned7, hi7, free7 = sem("turned7"), sem("hi7"), sem("free7")
    pv_done = sem("pv_done")
    o_copied = sem("o_copied")
    v_read = sem("v_read")

    with nc.Block(name="attention") as block:

        @block.sync
        def _(sp):
            def load_v(h):
                sp.dma_start(v_raw[:, 0:TC], ctx_kv_d[bass.ds(h * P, P), :]).then_inc(v_landed, 16)
                sp.dma_start(v_raw[:, TC:], proj_d[bass.ds((N_V - N_GA) * P + h * P, P), :]).then_inc(v_landed, 16)

            for k, name in enumerate(("lam_q1", "lam_k1", "lam_q2", "lam_k2")):
                sp.dma_start(lam_rows[0:1, k, :], t[name]).then_inc(lam_landed, 16)
            load_v(0)
            with sp.Fori(1, HEADS) as h:
                sp.wait_ge(k_split, 2 * h)
                load_k(sp, h)
                sp.wait_ge(q_split, 2 * h)
                load_q(sp, h)
                sp.wait_ge(v_read, h)
                load_v(h)

        @block.tensor
        def _(pe):
            def turn_v(h, rd, to, turned):
                k0, k1 = ROUNDS[rd]
                for k in range(k0, k1):
                    mm = pe.transpose(bank(to)[:, (k - k0) * P:(k - k0 + 1) * P], v_raw[:, k * P:(k + 1) * P], ident[:])
                mm.then_inc(turned, 1)

            def scores(h, st, b, m, s_, first=False):
                if st == 0 and m == 0:
                    pe.wait_ge(k_split, 2 * (h + 1))
                    pe.wait_ge(q_split, 2 * (h + 1))
                if not first:
                    pe.wait_ge(exp_done[m], s_)
                q = q_st[:, b, m, st * P:(st + 1) * P]
                for c0 in range(0, KEYS, BANK):
                    c1 = min(c0 + BANK, KEYS)
                    out = bank(3 * m, 3)[:, c0:c1]
                    pe.matmul(out, q, k_hi[:, b, m, c0:c1], start=True, stop=False)
                    mm = pe.matmul(out, q, k_lo[:, b, m, c0:c1], start=False, stop=True)
                mm.then_inc(scores_done[m], 1)

            def turn_diff(h, st, s_, rd):
                if rd == 0:
                    pe.wait_ge(diff_ready, s_ + 1)
                if rd == 1:
                    pe.wait_ge(free7, use7(h, st) + 1)
                    if st % 2 == 0:
                        pe.wait_ge(o_copied, 4 * h + st // 2 + 1)
                else:
                    pe.wait_ge(free6, use6(s_, rd // 2))
                if rd == 1:
                    pe.wait_ge(rest_ready, 2 * s_ + 2)
                k0, k1 = ROUNDS[rd]
                for k in range(k0, k1):
                    mm = pe.transpose(bank(7 if rd == 1 else 6)[:, (k - k0) * P:(k - k0 + 1) * P],
                                      diff[:, st % 2, k * P:(k + 1) * P], ident[:])
                mm.then_inc(turned7 if rd == 1 else turned6, 1)

            def product_v(h, st, b, s_, k0, k1):
                g = st // 2 % 2
                if k0 == 0:
                    pe.wait_ge(free7, use7(h, st) + 2)
                    pe.wait_ge(free6, use6(s_, 0) + 1)
                for k in range(k0, k1):
                    if k == ROUNDS[2][0]:
                        pe.wait_ge(free6, use6(s_, 1) + 1)
                    vh, vl = v_hi[:, b, k * P:(k + 1) * P], v_lo[:, b, k * P:(k + 1) * P]
                    mm = split_matmuls(pe, bank(7)[:, 0:QG], vh, vl, dT_hi[:, g, k, :], dT_lo[:, g, k, :],
                                       k == 0, k == KT - 1)
                if k1 == KT:
                    mm.then_inc(pv_done, 1)

            scores(0, 0, 0, 0, 0, first=True)
            scores(0, 0, 0, 1, 0, first=True)
            pe.wait_ge(lam_step, 2)
            pe.wait_ge(ones_ready, 1)
            pe.matmul(bank(7)[:, 0:2], ones_row[0:1, :], lam_dots[0:1, :], start=True, stop=True).then_inc(lam_spread, 1)
            pe.wait_ge(id_ready, 2)
            pe.wait_ge(v_landed, 32)
            turn_v(0, 0, 6, turned6)
            scores(0, 1, 0, 0, 1)
            pe.wait_ge(free6, 1)
            turn_v(0, 1, 6, turned6)
            scores(0, 1, 0, 1, 1)
            pe.wait_ge(free6, 2)
            turn_v(0, 2, 6, turned6)
            pe.sem_inc(pv_done, 2)
            scores(0, 2, 0, 0, 2)
            turn_diff(0, 0, 0, 0)

            def head(h, b, last=False):
                for st in range(TT):
                    s_ = TT * h + st
                    if st % 2:
                        turn_diff(h, st, s_, 0)
                    if not last and st in V_STEPS:
                        rd = V_STEPS.index(st)
                        if rd == 0:
                            pe.wait_ge(v_landed, 32 * (h + 2))
                        pe.wait_ge(free7, use7_v(h, rd) + 1)
                        turn_v(h + 1, rd, 7, turned7)
                    if not last or st + 2 < TT:
                        h2, st2 = ahead(h, st, 2)
                        scores(h2, st2, b if st + 2 < TT else 1 - b, 1, s_ + 2)
                    turn_diff(h, st, s_, 1)
                    turn_diff(h, st, s_, 2)
                    if not last or st + 3 < TT:
                        h3, st3 = ahead(h, st, 3)
                        scores(h3, st3, b if st + 3 < TT else 1 - b, 0, s_ + 3)
                    if st % 2:
                        product_v(h, st, b, s_, 0, KT // 2)
                        if not last or st + 1 < TT:
                            turn_diff(*ahead(h, st, 1), s_ + 1, 0)
                        product_v(h, st, b, s_, KT // 2, KT)

            head(0, 0)
            with pe.Fori(0, HEADS // 2 - 1) as i:
                head(2 * i + 1, 1)
                head(2 * i + 2, 0)
            head(HEADS - 1, 1, last=True)

        @block.scalar
        def _(act):
            act.sem_inc(o_copied, 1)
            def round_k(h, b, m):
                if m == 0:
                    act.wait_ge(k_landed, 64 * (h + 1))
                nc.scalar.activation(k_hi[:, b, m, :], k_raw[:, m, :], ACT.Copy).then_inc(k_rounded, 1)

            def round_q(h, b):
                act.wait_ge(q_landed, 32 * (h + 1))
                nc.scalar.activation(q_st[:, b], q_raw[:], ACT.Copy).then_inc(q_rounded, 1)

            def v_high(rd, b, frm, done):
                k0, k1 = ROUNDS[rd]
                nc.scalar.activation(v_hi[:, b, k0 * P:k1 * P], bank(frm)[:, 0:(k1 - k0) * P], ACT.Copy).then_inc(done, 1)

            def exp(st, m, s_, first=False):
                act.wait_ge(top_ready[m], s_ + 1)
                if not first:
                    act.wait_ge(diff_ready, s_ - 1)
                    act.wait_ge(rest_ready, 2 * s_ - 2)
                row_sum = p1_sum[:, st % 2:st % 2 + 1] if m else p0_sum[:, bass.ds(s_, 1)]
                nc.scalar.activation(prob[:, st % 2, m, :], bank(3 * m, 3)[:, 0:KEYS], ACT.Exp, scale=SCALE,
                                     bias=neg_top[:, st % 2, m:m + 1], accum_out=row_sum).then_inc(exp_done[m], 1)

            def diff_high(h, st, s_, rd):
                if rd == 1:
                    act.wait_ge(turned7, use7(h, st) + 1)
                else:
                    act.wait_ge(turned6, use6(s_, rd // 2) + 1)
                if rd == 0 and st % 2 == 0:
                    act.wait_ge(pv_done, 4 * h + st // 2 + 1)
                k0, k1 = ROUNDS[rd]
                nc.scalar.activation(dT_hi[:, st // 2 % 2, k0:k1, (st % 2) * P:(st % 2 + 1) * P],
                                     bank(7 if rd == 1 else 6)[:, 0:(k1 - k0) * P].rearrange("p (k q) -> p k q", q=P),
                                     ACT.Copy).then_inc(hi7 if rd == 1 else hi6, 1)

            def copy_o(h, st):
                act.wait_ge(pv_done, 4 * h + st // 2 + 3)
                nc.scalar.activation(o_all[:, bass.ds(h, 1), (st - 1) * P:(st + 1) * P].rearrange("p h t -> p (h t)"),
                                     bank(7)[:, 0:QG], ACT.Copy).then_inc(o_copied, 1)

            round_k(0, 0, 0)
            round_k(0, 0, 1)
            round_q(0, 0)
            act.preload_act_table(ACT.Exp)
            exp(0, 0, 0, first=True)
            exp(0, 1, 0, first=True)
            act.wait_ge(lam_spread, 1)
            nc.scalar.activation(lam_exp[:], bank(7)[:, 0:2], ACT.Exp).then_inc(lam_step, 1)
            act.wait_ge(turned6, 1)
            v_high(0, 0, 6, hi6)
            exp(1, 0, 1, first=True)
            for rd in range(1, 3):
                act.wait_ge(turned6, rd + 1)
                v_high(rd, 0, 6, hi6)

            def head(h, b, first=False, last=False):
                for st in range(TT):
                    s_ = TT * h + st
                    if not last or st + 1 < TT:
                        exp(st + 1, 1, s_ + 1, first=first and st == 0)
                    diff_high(h, st, s_, 0)
                    if not last and st in V_STEPS:
                        rd = V_STEPS.index(st)
                        act.wait_ge(turned7, use7_v(h, rd) + 1)
                        v_high(rd, 1 - b, 7, hi7)
                    if not last or st + 2 < TT:
                        exp(st + 2, 0, s_ + 2)
                    if st % 2 == 0:
                        if st:
                            copy_o(h, st - 1)
                        elif not first:
                            copy_o(h - 1, TT - 1)
                    diff_high(h, st, s_, 1)
                    diff_high(h, st, s_, 2)
                    if not last and st < 2:
                        round_k(h + 1, 1 - b, st)
                    if not last and st == 2:
                        round_q(h + 1, 1 - b)

            head(0, 0, first=True)
            with act.Fori(0, HEADS // 2 - 1) as i:
                head(2 * i + 1, 1)
                head(2 * i + 2, 0)
            head(HEADS - 1, 1, last=True)
            copy_o(HEADS - 1, TT - 1)

        @block.gpsimd
        def _(pool):
            pool.memset(ident[:], 0.0).then_inc(id_ready, 1)
            pool.wait_ge(id_ready, 1)
            pool.affine_select(out=ident[:], in_=ident[:], compare_op=ALU.not_equal, fill=1.0, base=0,
                               pattern=[[-1, P]], channel_multiplier=1).then_inc(id_ready, 1)

            def low_k(h, b, m):
                pool.wait_ge(k_rounded, 2 * h + m + 1)
                pool.tensor_tensor(k_lo[:, b, m, :], k_raw[:, m, :], k_hi[:, b, m, :].bitcast(F32), ALU.subtract
                                   ).then_inc(k_split, 1)

            def low_q(h, b, m):
                pool.wait_ge(q_rounded, h + 1)
                pool.tensor_tensor(q_st[DH:P, b, m, :], q_raw[DH:P, m, :], q_st[DH:P, b, m, :].bitcast(F32), ALU.subtract
                                   ).then_inc(q_split, 1)

            def difference_rest(st, s_, first=False):
                pool.wait_ge(factor_ready, s_ + 1)
                if not first:
                    pool.wait_ge(turned6, use6(s_ - 2, 1) + 1)
                b = st % 2
                rest = diff[:, b, SHARE:]
                pool.tensor_tensor(rest, prob[:, b, 1, SHARE:], map1_factor[:, b:b + 1].to_broadcast([P, KEYS - SHARE]),
                                   ALU.mult).then_inc(rest_ready, 1)
                pool.wait_ge(rest_ready, 2 * s_ + 1)
                pool.tensor_tensor(rest, rest, prob[:, b, 0, SHARE:], ALU.add).then_inc(rest_ready, 1)

            def head(h, b, first=False, last=False):
                for st in range(TT):
                    s_ = TT * h + st
                    if not last or st + 1 < TT:
                        difference_rest((st + 1) % TT, s_ + 1, first and st == 0)
                    if not last and st in (1, 2):
                        low_k(h + 1, 1 - b, st - 1)
                    if not last and st in (3, 4):
                        pool.wait_ge(rest_ready, 2 * s_ + 4)
                        low_q(h + 1, 1 - b, st - 3)
                        pool.wait_ge(q_split, 2 * (h + 1) + st - 2)

            difference_rest(0, 0, first=True)
            head(0, 0, first=True)
            with pool.Fori(0, HEADS // 2 - 1) as i:
                head(2 * i + 1, 1)
                head(2 * i + 2, 0)
            head(HEADS - 1, 1, last=True)

        @block.vector
        def _(dve):
            nc.vector.memset(ones_row[0:1, :], 1.0).then_inc(ones_ready, 1)
            dve.sem_inc(free7, 1)
            for m in range(2):
                dve.wait_ge(k_rounded, m + 1)
                nc.vector.tensor_tensor(k_lo[:, 0, m, :], k_raw[:, m, :], k_hi[:, 0, m, :].bitcast(F32), ALU.subtract
                                        ).then_inc(k_split, 1)
            dve.wait_ge(q_rounded, 1)
            for m in range(2):
                nc.vector.tensor_tensor(q_st[DH:P, 0, m, :], q_raw[DH:P, m, :], q_st[DH:P, 0, m, :].bitcast(F32),
                                        ALU.subtract).then_inc(q_split, 1)
            dve.wait_ge(lam_landed, 64)
            for k in range(2):
                nc.vector.tensor_tensor(lam_tmp[0:1, k, :], lam_rows[0:1, 2 * k, :], lam_rows[0:1, 2 * k + 1, :], ALU.mult
                                        ).then_inc(lam_ready, 1)
            dve.wait_ge(lam_ready, 2)
            for k in range(2):
                nc.vector.tensor_reduce(lam_dots[0:1, k:k + 1], lam_tmp[0:1, k, :], AXX, ALU.add).then_inc(lam_step, 1)
            def v_low(rd, b, frm, done):
                k0, k1 = ROUNDS[rd]
                part = slice(k0 * P, k1 * P)
                nc.vector.tensor_tensor(v_lo[:, b, part], bank(frm)[:, 0:(k1 - k0) * P], v_hi[:, b, part].bitcast(F32),
                                        ALU.subtract).then_inc(done, 1)
                if rd == 2:
                    dve.sem_inc(v_read, 1)

            def find_top(st, m, s_):
                dve.wait_ge(scores_done[m], s_ + 1)
                nc.vector.tensor_reduce(top[:, st % 2, m:m + 1], bank(3 * m, 3)[:, 0:KEYS], AXX, ALU.max
                                        ).then_inc(top_found[m], 1)

            def negate_top(st, m, s_):
                dve.wait_ge(top_found[m], s_ + 1)
                nc.vector.tensor_scalar(neg_top[:, st % 2, m:m + 1], top[:, st % 2, m:m + 1], -SCALE,
                                        0.0 if m else -P0_DOWN * math.log(2.0), ALU.mult, ALU.add
                                        ).then_inc(top_ready[m], 1)

            def invert(st, s_):
                dve.wait_ge(exp_done[1], s_ + 1)
                nc.vector.reciprocal(p1_inv[:, st % 2:st % 2 + 1], p1_sum[:, st % 2:st % 2 + 1]).then_inc(inv_ready, 1)

            def factor(st, s_):
                dve.wait_ge(inv_ready, s_ + 1)
                dve.wait_ge(exp_done[0], s_ + 1)
                nc.vector.scalar_tensor_tensor(out=map1_factor[:, st % 2:st % 2 + 1], in0=p0_sum[:, bass.ds(s_, 1)],
                                               scalar=neg_lam[:], in1=p1_inv[:, st % 2:st % 2 + 1],
                                               op0=ALU.mult, op1=ALU.mult).then_inc(factor_ready, 1)

            def difference(st, s_):
                dve.wait_ge(factor_ready, s_ + 1)
                nc.vector.scalar_tensor_tensor(out=diff[:, st % 2, 0:SHARE], in0=prob[:, st % 2, 1, 0:SHARE],
                                               scalar=map1_factor[:, st % 2:st % 2 + 1], in1=prob[:, st % 2, 0, 0:SHARE],
                                               op0=ALU.mult, op1=ALU.add).then_inc(diff_ready, 1)

            def diff_low(h, st, s_, rd):
                if rd == 1:
                    dve.wait_ge(hi7, use7(h, st) + 1)
                else:
                    dve.wait_ge(hi6, use6(s_, rd // 2) + 1)
                k0, k1 = ROUNDS[rd]
                at = (slice(None), st // 2 % 2, slice(k0, k1), slice((st % 2) * P, (st % 2 + 1) * P))
                nc.vector.tensor_tensor(dT_lo[at], bank(7 if rd == 1 else 6)[:, 0:(k1 - k0) * P]
                                        .rearrange("p (k q) -> p k q", q=P), dT_hi[at].bitcast(F32), ALU.subtract
                                        ).then_inc(free7 if rd == 1 else free6, 1)

            def v_first(rd):
                dve.wait_ge(hi6, rd + 1)
                v_low(rd, 0, 6, free6)

            for m in range(2):
                find_top(0, m, 0)
                negate_top(0, m, 0)
            v_first(0)
            find_top(1, 0, 1)
            negate_top(1, 0, 1)
            v_first(1)
            dve.wait_ge(lam_step, 3)
            nc.vector.scalar_tensor_tensor(out=neg_lam[:], in0=lam_exp[:, 0:1], scalar=LAM_INIT, in1=lam_exp[:, 1:2],
                                           op0=ALU.add, op1=ALU.subtract).then_inc(lam_ready, 1)
            dve.wait_ge(lam_ready, 3)
            nc.vector.tensor_scalar(neg_lam[:], neg_lam[:], -1.0, None, ALU.mult).then_inc(lam_ready, 1)
            dve.wait_ge(lam_ready, 4)

            invert(0, 0)
            factor(0, 0)
            difference(0, 0)
            v_first(2)
            find_top(1, 1, 1)
            negate_top(1, 1, 1)

            def head(h, b, last=False):
                for st in range(TT):
                    s_ = TT * h + st
                    nxt = not last or st + 1 < TT
                    front = not last or st + 2 < TT
                    if front:
                        find_top(st + 2, 0, s_ + 2)
                    if nxt:
                        invert(st + 1, s_ + 1)
                    if front:
                        negate_top(st + 2, 0, s_ + 2)
                    if nxt:
                        factor(st + 1, s_ + 1)
                    diff_low(h, st, s_, 0)
                    if not last and st in V_STEPS:
                        rd = V_STEPS.index(st)
                        dve.wait_ge(hi7, use7_v(h, rd) + 1)
                        v_low(rd, 1 - b, 7, free7)
                    if nxt:
                        difference(st + 1, s_ + 1)
                    if st % 2:
                        diff_low(h, st, s_, 1)
                    if front:
                        find_top(st + 2, 1, s_ + 2)
                        negate_top(st + 2, 1, s_ + 2)
                    if st % 2 == 0:
                        diff_low(h, st, s_, 1)
                    diff_low(h, st, s_, 2)

            head(0, 0)
            with dve.Fori(0, HEADS // 2 - 1) as i:
                head(2 * i + 1, 1)
                head(2 * i + 2, 0)
            head(HEADS - 1, 1, last=True)


def o_all_start(nc):
    return nc.sbuf_usable_end // 32 * 32 - HEADS * T * 4 - HEADS * TT * 4


def output(nc, t, sem, Region, base, bank, proj_d, gate_d, o_all, p0_sum):
    GROUPS = 8
    GT = 4
    RING = 4
    CONV_T = CONV_W // P
    r = Region(base)
    m_hi = r.take("m_hi", JT * T, F32R)[:].rearrange("p (k t) -> p k t", k=JT)
    lo_at = r.at
    m_lo = r.take("m_lo", JT * T, F32R)[:].rearrange("p (k t) -> p k t", k=JT)
    mixed = Region(lo_at).take("mixed", JT * T)[:].rearrange("p (k t) -> p k t", k=JT)
    o_sq = Region(base + CONV_T * T * 4).take("o_sq", HEADS * T)[:].rearrange("p (h t) -> p h t", h=HEADS)
    wo_raw = r.take("wo_raw", RING * BANK)[:].rearrange("p (s n) -> p s n", s=RING)
    wo_hi = r.take("wo_hi", RING * BANK, F32R)[:].rearrange("p (s n) -> p s n", s=RING)
    wo_lo = r.take("wo_lo", RING * BANK, F32R)[:].rearrange("p (s n) -> p s n", s=RING)
    gate = r.take("gate", D)
    xy = r.take("xy", GT * BANK)[:].rearrange("p (s n) -> p s n", s=GT)
    tmp_at = r.at
    tmp = r.take("tmp", 2 * BANK)[:].rearrange("p (s n) -> p s n", s=2)
    diag = Region(tmp_at).take("diag", TT * P)[:].rearrange("p (t q) -> p t q", t=TT)
    ident = r.take("ident_c", P)
    ones = r.take("ones_c", P)
    root = r.take("root", HEADS * TT)
    no_overflow = r.take("no_overflow", HEADS * TT)
    head_gain = r.take("head_gain", 1)
    p0_sq = r.take("p0_sq", HEADS * TT)
    assert r.at <= o_all_start(nc), r.at

    gain_landed = sem("gain_landed")
    gate_landed = sem("gate_landed")
    gate_biased = sem("gate_biased")
    mix_landed = [sem(f"mix_landed{k}") for k in range(JT // 4)]
    wo_landed = [sem(f"wo_landed{k}") for k in range(RING)]
    wo_hi_ready = [sem(f"wo_hi_ready{k}") for k in range(RING)]
    wo_lo_ready = [sem(f"wo_lo_ready{k}") for k in range(RING)]
    wo_used = [sem(f"wo_used{k}") for k in range(RING)]
    id2_ready = sem("id2_ready")
    const_ready = sem("const_ready")
    o_squared = sem("o_squared")
    o_bounded = sem("o_bounded")
    o_summed = sem("o_summed")
    o_root = sem("o_root")
    o_recip = sem("o_recip")
    diag_ready = sem("diag_ready")
    spread = sem("spread")
    o_normed = sem("o_normed")
    mix_gated = sem("mix_gated")
    mix_rounded = sem("mix_rounded")
    mix_ready = sem("mix_ready")
    sum_done = sem("sum_done")
    sum_freed = sem("sum_freed")
    y_done = sem("y_done")
    xo_landed = sem("xo_landed")
    out_stored = sem("out_stored")

    x_v = t["x"].rearrange("b (g s p) d -> p (b g) s d", p=P, s=GT)
    out_v = t["out"].rearrange("b (g s p) d -> p (b g) s d", p=P, s=GT)

    def w_row(k):
        return (ATT_W + k * P, (N_GC - N_GA + k) * P) if k < CONV_T else ((k - CONV_T) * P, (k - CONV_T) * P)

    with nc.Block(name="output") as block:

        @block.sync
        def _(sp):
            def columns(cb):
                return bass.ds((cb + 1) * BANK - BANK, BANK)

            def load_w(n4, k, cb, first=False):
                if not first:
                    sp.wait_ge(wo_lo_ready[k % RING], n4)
                row = w_row(k)[0]
                sp.dma_start(wo_raw[:, k % RING, :], t["w_out"][0, row:row + P, columns(cb)]
                             ).then_inc(wo_landed[k % RING], 16)

            def group(g, half, cb, first=False):
                uses = [4 * g + q for q in range(JT // RING)]
                if not isinstance(g, int):
                    uses = [sp.snap(u) for u in uses]
                for k in range(JT):
                    load_w(uses[k // RING], k, cb, first and k < RING)
                    if first and 0 <= k - RING + 1 < 4:
                        for kk in range(4 * (k - RING + 1), 4 * (k - RING + 2)):
                            row = w_row(kk)[1]
                            sp.dma_start(mixed[:, kk, :], proj_d[row:row + P, :]).then_inc(mix_landed[kk // 4], 16)
                    if k == 4 and first:
                        sp.dma_start(gate[:], gate_d.to_broadcast([P, D])).then_inc(gate_landed, 16)
                        sp.dma_start(xy[:].rearrange("p s n -> p (s n)"), t["b_ada"][:, 2 * D:].to_broadcast([P, D])
                                     ).then_inc(gate_landed, 16)
                    if k == 4 and not first:
                        sp.wait_ge(y_done, 4 * g)
                        last_cb = cb if half else cb - 1
                        sp.dma_start(out_v[:, 1 - half, :, columns(last_cb)], xy[:]).then_inc(out_stored, 16)
                    if k == 8:
                        if first:
                            sp.wait_ge(gate_biased, 1)
                        else:
                            sp.wait_ge(out_stored, 16 * g)
                        sp.dma_start(xy[:], x_v[:, half, :, columns(cb)]).then_inc(xo_landed, 16)

            sp.dma_start(head_gain[:], t["sub_norm_g"].rearrange("l d -> d l")).then_inc(gain_landed, 16)
            group(0, 0, 0, first=True)
            group(1, 1, 0)
            with sp.Fori(1, GROUPS // 2) as cb:
                for half in range(2):
                    group(2 * cb + half, half, cb)
            sp.wait_ge(y_done, GT * GROUPS)
            sp.dma_start(out_v[:, 1, :, D - BANK:D], xy[:]).then_inc(out_stored, 16)
            sp.wait_ge(out_stored, 16 * GROUPS)

        @block.gpsimd
        def _(pool):
            pool.memset(ident[:], 0.0).then_inc(id2_ready, 1)
            pool.wait_ge(id2_ready, 1)
            pool.affine_select(out=ident[:], in_=ident[:], compare_op=ALU.not_equal, fill=1.0, base=0,
                               pattern=[[-1, P]], channel_multiplier=1).then_inc(id2_ready, 1)

            def low_w(n, s_):
                pool.wait_ge(wo_hi_ready[s_], n + 1)
                pool.tensor_tensor(wo_lo[:, s_, :], wo_raw[:, s_, :], wo_hi[:, s_, :].bitcast(F32), ALU.subtract
                                   ).then_inc(wo_lo_ready[s_], 1)

            for k in range(JT):
                h = k - CONV_T
                if h >= 0:
                    pool.wait_ge(o_normed, h + 1)
                    pool.wait_ge(mix_landed[k // 4], 16 * 4)
                    pool.tensor_tensor(mixed[:, k, :], mixed[:, k, :], o_all[:, h, :], ALU.mult).then_inc(mix_gated, 1)
                low_w(k // RING, k % RING)
            with pool.Fori(JT // RING, GROUPS * JT // RING) as n:
                for s_ in range(RING):
                    low_w(n, s_)

        @block.tensor
        def _(pe):
            pe.wait_ge(const_ready, 1)
            for h in range(HEADS):
                pe.wait_ge(o_squared, h + 1)
                for tt in range(TT):
                    mm = pe.matmul(bank(4)[:, h * TT + tt:h * TT + tt + 1], o_sq[:, h, tt * P:(tt + 1) * P], ones[:, 0:1],
                                   start=True, stop=True, skip_group_check=True)
            mm.then_inc(o_summed, 1)

            def spread_norm(h):
                pe.wait_ge(diag_ready, h + 1)
                if h >= 2:
                    pe.wait_ge(o_normed, h - 1)
                for tt in range(TT):
                    b = 4 + 2 * (h % 2) + tt // 4
                    mm = pe.matmul(bank(b)[:, (tt % 4) * P:(tt % 4 + 1) * P], ones[:], diag[:, tt, :],
                                   start=True, stop=True, skip_group_check=True)
                mm.then_inc(spread, 1)

            def group(g, half, first=False):
                for k in range(JT):
                    if first and CONV_T - 2 <= k < JT - 2:
                        spread_norm(k + 2 - CONV_T)
                    if first:
                        pe.wait_ge(mix_ready, k + 1)
                    n = 4 * g + k // RING + 1
                    s_ = k % RING
                    pe.wait_ge(wo_hi_ready[s_], n)
                    pe.wait_ge(wo_lo_ready[s_], n)
                    for q in range(GT):
                        if k == 0 and not first:
                            if isinstance(g, int):
                                pass
                            else:
                                pe.wait_ge(sum_freed, 4 * g - 8 + q + 1)
                        tok = slice((half * GT + q) * P, (half * GT + q + 1) * P)
                        mm = split_matmuls(pe, bank(half * GT + q), m_hi[:, k, tok], m_lo[:, k, tok],
                                           wo_hi[:, s_, :], wo_lo[:, s_, :], k == 0, k == JT - 1)
                        if k == JT - 1:
                            mm.then_inc(sum_done, 1)
                    if k < JT - 1:
                        mm.then_inc(wo_used[s_], 1)
                    else:
                        pe.wait_ge(sum_done, 4 * g + GT)
                        pe.sem_inc(wo_used[s_], 1)

            group(0, 0, first=True)
            pe.wait_ge(o_normed, HEADS)
            group(1, 1)
            with pe.Fori(1, GROUPS // 2) as cb:
                for half in range(2):
                    group(2 * cb + half, half)

        @block.scalar
        def _(act):
            for h in range(HEADS):
                act.wait_ge(o_bounded, h + 1)
                nc.scalar.activation(o_sq[:, h, :], o_sq[:, h, :], ACT.Square, scale=O_DOWN).then_inc(o_squared, 1)

            def round_w(g, k, first=False):
                s_ = k % RING
                n = 4 * g + k // RING
                act.wait_ge(wo_landed[s_], 16 * (n + 1))
                if not (first and k < RING):
                    act.wait_ge(wo_used[s_], n)
                nc.scalar.activation(wo_hi[:, s_, :], wo_raw[:, s_, :], ACT.Copy).then_inc(wo_hi_ready[s_], 1)

            def round_mix(k):
                nc.scalar.activation(m_hi[:, k, :], mixed[:, k, :], ACT.Copy).then_inc(mix_rounded, 1)

            for k in range(CONV_T):
                if k == RING:
                    act.wait_ge(o_recip, 3)
                    nc.scalar.activation(root[:], root[:], ACT.Sqrt, scale=1.0 / P).then_inc(o_root, 1)
                round_w(0, k, first=True)
                act.wait_ge(mix_landed[k // 4], 16 * 4)
                round_mix(k)
            for k in range(CONV_T, JT):
                round_w(0, k, first=True)
                act.wait_ge(mix_gated, k - CONV_T + 1)
                round_mix(k)
            for k in range(JT):
                round_w(1, k)
            with act.Fori(1, GROUPS // 2) as cb:
                for half in range(2):
                    for k in range(JT):
                        round_w(2 * cb + half, k)

        @block.vector
        def _(dve):
            nc.vector.memset(ones[:], 1.0).then_inc(const_ready, 1)
            nc.vector.tensor_tensor(p0_sq[:], p0_sum[:], p0_sum[:], ALU.mult).then_inc(const_ready, 1)
            for h in range(HEADS):
                nc.vector.tensor_scalar(o_sq[:, h, :], o_all[:, h, :], O_BOUND, -O_BOUND, ALU.min, ALU.max
                                        ).then_inc(o_bounded, 1)

            def low_mix(k):
                dve.wait_ge(mix_rounded, k + 1)
                nc.vector.tensor_tensor(m_lo[:, k, :], mixed[:, k, :], m_hi[:, k, :].bitcast(F32), ALU.subtract
                                        ).then_inc(mix_ready, 1)

            for k in range(RING):
                low_mix(k)
            dve.wait_ge(gain_landed, 16)
            nc.vector.tensor_scalar(head_gain[:], head_gain[:], (1.0 - LAM_INIT) * O_DOWN, None, ALU.mult
                                    ).then_inc(o_recip, 1)
            dve.wait_ge(const_ready, 2)
            dve.wait_ge(o_summed, 1)
            nc.vector.scalar_tensor_tensor(out=no_overflow[:], in0=p0_sq[:], scalar=SQ_OVERFLOW,
                                           in1=bank(4)[:, 0:HEADS * TT], op0=ALU.mult, op1=ALU.is_gt).then_inc(o_recip, 1)
            nc.vector.scalar_tensor_tensor(out=root[:], in0=p0_sq[:], scalar=P * EPS * O_DOWN ** 2,
                                           in1=bank(4)[:, 0:HEADS * TT], op0=ALU.mult, op1=ALU.add).then_inc(o_recip, 1)
            dve.wait_ge(o_root, 1)
            nc.vector.reciprocal(root[:], root[:]).then_inc(o_recip, 1)
            dve.wait_ge(o_recip, 4)
            nc.vector.tensor_tensor(root[:], root[:], no_overflow[:], ALU.mult).then_inc(o_recip, 1)
            dve.wait_ge(o_recip, 5)
            dve.wait_ge(id2_ready, 2)

            def spread_diag(h):
                if h >= 1:
                    dve.wait_ge(spread, h)
                nc.vector.tensor_tensor(diag[:], ident[:].unsqueeze(1).to_broadcast([P, TT, P]),
                                        root[:, h * TT:(h + 1) * TT].unsqueeze(2).to_broadcast([P, TT, P]), ALU.mult
                                        ).then_inc(diag_ready, 1)

            spread_diag(0)
            for k in range(RING, CONV_T):
                low_mix(k)
            dve.wait_ge(gate_landed, 32)
            nc.vector.tensor_tensor(gate[:], gate[:], xy[:].rearrange("p s n -> p (s n)"), ALU.add).then_inc(gate_biased, 1)
            for h in range(HEADS):
                dve.wait_ge(spread, h + 1)
                nc.vector.scalar_tensor_tensor(out=o_all[:, h, :], in0=o_all[:, h, :], scalar=head_gain[:],
                                               in1=bank(4 + 2 * (h % 2), 2), op0=ALU.mult, op1=ALU.mult
                                               ).then_inc(o_normed, 1)
                if h + 1 < HEADS:
                    spread_diag(h + 1)
                if h >= 1:
                    low_mix(CONV_T + h - 1)
            low_mix(JT - 1)

            def result(g, half, cb):
                for q in range(GT):
                    dve.wait_ge(sum_done, 4 * g + q + 1)
                    if q == 0:
                        dve.wait_ge(xo_landed, 16 * (g + 1))
                    nc.vector.tensor_tensor(tmp[:, q % 2, :], bank(half * GT + q), gate[:, bass.ds(cb * BANK, BANK)], ALU.mult
                                            ).then_inc(sum_freed, 1)
                    dve.wait_ge(sum_freed, 4 * g + q + 1)
                    nc.vector.tensor_tensor(xy[:, q, :], xy[:, q, :], tmp[:, q % 2, :], ALU.add).then_inc(y_done, 1)

            dve.wait_ge(gate_biased, 1)
            with dve.Fori(0, GROUPS // 2) as cb:
                for half in range(2):
                    result(2 * cb + half, half, cb)


_INS = ["x", "c", "ctx", "c_ctx", "w_ada", "b_ada", "norm_g", "w_in", "q_norm_g", "k_norm_g", "lam_q1", "lam_k1",
        "lam_q2", "lam_k2", "sub_norm_g", "conv_w", "conv_b", "conv_ln_g", "conv_ln_b", "w_out"]


def kernel(**inputs):
    import concourse.bacc as _bacc
    from concourse.bass_utils import run_bass_kernel_spmd as _run

    nc = _bacc.Bacc("TRN2", target_bir_lowering=False, num_devices=1)
    cos, sin = rope_tables()
    arrays, tensors = {}, {}
    for name in _INS + ["rope_cos", "rope_sin"]:
        a = {"rope_cos": cos, "rope_sin": sin}.get(name)
        if a is None:
            a = np.ascontiguousarray(inputs[name])
        arrays[f"in_{name}_dram"] = a
        tensors[name] = nc.dram_tensor(f"in_{name}_dram", a.shape, mybir.dt.from_np(a.dtype), kind="ExternalInput").ap()
    tensors["out"] = nc.dram_tensor("out_0_dram", (1, T, D), F32, kind="ExternalOutput").ap()
    with nc.allow_non_contiguous_dma(reason="gains of 64 or 128 channels, one per partition"):
        build(nc, tensors)
    r = _run(nc, [arrays], core_ids=[0])
    return r.results[0]["out_0_dram"]
```
